# Optimizing a Trainium2 kernel written in Bass

```python
import math
import jax, jax.numpy as jnp
from jax import lax
import numpy as np

D_MODEL = 1024
BATCH = 1
SEQ = 512
DEPTH = 2

HEAD_DIM = 64
D_MIX = D_MODEL
DN_HEADS = 6
DN_WIDTH = DN_HEADS * HEAD_DIM
FX_HEADS = 6
FX_WIDTH = FX_HEADS * HEAD_DIM
POOL_GROUPS = 4
POOL_WIDTH = D_MIX - DN_WIDTH - FX_WIDTH
POOL_GROUP_DIM = POOL_WIDTH // POOL_GROUPS
POOL_WINDOWS = (2, 4, 8, 16)
CONV_WIDTH = 4
DN_CHUNK = 64
FX_BLOCK = 128
D_FF = 2816
N_EXPERTS = 8
TOP_K = 2
D_FF_EXPERT = 1536
N_DENSE = (DEPTH + 1) // 2
N_MOE = DEPTH // 2
EPS = 1e-6
N_IN = 4 * DN_WIDTH + 2 * DN_HEADS + 3 * FX_WIDTH + FX_HEADS + POOL_WIDTH


F32 = jnp.float32

def rmsnorm(x, g):
    xf = x.astype(F32)
    y = xf * lax.rsqrt(jnp.mean(xf * xf, axis=-1, keepdims=True) + EPS)
    return (y * g.astype(F32)).astype(x.dtype)

def l2norm(x):
    return x * lax.rsqrt(jnp.sum(x * x, axis=-1, keepdims=True) + EPS)

def causal_conv(x, w):
    c = x.shape[-1]
    return lax.conv_general_dilated(x, w.astype(x.dtype)[:, None, :], window_strides=(1,),
                                    padding=[(CONV_WIDTH - 1, 0)],
                                    dimension_numbers=('NWC', 'WIO', 'NWC'),
                                    feature_group_count=c)

def chunk_gated_delta_rule(q, k, v, g, beta):
    B, T, H, Dk = q.shape
    Dv = v.shape[-1]
    C = DN_CHUNK
    N = T // C

    def to_chunks(a):
        a = a.reshape((B, N, C, H) + a.shape[3:])
        return jnp.moveaxis(a, 3, 1)

    q, k, v, g, beta = (to_chunks(a) for a in (q, k, v, g, beta))
    G = jnp.cumsum(g, axis=-1)
    causal = jnp.tril(jnp.ones((C, C), bool))
    strict = jnp.tril(jnp.ones((C, C), bool), -1)
    diff = G[..., :, None] - G[..., None, :]
    decay = jnp.where(causal, jnp.exp(jnp.where(causal, diff, 0.0)), 0.0)
    kb = k * beta[..., None]
    a_mat = jnp.where(strict, jnp.einsum('bhnid,bhnjd->bhnij', kb, k) * decay, 0.0)
    eye = jnp.eye(C, dtype=q.dtype)
    rhs = jnp.concatenate([v * beta[..., None], kb * jnp.exp(G)[..., None]], axis=-1)
    uw = lax.linalg.triangular_solve(a_mat + eye, rhs, left_side=True, lower=True,
                                     transpose_a=False, conjugate_a=False, unit_diagonal=True)
    u, w = uw[..., :Dv], uw[..., Dv:]
    qk = jnp.where(causal, jnp.einsum('bhnid,bhnjd->bhnij', q, k) * decay, 0.0)
    q_dec = q * jnp.exp(G)[..., None]
    k_dec = k * jnp.exp(G[..., -1:] - G)[..., None]
    last = jnp.exp(G[..., -1])

    def step(S, xs):
        u_n, w_n, qk_n, q_n, k_n, l_n = xs
        v_new = u_n - jnp.einsum('bhck,bhkv->bhcv', w_n, S)
        o_n = jnp.einsum('bhck,bhkv->bhcv', q_n, S) + jnp.einsum('bhij,bhjv->bhiv', qk_n, v_new)
        S = S * l_n[..., None, None] + jnp.einsum('bhck,bhcv->bhkv', k_n, v_new)
        return S, o_n

    xs = tuple(jnp.moveaxis(a, 2, 0) for a in (u, w, qk, q_dec, k_dec, last))
    S0 = jnp.zeros((B, H, Dk, Dv), q.dtype)
    _, o = lax.scan(step, S0, xs)
    return jnp.transpose(o, (1, 0, 3, 2, 4)).reshape(B, T, H, Dv)

def gated_deltanet(q, k, v, z, a, b, conv_w, a_log, dt_bias, onorm_g):
    B, T, _ = q.shape
    dt = q.dtype
    qkv = jax.nn.silu(causal_conv(jnp.concatenate([q, k, v], axis=-1), conv_w)).astype(F32)
    q, k, v = jnp.split(qkv, 3, axis=-1)
    heads = lambda t: t.reshape(B, T, DN_HEADS, HEAD_DIM)
    q = l2norm(heads(q)) * (HEAD_DIM ** -0.5)
    k = l2norm(heads(k))
    v = heads(v)
    beta = jax.nn.sigmoid(b.astype(F32))
    g = -jnp.exp(a_log.astype(F32)) * jax.nn.softplus(a.astype(F32) + dt_bias.astype(F32))
    o = chunk_gated_delta_rule(q, k, v, g, beta)
    o = rmsnorm(o, onorm_g) * jax.nn.silu(heads(z).astype(F32))
    return o.reshape(B, T, DN_WIDTH).astype(dt)

def forgetting_attention(q, k, v, f, qnorm_g, knorm_g, f_bias):
    B, T, _ = q.shape
    dt = q.dtype
    heads = lambda t: t.reshape(B, T, FX_HEADS, HEAD_DIM).transpose(0, 2, 1, 3)
    q = rmsnorm(heads(q), qnorm_g)
    k = rmsnorm(heads(k), knorm_g)
    v = heads(v)
    logf = jax.nn.log_sigmoid(f.astype(F32) + f_bias.astype(F32))
    c = jnp.cumsum(logf, axis=1).transpose(0, 2, 1)
    scale = HEAD_DIM ** -0.5
    outs = []
    for i in range(T // FX_BLOCK):
        lo, hi = i * FX_BLOCK, (i + 1) * FX_BLOCK
        s = jnp.einsum('bhqd,bhkd->bhqk', q[:, :, lo:hi], k[:, :, :hi]).astype(F32) * scale
        s = s + c[:, :, lo:hi, None] - c[:, :, None, :hi]
        q_pos = jnp.arange(lo, hi)[:, None]
        k_pos = jnp.arange(hi)[None, :]
        s = jnp.where(k_pos <= q_pos, s, -jnp.inf)
        p = jax.nn.softmax(s, axis=-1).astype(dt)
        outs.append(jnp.einsum('bhqk,bhkd->bhqd', p, v[:, :, :hi]))
    o = jnp.concatenate(outs, axis=2)
    return o.transpose(0, 2, 1, 3).reshape(B, T, FX_WIDTH)

def pool_mixer(xp, pool_w, pool_scale):
    B, T, _ = xp.shape
    xg = xp.reshape(B, T, POOL_GROUPS, POOL_GROUP_DIM).astype(F32)
    cs = jnp.concatenate([jnp.zeros((B, 1, POOL_GROUPS, POOL_GROUP_DIM), F32),
                          jnp.cumsum(xg, axis=1)], axis=1)
    win = jnp.array(POOL_WINDOWS, jnp.int32)
    t1 = jnp.arange(1, T + 1, dtype=jnp.int32)[:, None]
    start = jnp.maximum(t1 - win[None, :], 0)
    count = (t1 - start).astype(F32)
    gidx = jnp.arange(POOL_GROUPS)[None, :]
    window_sum = cs[:, 1:] - cs[:, start, gidx]
    y = (window_sum / count[..., None] - xg).astype(xp.dtype)
    y = jnp.einsum('btgc,gcd->btgd', y, pool_w)
    return y.reshape(B, T, POOL_WIDTH) * pool_scale

def hybrid_mixer(h, w_in, dn_conv, dn_a_log, dn_dt_bias, dn_onorm, fx_qnorm, fx_knorm, fx_f_bias,
                 pool_w, pool_scale, w_out):
    proj = h @ w_in
    sizes = (DN_WIDTH, DN_WIDTH, DN_WIDTH, DN_WIDTH, DN_HEADS, DN_HEADS,
             FX_WIDTH, FX_WIDTH, FX_WIDTH, FX_HEADS, POOL_WIDTH)
    (dn_q, dn_k, dn_v, dn_z, dn_a, dn_b, fx_q, fx_k, fx_v, fx_f, pl_x) = jnp.split(
        proj, np.cumsum(sizes)[:-1].tolist(), axis=-1)
    o_dn = gated_deltanet(dn_q, dn_k, dn_v, dn_z, dn_a, dn_b, dn_conv, dn_a_log, dn_dt_bias, dn_onorm)
    o_fx = forgetting_attention(fx_q, fx_k, fx_v, fx_f, fx_qnorm, fx_knorm, fx_f_bias)
    o_pl = pool_mixer(pl_x, pool_w, pool_scale)
    return jnp.concatenate([o_dn, o_fx, o_pl], axis=-1) @ w_out

def swiglu(h, w_gate, w_up, w_down):
    return (jax.nn.silu(h @ w_gate) * (h @ w_up)) @ w_down

def moe_swiglu(h, router, w_gate, w_up, w_down):
    B, T, D = h.shape
    ht = h.reshape(B * T, D)
    probs = jax.nn.softmax((ht @ router).astype(F32), axis=-1)
    top_p, top_i = lax.top_k(probs, TOP_K)
    top_p = top_p / jnp.sum(top_p, axis=-1, keepdims=True)
    gates = jnp.sum(jax.nn.one_hot(top_i, N_EXPERTS, dtype=F32) * top_p[..., None], axis=1).astype(h.dtype)
    out = jnp.zeros_like(ht)
    for e in range(N_EXPERTS):
        out = out + gates[:, e:e + 1] * swiglu(ht, w_gate[e], w_up[e], w_down[e])
    return out.reshape(B, T, D)

def first_inputs(seed: int = 0) -> dict:
    key = jax.random.key(seed)
    ks = list(jax.random.split(key, 32))
    counter = [0]

    def nk():
        counter[0] += 1
        return ks[counter[0] - 1]

    def nrm(shape, scale):
        return scale * jax.random.normal(nk(), shape, F32)

    def gain(shape):
        return 1.0 + nrm(shape, 0.05)

    L = DEPTH
    x = nrm((BATCH, SEQ, D_MODEL), 1.0)
    norm1 = gain((L, D_MODEL))
    w_in = nrm((L, D_MODEL, N_IN), D_MODEL ** -0.5)
    dn_conv = nrm((L, CONV_WIDTH, 3 * DN_WIDTH), CONV_WIDTH ** -0.5)
    dn_a_log = jnp.log(jax.random.uniform(nk(), (L, DN_HEADS), F32, 1.0, 16.0))
    dt0 = jnp.exp(jax.random.uniform(nk(), (L, DN_HEADS), F32, math.log(1e-3), math.log(1e-1)))
    dn_dt_bias = dt0 + jnp.log(-jnp.expm1(-dt0))
    dn_onorm = gain((L, HEAD_DIM))
    fx_qnorm = gain((L, HEAD_DIM))
    fx_knorm = gain((L, HEAD_DIM))
    fx_f_bias = 2.0 + nrm((L, FX_HEADS), 0.5)
    pool_w = nrm((L, POOL_GROUPS, POOL_GROUP_DIM, POOL_GROUP_DIM), POOL_GROUP_DIM ** -0.5)
    pool_scale = 1.0 + nrm((L, POOL_WIDTH), 0.1)
    w_out = nrm((L, D_MIX, D_MODEL), 0.5 * D_MIX ** -0.5)
    norm2 = gain((L, D_MODEL))
    ffn_gate = nrm((N_DENSE, D_MODEL, D_FF), D_MODEL ** -0.5)
    ffn_up = nrm((N_DENSE, D_MODEL, D_FF), D_MODEL ** -0.5)
    ffn_down = nrm((N_DENSE, D_FF, D_MODEL), 0.5 * D_FF ** -0.5)
    router = nrm((N_MOE, D_MODEL, N_EXPERTS), D_MODEL ** -0.5)
    moe_gate = nrm((N_MOE, N_EXPERTS, D_MODEL, D_FF_EXPERT), D_MODEL ** -0.5)
    moe_up = nrm((N_MOE, N_EXPERTS, D_MODEL, D_FF_EXPERT), D_MODEL ** -0.5)
    moe_down = nrm((N_MOE, N_EXPERTS, D_FF_EXPERT, D_MODEL), 0.5 * D_FF_EXPERT ** -0.5)
    return {'x': x, 'norm1': norm1, 'w_in': w_in, 'dn_conv': dn_conv, 'dn_a_log': dn_a_log,
            'dn_dt_bias': dn_dt_bias, 'dn_onorm': dn_onorm, 'fx_qnorm': fx_qnorm, 'fx_knorm': fx_knorm,
            'fx_f_bias': fx_f_bias, 'pool_w': pool_w, 'pool_scale': pool_scale, 'w_out': w_out,
            'norm2': norm2, 'ffn_gate': ffn_gate, 'ffn_up': ffn_up, 'ffn_down': ffn_down,
            'router': router, 'moe_gate': moe_gate, 'moe_up': moe_up, 'moe_down': moe_down}

def first_block(x, norm1, w_in, dn_conv, dn_a_log, dn_dt_bias, dn_onorm, fx_qnorm, fx_knorm, fx_f_bias,
              pool_w, pool_scale, w_out, norm2, ffn_gate, ffn_up, ffn_down, router, moe_gate, moe_up,
              moe_down):
    for layer in range(DEPTH):
        h = rmsnorm(x, norm1[layer])
        x = x + hybrid_mixer(h, w_in[layer], dn_conv[layer], dn_a_log[layer], dn_dt_bias[layer],
                             dn_onorm[layer], fx_qnorm[layer], fx_knorm[layer], fx_f_bias[layer],
                             pool_w[layer], pool_scale[layer], w_out[layer])
        h = rmsnorm(x, norm2[layer])
        j = layer // 2
        if layer % 2 == 0:
            x = x + swiglu(h, ffn_gate[j], ffn_up[j], ffn_down[j])
        else:
            x = x + moe_swiglu(h, router[j], moe_gate[j], moe_up[j], moe_down[j])
    return x


DEPTH_2 = 1

CHUNK = 64
N_MEM = 256

A_HEADS = 8
A_HEAD_DIM = 64
A_WIDTH = A_HEADS * A_HEAD_DIM
DECAY_LORA = 64
AAA_LORA = 64
GATE_LORA = 128
LNX_EPS = 64e-5

B_BLOCKS = 8
B_WIDTH = 512
B_BLOCK_DIM = B_WIDTH // B_BLOCKS
B_CONV = 4
LRU_C = 8.0

X_HEADS = 4
X_HEAD_DIM = D_MODEL // X_HEADS

FFN_CONV = 3

NORM_EPS = 1e-6

RWKV_COLS = 3 * A_WIDTH + DECAY_LORA + AAA_LORA + GATE_LORA
P_IN = RWKV_COLS + 2 * B_WIDTH + 2 * D_MODEL


def rms_norm(x, g):
    xf = x.astype(jnp.float32)
    y = xf * lax.rsqrt(jnp.mean(xf * xf, axis=-1, keepdims=True) + NORM_EPS)
    return (y * g.astype(jnp.float32)).astype(x.dtype)

def causal_dwconv(x, w, b):
    k_width = w.shape[0]
    s = x.shape[1]
    xp = jnp.pad(x, ((0, 0), (k_width - 1, 0), (0, 0)))
    y = b
    for j in range(k_width):
        y = y + xp[:, j:j + s] * w[j]
    return y

def token_shift(p):
    return jnp.pad(p, ((0, 0), (1, 0), (0, 0)))[:, :-1]

def rwkv7_recurrence(r, decay, k, v, a, b):
    def step(state, inp):
        r_t, w_t, k_t, v_t, a_t, b_t = inp
        sa = jnp.einsum('bhij,bhj->bhi', state, a_t)
        state = (state * w_t[:, :, None, :]
                 + sa[..., None] * b_t[:, :, None, :]
                 + v_t[..., None] * k_t[:, :, None, :])
        y_t = jnp.einsum('bhij,bhj->bhi', state, r_t)
        return state, y_t
    bsz, _, nh, nd = r.shape
    xs = tuple(jnp.swapaxes(t, 0, 1) for t in (r, decay, k, v, a, b))
    s0 = jnp.zeros((bsz, nh, nd, nd), jnp.float32)
    _, ys = lax.scan(step, s0, xs)
    return jnp.swapaxes(ys, 0, 1)

def rwkv7_branch(p, mu, w0, w_up, a0, a_up, g_up, k_k, k_a, r_k, lnx_g, lnx_b):
    bsz, s, _ = p.shape
    p = p.astype(jnp.float32)
    p = p + (token_shift(p) - p) * mu
    c0, c1, c2 = A_WIDTH, 2 * A_WIDTH, 3 * A_WIDTH
    c3, c4 = c2 + DECAY_LORA, c2 + DECAY_LORA + AAA_LORA
    r, k, v = p[..., :c0], p[..., c0:c1], p[..., c1:c2]
    pw, pa, pg = p[..., c2:c3], p[..., c3:c4], p[..., c4:]
    w_log = -jax.nn.softplus(-(w0 + jnp.tanh(pw) @ w_up)) - 0.5
    decay = jnp.exp(-jnp.exp(w_log))
    a = jax.nn.sigmoid(a0 + pa @ a_up)
    g = jax.nn.sigmoid(pg) @ g_up
    kk = k * k_k
    k = k * (1.0 + (a - 1.0) * k_a)
    hs = lambda t: t.reshape(bsz, s, A_HEADS, A_HEAD_DIM)
    r, k, v, kk, a, decay = hs(r), hs(k), hs(v), hs(kk), hs(a), hs(decay)
    kk = kk / jnp.maximum(jnp.sqrt(jnp.sum(kk * kk, axis=-1, keepdims=True)), 1e-12)
    y = rwkv7_recurrence(r, decay, k, v, -kk, kk * a)
    mean = jnp.mean(y, axis=-1, keepdims=True)
    var = jnp.mean(jnp.square(y - mean), axis=-1, keepdims=True)
    y = ((y - mean) * lax.rsqrt(var + LNX_EPS)).reshape(bsz, s, A_WIDTH) * lnx_g + lnx_b
    bonus = jnp.sum(r * k * r_k, axis=-1, keepdims=True) * v
    return (y + bonus.reshape(bsz, s, A_WIDTH)) * g

def _lin_combine(c1, c2):
    a1, b1 = c1
    a2, b2 = c2
    return a1 * a2, a2 * b1 + b2

def rglru_branch(px, py, conv_w, conv_b, w_ga, b_ga, w_gx, b_gx, lam):
    bsz, s, _ = px.shape
    xb = causal_dwconv(px.astype(jnp.float32), conv_w, conv_b)
    xh = xb.reshape(bsz, s, B_BLOCKS, B_BLOCK_DIM)
    gate_a = jax.nn.sigmoid(jnp.einsum('bshi,hij->bshj', xh, w_ga).reshape(bsz, s, B_WIDTH) + b_ga)
    gate_x = jax.nn.sigmoid(jnp.einsum('bshi,hij->bshj', xh, w_gx).reshape(bsz, s, B_WIDTH) + b_gx)
    log_a = LRU_C * gate_a * jax.nn.log_sigmoid(lam)
    a = jnp.exp(log_a)
    mult = jnp.sqrt(-jnp.expm1(2.0 * log_a))
    pos = jnp.arange(s)[None, :, None]
    mult = jnp.where(pos == 0, 1.0, mult)
    u = xb * gate_x * mult
    _, h = lax.associative_scan(_lin_combine, (a, u), axis=1)
    return h * jax.nn.gelu(py.astype(jnp.float32))

def cross_attention(h, m, w_q, w_kv, w_o):
    bsz, s, _ = h.shape
    q = (h @ w_q).reshape(bsz, s, X_HEADS, X_HEAD_DIM)
    kv = m @ w_kv
    k = kv[..., :D_MODEL].reshape(bsz, -1, X_HEADS, X_HEAD_DIM)
    v = kv[..., D_MODEL:].reshape(bsz, -1, X_HEADS, X_HEAD_DIM)
    sc = jnp.einsum('bqhd,bkhd->bhqk', q, k).astype(jnp.float32) * (X_HEAD_DIM ** -0.5)
    pr = jax.nn.softmax(sc, axis=-1).astype(v.dtype)
    o = jnp.einsum('bhqk,bkhd->bqhd', pr, v).reshape(bsz, s, D_MODEL)
    return o @ w_o

def conv_ffn(h, w_in, conv_w, conv_b, w_out):
    u = h @ w_in
    gate = causal_dwconv(u[..., :D_FF], conv_w, conv_b)
    return (jax.nn.gelu(gate) * u[..., D_FF:]) @ w_out

def second_inputs(seed: int = 0) -> dict:
    key = jax.random.key(seed)
    ks = iter(jax.random.split(key, 48))
    L = DEPTH_2
    f32 = jnp.float32

    def nrm(shape, scale):
        return jax.random.normal(next(ks), shape, f32) * scale

    u_lam = jax.random.uniform(next(ks), (L, B_WIDTH), f32, minval=0.9, maxval=0.999)
    return {
        "x": nrm((BATCH, SEQ, D_MODEL), 1.0),
        "mem": nrm((BATCH, N_MEM, D_MODEL), 1.0),
        "norm_mix_g": 1.0 + nrm((L, D_MODEL), 0.05),
        "w_in": nrm((L, D_MODEL, P_IN), D_MODEL ** -0.5),
        "b_in": nrm((L, P_IN), 0.02),
        "mu_shift": jax.random.uniform(next(ks), (L, RWKV_COLS), f32),
        "w0": nrm((L, A_WIDTH), 0.5) - 0.5,
        "w_lora_up": nrm((L, DECAY_LORA, A_WIDTH), 0.1),
        "a0": nrm((L, A_WIDTH), 0.5),
        "a_lora_up": nrm((L, AAA_LORA, A_WIDTH), AAA_LORA ** -0.5),
        "g_lora_up": nrm((L, GATE_LORA, A_WIDTH), GATE_LORA ** -0.5),
        "k_k": 0.85 + nrm((L, A_WIDTH), 0.05),
        "k_a": 1.0 + nrm((L, A_WIDTH), 0.05),
        "r_k": nrm((L, A_HEADS, A_HEAD_DIM), 0.1),
        "lnx_g": 1.0 + nrm((L, A_WIDTH), 0.05),
        "lnx_b": nrm((L, A_WIDTH), 0.02),
        "w_branch_a": nrm((L, A_WIDTH, D_MODEL), A_WIDTH ** -0.5),
        "conv_b_w": nrm((L, B_CONV, B_WIDTH), B_CONV ** -0.5),
        "conv_b_b": nrm((L, B_WIDTH), 0.02),
        "w_rg_a": nrm((L, B_BLOCKS, B_BLOCK_DIM, B_BLOCK_DIM), B_BLOCK_DIM ** -0.5),
        "b_rg_a": nrm((L, B_WIDTH), 0.02),
        "w_rg_x": nrm((L, B_BLOCKS, B_BLOCK_DIM, B_BLOCK_DIM), B_BLOCK_DIM ** -0.5),
        "b_rg_x": nrm((L, B_WIDTH), 0.02),
        "lru_lambda": jnp.log(u_lam) - jnp.log1p(-u_lam),
        "w_branch_b": nrm((L, B_WIDTH, D_MODEL), B_WIDTH ** -0.5),
        "w_mix_out": nrm((L, D_MODEL, D_MODEL), D_MODEL ** -0.5),
        "norm_x_g": 1.0 + nrm((L, D_MODEL), 0.05),
        "norm_mem_g": 1.0 + nrm((L, D_MODEL), 0.05),
        "w_cq": nrm((L, D_MODEL, D_MODEL), D_MODEL ** -0.5),
        "w_ckv": nrm((L, D_MODEL, 2 * D_MODEL), D_MODEL ** -0.5),
        "w_co": nrm((L, D_MODEL, D_MODEL), D_MODEL ** -0.5),
        "norm_ffn_g": 1.0 + nrm((L, D_MODEL), 0.05),
        "w_ffn_in": nrm((L, D_MODEL, 2 * D_FF), D_MODEL ** -0.5),
        "ffn_conv_w": nrm((L, FFN_CONV, D_FF), FFN_CONV ** -0.5),
        "ffn_conv_b": nrm((L, D_FF), 0.02),
        "w_ffn_out": nrm((L, D_FF, D_MODEL), D_FF ** -0.5),
        "norm_final_g": 1.0 + nrm((D_MODEL,), 0.05),
    }

def second_block(x, mem, norm_mix_g, w_in, b_in, mu_shift, w0, w_lora_up, a0, a_lora_up,
              g_lora_up, k_k, k_a, r_k, lnx_g, lnx_b, w_branch_a, conv_b_w, conv_b_b,
              w_rg_a, b_rg_a, w_rg_x, b_rg_x, lru_lambda, w_branch_b, w_mix_out,
              norm_x_g, norm_mem_g, w_cq, w_ckv, w_co, norm_ffn_g, w_ffn_in,
              ffn_conv_w, ffn_conv_b, w_ffn_out, norm_final_g):
    dt = x.dtype
    cb0 = RWKV_COLS
    cb1 = cb0 + B_WIDTH
    cb2 = cb1 + B_WIDTH
    cg1 = cb2 + D_MODEL
    for l in range(DEPTH_2):
        h = rms_norm(x, norm_mix_g[l])
        proj = h @ w_in[l] + b_in[l]
        y_a = rwkv7_branch(proj[..., :cb0], mu_shift[l], w0[l], w_lora_up[l], a0[l],
                           a_lora_up[l], g_lora_up[l], k_k[l], k_a[l], r_k[l],
                           lnx_g[l], lnx_b[l]).astype(dt) @ w_branch_a[l]
        y_b = rglru_branch(proj[..., cb0:cb1], proj[..., cb1:cb2], conv_b_w[l], conv_b_b[l],
                           w_rg_a[l], b_rg_a[l], w_rg_x[l], b_rg_x[l],
                           lru_lambda[l]).astype(dt) @ w_branch_b[l]
        merged = (jax.nn.sigmoid(proj[..., cb2:cg1]) * y_a
                  + jax.nn.sigmoid(proj[..., cg1:]) * y_b)
        x = x + merged @ w_mix_out[l]
        x = x + cross_attention(rms_norm(x, norm_x_g[l]), rms_norm(mem, norm_mem_g[l]),
                                w_cq[l], w_ckv[l], w_co[l])
        x = x + conv_ffn(rms_norm(x, norm_ffn_g[l]), w_ffn_in[l], ffn_conv_w[l],
                         ffn_conv_b[l], w_ffn_out[l])
    return rms_norm(x, norm_final_g)


def setup_inputs(seed=0):
    out = dict(first_inputs(seed))
    for name, value in second_inputs(seed + 1).items():
        if name != "x":
            out[name + "_2"] = value
    return out


def reference(
    x, norm1, w_in, dn_conv, dn_a_log, dn_dt_bias, dn_onorm, fx_qnorm, fx_knorm, fx_f_bias,
    pool_w, pool_scale, w_out, norm2, ffn_gate, ffn_up, ffn_down, router, moe_gate, moe_up,
    moe_down, mem_2, norm_mix_g_2, w_in_2, b_in_2, mu_shift_2, w0_2, w_lora_up_2, a0_2,
    a_lora_up_2, g_lora_up_2, k_k_2, k_a_2, r_k_2, lnx_g_2, lnx_b_2, w_branch_a_2, conv_b_w_2,
    conv_b_b_2, w_rg_a_2, b_rg_a_2, w_rg_x_2, b_rg_x_2, lru_lambda_2, w_branch_b_2, w_mix_out_2,
    norm_x_g_2, norm_mem_g_2, w_cq_2, w_ckv_2, w_co_2, norm_ffn_g_2, w_ffn_in_2, ffn_conv_w_2,
    ffn_conv_b_2, w_ffn_out_2, norm_final_g_2,
):
    x = first_block(
        x, norm1, w_in, dn_conv, dn_a_log, dn_dt_bias, dn_onorm, fx_qnorm, fx_knorm, fx_f_bias,
        pool_w, pool_scale, w_out, norm2, ffn_gate, ffn_up, ffn_down, router, moe_gate, moe_up,
        moe_down,
    )
    return second_block(
        x, mem_2, norm_mix_g_2, w_in_2, b_in_2, mu_shift_2, w0_2, w_lora_up_2, a0_2,
        a_lora_up_2, g_lora_up_2, k_k_2, k_a_2, r_k_2, lnx_g_2, lnx_b_2, w_branch_a_2,
        conv_b_w_2, conv_b_b_2, w_rg_a_2, b_rg_a_2, w_rg_x_2, b_rg_x_2, lru_lambda_2,
        w_branch_b_2, w_mix_out_2, norm_x_g_2, norm_mem_g_2, w_cq_2, w_ckv_2, w_co_2,
        norm_ffn_g_2, w_ffn_in_2, ffn_conv_w_2, ffn_conv_b_2, w_ffn_out_2, norm_final_g_2,
    )


_drawn_inputs = setup_inputs


def setup_inputs(seed=0):
    import zlib

    import numpy as np

    out = dict(_drawn_inputs(seed))
    spreads = {}
    factors = {'fx_qnorm': 3.849,
     'fx_knorm': 3.444,
     'b_in_2': 2.725,
     'k_k_2': 8.0,
     'k_a_2': 3.254,
     'lnx_g_2': 4.09,
     'lnx_b_2': 8.0,
     'conv_b_b_2': 3.892,
     'b_rg_a_2': 8.0,
     'b_rg_x_2': 8.0,
     'norm_x_g_2': 8.0,
     'norm_mem_g_2': 7.849,
     'ffn_conv_b_2': 33.618,
     'norm_ffn_g_2': 8.0}
    for name, (base, spread) in spreads.items():
        noise = np.random.default_rng([zlib.crc32(name.encode()), seed]).standard_normal(out[name].shape)
        drawn = base * np.exp(spread * noise) if base else spread * noise
        out[name] = __import__('jax').numpy.asarray(drawn.astype(out[name].dtype))
    for name, factor in factors.items():
        out[name] = (out[name] * factor).astype(out[name].dtype)
    return out
```

```python
import math
from contextlib import ExitStack

import concourse.bass as bass
from concourse import mybir

F32 = mybir.dt.float32
F32R = mybir.dt.float32r
ALU = mybir.AluOpType
ACT = mybir.ActivationFunctionType
AX = mybir.AxisListType

P = 128
T = 512
D = 1024
DT = D // P
TT = T // P
HD = 64
CH = 64
NCH = T // CH
EPS = 1e-6
BANK = 512
SLOT = 3 * DT * P


class Machine:

    def __init__(self, nc, ins, out):
        self.nc, self.ins, self.out = nc, ins, out
        self.columns = {}
        self.phases = 0
        self.free_sems, self.cleared_sems = [], []

    def name(self, what):
        self.phases += 1
        return f"{what}_{self.phases}"


class Phase(ExitStack):

    def __init__(self, m, what):
        super().__init__()
        self.m, self.nc, self.what, self.sems = m, m.nc, m.name(what), []

    def sb(self, name, shape, dt=F32):
        return self.enter_context(self.nc.sbuf_tensor(f"{self.what}_{name}", shape, dt))

    def banks(self, n=8):
        return self.enter_context(self.nc.psum_tensor(f"{self.what}_psum", [P, n, BANK], F32))

    def sem(self, name):
        s = self.m.free_sems.pop() if self.m.free_sems else self.nc.alloc_semaphore(f"{name}_{self.what}")
        self.sems.append(s)
        return s

    def __exit__(self, *error):
        result = super().__exit__(*error)
        if error[0] is None and self.sems:
            for s in self.sems:
                self.nc.gpsimd.sem_clear(s)
            self.m.free_sems += self.m.cleared_sems
            self.m.cleared_sems = self.sems
        return result


def k_major(w):
    return w.rearrange("(k p) n -> p k n", p=P)




def row_params(m):
    rows = []

    def vector(name, ap, n, width=P, twice=False):
        src = ap.rearrange("(k p) -> k p", p=width)
        rows.append((name, src, n // width, width, twice))

    i = m.ins
    for l in range(2):
        vector(f"norm1_{l}", i["norm1"][l], D)
        vector(f"norm2_{l}", i["norm2"][l], D)
        for j in range(4):
            vector(f"dn_conv_{l}_{j}", i["dn_conv"][l, j], 9 * P)
        vector(f"dn_onorm_{l}", i["dn_onorm"][l], HD, HD, True)
        vector(f"fx_qnorm_{l}", i["fx_qnorm"][l], HD, HD, True)
        vector(f"fx_knorm_{l}", i["fx_knorm"][l], HD, HD, True)
        vector(f"pool_scale_{l}", i["pool_scale"][l], 2 * P)
        vector(f"a_log_{l}", i["dn_a_log"][l], 6, 6)
        vector(f"dt_bias_{l}", i["dn_dt_bias"][l], 6, 6)
        vector(f"f_bias_{l}", i["fx_f_bias"][l], 6, 6)
    for name, n in (("norm_mix_g", D), ("norm_x_g", D), ("norm_mem_g", D), ("norm_ffn_g", D), ("b_in", 4864),
                    ("mu_shift", 1792), ("w0", 512), ("a0", 512), ("k_k", 512), ("k_a", 512), ("lnx_g", 512),
                    ("lnx_b", 512), ("conv_b_b", 512), ("b_rg_a", 512), ("b_rg_x", 512), ("lru_lambda", 512),
                    ("ffn_conv_b", 2816)):
        vector(name, i[name + "_2"][0], n)
    vector("norm_final_g", i["norm_final_g_2"], D)
    vector("r_k", i["r_k_2"][0].rearrange("h d -> (h d)"), 512)
    for j in range(4):
        vector(f"conv_b_w_{j}", i["conv_b_w_2"][0, j], 512)
    for j in range(3):
        vector(f"ffn_conv_w_{j}", i["ffn_conv_w_2"][0, j], 2816)
    return rows


def setup_phase(m, persist):
    nc = m.nc
    rows = row_params(m)
    total = sum(n for _, _, n, _, _ in rows)
    stages = -(-total // P)
    m.ident = persist.sb("ident", [P, P])
    m.ones = persist.sb("ones", [P, P])
    m.pair_ones = persist.sb("pair_ones", [P, P])
    m.params = persist.sb("params", [P, stages * P])
    m.xT = persist.sb("xT", [P, DT, T])
    m.act_hi = persist.sb("act_hi", [P, DT, T], F32R)
    m.act_lo = persist.sb("act_lo", [P, DT, T], F32R)
    m.eps = persist.sb("eps", [P, 1])
    with Phase(m, "setup") as ph:
        stage = ph.sb("stage", [P, stages, P])
        xs = ph.sb("xs", [P, TT, D])
        ps = ph.banks()
        zeroed, filled, const = ph.sem("zeroed"), ph.sem("filled"), ph.sem("const")
        x_landed, turned, copied = ph.sem("x_landed"), ph.sem("turned"), ph.sem("copied")
        block = ph.enter_context(nc.Block())
        places, at = [], 0
        for name, src, n, width, twice in rows:
            m.columns[name] = at
            done = 0
            while done < n:
                k = min(n - done, P - at % P)
                for o in (0, HD) if twice else (0,):
                    places.append((at // P, at % P, k, o, width, src[done:done + k, :]))
                at += k
                done += k

        @block.gpsimd
        def _(pool):
            pool.memset(stage[:, :, :], 0.0).then_inc(zeroed, 1)
            pool.memset(m.ident[:, :], 0.0).then_inc(const, 1)
            pool.memset(m.ones[:, :], 1.0).then_inc(const, 1)
            pool.memset(m.eps[:, :], EPS).then_inc(const, 1)
            pool.memset(m.pair_ones[:, :], 0.0).then_inc(const, 1)
            pool.wait_ge(const, 4)
            pool.memset(m.pair_ones[0:HD, 0:HD], 1.0).then_inc(const, 1)
            pool.memset(m.pair_ones[HD:P, HD:P], 1.0).then_inc(const, 1)
            pool.wait_ge(const, 6)
            pool.affine_select(out=m.ident[:, :], in_=m.ident[:, :], compare_op=ALU.not_equal, fill=1.0, base=0,
                               pattern=[[-1, P]], channel_multiplier=1).then_inc(const, 1)

        @block.sync
        def _(sp):
            sp.dma_start(xs[:, :, :], m.ins["x"][0].rearrange("(t p) d -> p t d", p=P)).then_inc(x_landed, 16)
            sp.wait_ge(zeroed, 1)
            for s, r, k, o, width, src in places:
                sp.dma_start(stage[r:r + k, s, o:o + width], src).then_inc(filled, 16)

        jobs = [("x", k) for k in range(DT)] + [("param", s) for s in range(stages)]

        @block.tensor
        def _(pe):
            pe.wait_ge(const, 7)
            pe.wait_ge(x_landed, 16)
            for n, (kind, k) in enumerate(jobs):
                if n >= 8:
                    pe.wait_ge(copied, n - 7)
                if kind == "x":
                    for t in range(TT):
                        last = pe.transpose(ps[:, n % 8, t * P:(t + 1) * P], xs[:, t, k * P:(k + 1) * P], m.ident[:, :])
                else:
                    if k == 0:
                        pe.wait_ge(filled, 16 * len(places))
                    last = pe.transpose(ps[:, n % 8, 0:P], stage[:, k, :], m.ident[:, :])
                last.then_inc(turned, 1)

        @block.vector
        def _(dve):
            for n, (kind, k) in enumerate(jobs):
                dve.wait_ge(turned, n + 1)
                dst, w = (m.xT[:, k, :], T) if kind == "x" else (m.params[:, k * P:(k + 1) * P], P)
                dve.tensor_copy(dst, ps[:, n % 8, 0:w]).then_inc(copied, 1)


def col(m, name, k=0):
    c = m.columns[name] + k
    return m.params[:, c:c + 1]




def norm_phase(m, x, gain, hi, lo, nt=DT, n=T, full=None):
    nc = m.nc
    with Phase(m, "norm") as ph:
        sq = full if full is not None else ph.sb("sq", [P, nt, n])
        rstd = ph.sb("rstd", [P, n])
        ps = ph.banks(1)
        squared, summed, root, scaled, rounded = (ph.sem(s) for s in ("squared", "summed", "root", "scaled", "rounded"))
        block = ph.enter_context(nc.Block())

        @block.scalar
        def _(act):
            for k in range(nt):
                act.activation(sq[:, k, :], x[:, k, :], ACT.Square).then_inc(squared, 1)
            act.wait_ge(summed, 1)
            act.activation(rstd[:, :], ps[:, 0, 0:n], ACT.Ln, scale=1.0 / D, bias=m.eps[:, 0:1]).then_inc(root, 1)
            act.wait_ge(root, 1)
            act.activation(rstd[:, :], rstd[:, :], ACT.Exp, scale=-0.5).then_inc(root, 1)
            for k in range(nt):
                act.wait_ge(scaled, k + 1)
                act.activation(hi[:, k, :], sq[:, k, :], ACT.Copy).then_inc(rounded, 1)

        @block.tensor
        def _(pe):
            for k in range(nt):
                pe.wait_ge(squared, k + 1)
                last = pe.matmul(ps[:, 0, 0:n], m.ones[:, :], sq[:, k, :], start=k == 0, stop=k == nt - 1)
            last.then_inc(summed, 1)

        @block.vector
        def _(dve):
            dve.wait_ge(root, 2)
            for k in range(nt):
                dve.scalar_tensor_tensor(out=sq[:, k, :], in0=x[:, k, :], scalar=col(m, gain, k), in1=rstd[:, :],
                                         op0=ALU.mult, op1=ALU.mult).then_inc(scaled, 1)
            for k in range(nt):
                dve.wait_ge(rounded, k + 1)
                dve.tensor_tensor(lo[:, k, :], sq[:, k, :], hi[:, k, :].bitcast(F32), ALU.subtract).then_inc(scaled, 1)




class Job:

    def __init__(self, groups, nf, load, hi, lo, dve, act=None, kt=DT, parts=1, n=T, loads=1, after=None):
        self.groups, self.nf, self.load, self.hi, self.lo = groups, nf, load, hi, lo
        self.dve, self.act, self.kt, self.parts, self.n, self.loads, self.after = dve, act, kt, parts, n, loads, after
        assert kt * nf * P <= SLOT and nf <= 4


def over_groups(eng, groups, body):
    pairs = groups // 2
    if pairs > 1:
        with eng.Fori(0, pairs) as i:
            for k in range(2):
                body(i, k)
    else:
        for g in range(2 * pairs):
            body(0, g)
    if groups % 2:
        body(pairs, 0)


def dense_phase(m, make_jobs, what="dense"):
    nc = m.nc
    with Phase(m, what) as ph:
        raw = [ph.sb(f"raw{s}", [P, SLOT]) for s in range(2)]
        w_hi = [ph.sb(f"w_hi{s}", [P, SLOT], F32R) for s in range(2)]
        w_lo = [ph.sb(f"w_lo{s}", [P, SLOT], F32R) for s in range(2)]
        ps = ph.banks()
        landed = [ph.sem("landed0"), ph.sem("landed1")]
        rounded, split, used, full, taken = (ph.sem(s) for s in ("rounded", "split", "used", "full", "taken"))
        jobs = make_jobs(ph, ps)
        block = ph.enter_context(nc.Block())
        unit0, group0, land0 = [], [], []
        u = g = 0
        at = [0, 0]
        for job in jobs:
            unit0.append(u)
            group0.append(g)
            land0.append(tuple(at))
            for r in range(job.groups * job.parts):
                at[(u + r) % 2] += 16 * job.loads
            u += job.groups * job.parts
            g += job.groups

        def place(j, i, k, c):
            job = jobs[j]
            r = k * job.parts + c
            slot = (unit0[j] + r) % 2
            return slot, i * (2 * job.parts) + (unit0[j] + r), (
                i * (16 * job.loads * job.parts) + (land0[j][slot] + 16 * job.loads * (r // 2 + 1)))

        def bank(j, k):
            return 4 * ((group0[j] + k) % 2)

        @block.sync
        def _(sp):
            for j, job in enumerate(jobs):
                def body(i, k, j=j, job=job):
                    for c in range(job.parts):
                        slot, unit, _ = place(j, i, k, c)
                        sp.wait_ge(split, unit + 1)
                        dst = raw[slot][:, 0:job.kt * job.nf * P].rearrange("p (k n) -> p k n", k=job.kt)
                        for first, width, src in job.load(i * 2 + k, c):
                            sp.dma_start(dst[:, :, first:first + width], src).then_inc(landed[slot], 16)

                over_groups(sp, job.groups, body)

        def walk(eng, split_unit, empty):

            def split_group(j, i, k):
                for c in range(jobs[j].parts):
                    split_unit(j, i, k, c)

            split_group(0, 0, 0)
            for j, job in enumerate(jobs):
                looped = (job.groups - 1) // 2

                def pair(i, j=j):
                    split_group(j, i, 1)
                    empty(j, i, 0)
                    split_group(j, i + 1, 0)
                    empty(j, i, 1)

                if looped > 1:
                    with eng.Fori(0, looped) as i:
                        pair(i)
                elif looped:
                    pair(0)
                for g in range(2 * looped, job.groups):
                    if g + 1 < job.groups:
                        split_group(j, (g + 1) // 2, (g + 1) % 2)
                    elif j + 1 < len(jobs):
                        split_group(j + 1, 0, 0)
                    empty(j, g // 2, g % 2)

        @block.scalar
        def _(act):
            def round_unit(j, i, k, c):
                slot, unit, land = place(j, i, k, c)
                n = jobs[j].kt * jobs[j].nf * P
                act.wait_ge(landed[slot], land)
                act.wait_ge(used, unit + 1)
                act.activation(w_hi[slot][:, 0:n], raw[slot][:, 0:n], ACT.Copy).then_inc(rounded, 1)

            def empty(j, i, k):
                if jobs[j].act:
                    act.wait_ge(full, i * 2 + (group0[j] + k + 1))
                    jobs[j].act(act, i * 2 + k, bank(j, k), i * 2 + (k + 1))

            walk(act, round_unit, empty)

        @block.vector
        def _(dve):
            dve.nop().then_inc(split, 2)
            dve.nop().then_inc(taken, 2)

            def rest_unit(j, i, k, c):
                slot, unit, _ = place(j, i, k, c)
                n = jobs[j].kt * jobs[j].nf * P
                dve.wait_ge(rounded, unit + 1)
                dve.tensor_tensor(w_lo[slot][:, 0:n], raw[slot][:, 0:n], w_hi[slot][:, 0:n].bitcast(F32),
                                  ALU.subtract).then_inc(split, 1)

            def empty(j, i, k):
                dve.wait_ge(full, i * 2 + (group0[j] + k + 1))
                dve.wait_ge(taken, i * 2 + (group0[j] + k + 2))
                jobs[j].dve(dve, i * 2 + k, bank(j, k), i * 2 + (k + 1)).then_inc(taken, 1)

            walk(dve, rest_unit, empty)

        @block.tensor
        def _(pe):
            pe.nop().then_inc(used, 2)
            for j, job in enumerate(jobs):
                if job.after is not None:
                    pe.wait_ge(taken, 2 + group0[job.after] + jobs[job.after].groups)

                def body(i, k, j=j, job=job):
                    pe.wait_ge(taken, i * 2 + (group0[j] + k + 1))
                    for c in range(job.parts):
                        slot, unit, _ = place(j, i, k, c)
                        pe.wait_ge(split, unit + 3)
                        hi = w_hi[slot][:, 0:job.kt * job.nf * P].rearrange("p (k n) -> p k n", k=job.kt)
                        lo = w_lo[slot][:, 0:job.kt * job.nf * P].rearrange("p (k n) -> p k n", k=job.kt)
                        for f in range(job.nf):
                            out = ps[:, bank(j, k) + f, 0:job.n]
                            for t in range(job.kt):
                                x_hi, x_lo = (x[:, c * job.kt + t, :] for x in (job.hi, job.lo))
                                cols = slice(f * P, (f + 1) * P)
                                first, end = c == 0 and t == 0, c == job.parts - 1 and t == job.kt - 1
                                pe.matmul(out, lo[:, t, cols], x_hi, start=first, stop=False)
                                pe.matmul(out, hi[:, t, cols], x_lo, start=False, stop=False)
                                last = pe.matmul(out, hi[:, t, cols], x_hi, start=False, stop=end)
                        if c == job.parts - 1:
                            last.then_inc(full, 1)
                            pe.wait_ge(full, i * 2 + (group0[j] + k + 1))
                            pe.nop().then_inc(used, 1)
                        else:
                            last.then_inc(used, 1)

                over_groups(pe, job.groups, body)


def swiglu_jobs(m, ph, ps, gate, up, down, ft, kt_down, parts_down, weight=None):
    hid_hi = ph.sb("hid_hi", [P, ft, T], F32R)
    hid_lo = ph.sb("hid_lo", [P, ft, T], F32R)
    s, h = ph.sb("s", [P, T]), ph.sb("h", [P, T])
    silu_done, h_done, h_rounded, weighed = (ph.sem(n) for n in ("silu_done", "h_done", "h_rounded", "weighed"))

    def load(g, c):
        return [(0, P, k_major(gate)[:, :, bass.ds(g * P, P)]), (P, P, k_major(up)[:, :, bass.ds(g * P, P)])]

    def act(eng, g, b, n, src=None, func=ACT.Silu):
        eng.activation(s[:, :], ps[:, b, :] if src is None else src, func).then_inc(silu_done, 1)
        eng.wait_ge(h_done, n)
        eng.activation(hid_hi[:, bass.ds(g, 1), :], h[:, :], ACT.Copy).then_inc(h_rounded, 1)

    def dve(eng, g, b, n):
        eng.wait_ge(silu_done, n)
        eng.tensor_tensor(h[:, :], s[:, :], ps[:, b + 1, :], ALU.mult).then_inc(h_done, 1)
        eng.wait_ge(h_rounded, n)
        return eng.tensor_tensor(hid_lo[:, bass.ds(g, 1), :], h[:, :], hid_hi[:, bass.ds(g, 1), :].bitcast(F32), ALU.subtract)

    nf = 4 if kt_down <= 6 else 2

    def load_down(g, c):
        src = down[:, :].rearrange("(c k p) n -> c p k n", p=P, k=kt_down)[c]
        return [(0, nf * P, src[:, :, bass.ds(g * (nf * P), nf * P)])]

    def dve_down(eng, g, b, n):
        if weight is not None:
            view = ps[:, b:b + nf, :]
            eng.tensor_tensor(view, view, weight.unsqueeze(1).to_broadcast([P, nf, T]), ALU.mult).then_inc(weighed, 1)
            eng.wait_ge(weighed, n)
        dst = m.xT[:, bass.ds(g * nf, nf), :]
        return eng.tensor_tensor(dst, dst, ps[:, b:b + nf, :], ALU.add)

    return [Job(ft, 2, load, m.act_hi, m.act_lo, dve, act, loads=2),
            Job(DT // nf, nf, load_down, hid_hi, hid_lo, dve_down, kt=kt_down, parts=parts_down, after=0)]


def ffn_phase(m):
    gate, up, down = m.ins["ffn_gate"][0], m.ins["ffn_up"][0], m.ins["ffn_down"][0]
    half = 11
    for s in range(2):
        f = slice(s * half * P, (s + 1) * half * P)
        dense_phase(m, lambda ph, ps: swiglu_jobs(m, ph, ps, gate[:, f], up[:, f], down[f, :], half, half, 1), "ffn")




def out_phase(m, x):
    nc = m.nc
    with Phase(m, "out") as ph:
        rows = ph.sb("rows", [P, TT, D])
        ps = ph.banks()
        turned, copied, stored = ph.sem("turned"), ph.sem("copied"), ph.sem("stored")
        block = ph.enter_context(nc.Block())

        @block.tensor
        def _(pe):
            for n in range(2 * TT):
                if n >= 8:
                    pe.wait_ge(copied, n - 7)
                for k in range(4):
                    last = pe.transpose(ps[:, n % 8, k * P:(k + 1) * P], x[:, 4 * (n % 2) + k, (n // 2) * P:(n // 2 + 1) * P],
                                        m.ident[:, :])
                last.then_inc(turned, 1)

        @block.vector
        def _(dve):
            for n in range(2 * TT):
                dve.wait_ge(turned, n + 1)
                dve.tensor_copy(rows[:, n // 2, (n % 2) * BANK:(n % 2 + 1) * BANK], ps[:, n % 8, :]).then_inc(copied, 1)

        @block.sync
        def _(sp):
            for t in range(TT):
                sp.wait_ge(copied, 2 * t + 2)
                sp.dma_start(m.out[0, t * P:(t + 1) * P, :], rows[:, t, :]).then_inc(stored, 16)
            sp.wait_ge(stored, 16 * TT)




def masks_phase(m, persist):
    nc = m.nc
    m.upto = persist.sb("upto", [P, P])
    m.before = persist.sb("before", [P, P])
    m.level = persist.sb("level", [P, 6, P])
    m.reset = persist.sb("reset", [P, T])
    m.head_rows = persist.sb("head_rows", [P, 3 * P])
    m.causal = persist.sb("causal", [P, P])
    with Phase(m, "masks") as ph:
        done = ph.sem("done")
        block = ph.enter_context(nc.Block())

        @block.gpsimd
        def _(pool):
            n = [0]

            def step(ins):
                n[0] += 1
                ins.then_inc(done, 1)
                pool.wait_ge(done, n[0])

            def keep(view, base, pattern, mult, op=ALU.is_ge, fill=0.0):
                step(pool.affine_select(out=view, in_=view, compare_op=op, fill=fill, base=base, pattern=pattern,
                                        channel_multiplier=mult))

            for mask, base in ((m.upto, 0), (m.before, -1)):
                step(pool.memset(mask[:, :], 0.0))
                for o in (0, CH):
                    step(pool.memset(mask[o:o + CH, o:o + CH], 1.0))
                    keep(mask[o:o + CH, o:o + CH], base, [[1, CH]], -1)
            for l in range(6):
                b = 1 << l
                blocks = P // (2 * b)
                mask = m.level[:, l, :]
                step(pool.memset(mask, 1.0))
                keep(mask, 0, [[-2 * b, blocks], [0, 2], [0, b]], 1)
                keep(mask, b - 1, [[2 * b, blocks], [0, 2], [0, b]], -1)
                step(pool.memset(mask.rearrange("p (j h b) -> p j h b", h=2, b=b)[:, :, 0, :], 0.0))
            step(pool.memset(m.reset[:, :], 1.0))
            step(pool.memset(m.reset[:, :].rearrange("p (c t) -> p c t", t=CH)[:, :, 0:1], 0.0))
            step(pool.memset(m.head_rows[:, :], 1.0))
            keep(m.head_rows[:, :], 0, [[1, 3 * P]], -HD)
            keep(m.head_rows[:, :], HD - 1, [[-1, 3 * P]], HD)
            step(pool.memset(m.causal[:, :], 0.0))
            keep(m.causal[:, :], 0, [[-1, P]], 1, fill=-1e30)




class Rule:
    pass


def chunk_phase(m, r):
    nc = m.nc
    H, pairs = r.heads, r.heads // 2
    L = 6
    with Phase(m, "chunk") as ph:
        nt = ph.sb("nt", [P, 2, TT, P])
        nb = ph.sb("nb", [P, 2, TT, P])
        x = ph.sb("x", [P, 2, TT, P])
        xt = ph.sb("xt", [P, 2, TT, P])
        p1 = ph.sb("p1", [P, 2, TT, P])
        if r.decayed:
            dec = ph.sb("dec", [P, 2, TT, P])
            own = ph.sb("own", [HD, 2, T])
        else:
            ak = ph.sb("ak", [P, 2, TT, P])
            qk = ph.sb("qk", [P, 2, TT, P])
            z = ph.sb("z", [P, 2, TT, HD])
        ps = ph.banks()
        own_ready, raw, low, low2, exped, formed, masked = (ph.sem(s) for s in ("own", "raw", "low", "low2", "exped", "formed", "masked"))
        p1_full, p1_kept, x_full, xt_full, x_new, xt_new = (
            ph.sem(s) for s in ("p1_full", "p1_kept", "x_full", "xt_full", "x_new", "xt_new"))
        z_full, z_kept, post_full, post_kept = (ph.sem(s) for s in ("z_full", "z_kept", "post_full", "post_kept"))
        block = ph.enter_context(nc.Block())
        heads = [(p, k, 2 * p + k, k * HD) for p in range(pairs) for k in range(2)]
        tile = lambda t: slice(t * P, (t + 1) * P)
        n_forms = 2 if r.decayed else 4
        n_post = 2 if r.decayed else 3
        four = lambda mask: mask[:, :].unsqueeze(1).to_broadcast([P, TT, P])

        @block.gpsimd
        def _(pool):
            for p in range(pairs):
                if r.decayed:
                    for k in range(2):
                        h = 2 * p + k
                        if p:
                            pool.wait_ge(raw, 3 * (h - 1))
                        pool.tensor_scalar(own[:, k, :], r.rhs_rows[0:HD, :], r.row_of_head[0:HD, h:h + 1], None,
                                           ALU.mult).then_inc(own_ready, 1)
                for l in range(L):
                    for k in range(2):
                        s = (p * L + l) * 2 + k
                        pool.wait_ge(formed, n_forms * (2 * p + k + 1))
                        if s >= 2:
                            pool.wait_ge(p1_full, s - 1)
                        pool.tensor_tensor(nb[:, k], nt[:, k], four(m.level[:, l, :]), ALU.mult).then_inc(masked, 1)

        @block.tensor
        def _(pe):
            for p in range(pairs):
                for k in range(2):
                    h, o, b = 2 * p + k, k * HD, 4 * k
                    if p:
                        pe.wait_ge(post_kept, n_post * (h - 1))
                    rows = slice(o, o + HD)
                    if r.decayed:
                        pe.wait_ge(own_ready, h + 1)
                        products = [(b, None, None), (b + 1, r.k_t, r.a_t), (b + 2, r.k_t, r.q_t)]
                    else:
                        products = [(b, r.k_t, r.a_t), (b + 1, r.b_t, r.a_t), (b + 2, r.b_t, r.q_t), (b + 3, r.k_t, r.q_t)]
                    for bank, lhs, rhs in products:
                        for t in range(TT):
                            if lhs is None:
                                last = pe.matmul(ps[:, bank, tile(t)], r.lhs_rows[0:HD, tile(t)], own[:, k, tile(t)],
                                                 start=True, stop=True)
                            else:
                                last = pe.matmul(ps[:, bank, tile(t)], lhs[rows, p, tile(t)], rhs[rows, p, tile(t)],
                                                 start=True, stop=True)
                        last.then_inc(raw, 1)
                for l in range(L):
                    for k in range(2):
                        s, h = (p * L + l) * 2 + k, 2 * p + k
                        pe.wait_ge(masked, s + 1)
                        pe.wait_ge(formed, n_forms * (h + 1))
                        if l:
                            pe.wait_ge(x_new, s - 1)
                        for t in range(TT):
                            last = pe.matmul(ps[:, 4 * k, tile(t)], nb[:, k, t, :], x[:, k, t, :] if l else m.ident[:, :],
                                             start=True, stop=True)
                        last.then_inc(p1_full, 1)
                    for k in range(2):
                        s = (p * L + l) * 2 + k
                        pe.wait_ge(p1_kept, s + 1)
                        if l:
                            pe.wait_ge(xt_new, s - 1)
                        for t in range(TT):
                            last = pe.matmul(ps[:, 4 * k + 1, tile(t)], xt[:, k, t, :] if l else m.ident[:, :], p1[:, k, t, :],
                                             start=True, stop=True)
                        last.then_inc(x_full, 1)
                        for t in range(TT):
                            last = pe.matmul(ps[:, 4 * k + 2, tile(t)], p1[:, k, t, :], xt[:, k, t, :] if l else m.ident[:, :],
                                             start=True, stop=True)
                        last.then_inc(xt_full, 1)
                for k in range(2):
                    s, h, o, b = (p * L + L - 1) * 2 + k, 2 * p + k, k * HD, 4 * k
                    cols = slice(p * P + o, p * P + o + HD)
                    if not r.decayed:
                        for t in range(TT):
                            last = pe.matmul(ps[:, b, t * HD:(t + 1) * HD], ak[:, k, t, :], r.v_tok[:, t, cols], start=True, stop=True)
                        last.then_inc(z_full, 1)
                        for t in range(TT):
                            last = pe.matmul(ps[o:o + HD, b + 3, tile(t)], r.v_tok[:, t, cols], qk[:, k, t, :], start=True, stop=True)
                        last.then_inc(post_full, 1)
                    pe.wait_ge(xt_new, s + 1)
                    for t in range(TT):
                        last = pe.matmul(ps[o:o + HD, b + 2, tile(t)], r.a_tok[:, t, cols], xt[:, k, t, :], start=True, stop=True)
                    last.then_inc(post_full, 1)
                    if not r.decayed:
                        pe.wait_ge(z_kept, h + 1)
                    pe.wait_ge(x_new, s + 1)
                    for t in range(TT):
                        last = pe.matmul(ps[:, b + 1, t * HD:(t + 1) * HD], xt[:, k, t, :],
                                         r.z_tok[:, t, cols] if r.decayed else z[:, k, t, :], start=True, stop=True)
                    last.then_inc(post_full, 1)

        @block.scalar
        def _(act):
            for p in range(pairs):
                if r.decayed:
                    for k in range(2):
                        h = 2 * p + k
                        act.wait_ge(low, h + 1)
                        act.activation(dec[:, k], dec[:, k], ACT.Exp).then_inc(exped, 1)
                for l in range(L):
                    for k in range(2):
                        s = (p * L + l) * 2 + k
                        act.wait_ge(p1_full, s + 1)
                        if s >= 2:
                            act.wait_ge(xt_full, s - 1)
                        act.activation(p1[:, k], ps[:, 4 * k, :].rearrange("p (t n) -> p t n", t=TT), ACT.Copy).then_inc(p1_kept, 1)

        @block.vector
        def _(dve):
            view = lambda b: ps[:, b, :].rearrange("p (t n) -> p t n", t=TT)
            for p in range(pairs):
                for k in range(2):
                    h, b = 2 * p + k, 4 * k
                    if p:
                        dve.wait_ge(masked, p * L * 2)
                        dve.wait_ge(post_kept, n_post * (h - 1))
                    if r.decayed:
                        dve.wait_ge(raw, 3 * h + 1)
                        dve.wait_ge(formed, n_forms * h) if h else None
                        dve.tensor_scalar(dec[:, k], view(b), 0.0, None, ALU.min).then_inc(low, 1)
                        dve.wait_ge(exped, h + 1)
                        dve.tensor_tensor(dec[:, k], dec[:, k], four(m.upto), ALU.mult).then_inc(low2, 1)
                        dve.wait_ge(low2, h + 1)
                        dve.wait_ge(raw, 3 * h + 3)
                        dve.tensor_tensor(nt[:, k], view(b + 1), dec[:, k], ALU.mult).then_inc(formed, 1)
                        dve.tensor_tensor(r.qb[:, h], view(b + 2), dec[:, k], ALU.mult).then_inc(formed, 1)
                    else:
                        for n, (dst, mask) in enumerate(((ak[:, k], m.before), (nt[:, k], m.before), (r.qb[:, h], m.upto),
                                                         (qk[:, k], m.upto))):
                            dve.wait_ge(raw, 4 * h + n + 1)
                            dve.tensor_tensor(dst, view(b + n), four(mask), ALU.mult).then_inc(formed, 1)
                for l in range(L):
                    for k in range(2):
                        s = (p * L + l) * 2 + k
                        dve.wait_ge(x_full, s + 1)
                        if s >= 2:
                            dve.wait_ge(x_new, s - 1)
                            dve.wait_ge(xt_new, s - 1)
                        dve.tensor_tensor(x[:, k], x[:, k] if l else four(m.ident), view(4 * k + 1), ALU.add).then_inc(x_new, 1)
                        dve.wait_ge(xt_full, s + 1)
                        dve.tensor_tensor(xt[:, k], xt[:, k] if l else four(m.ident), view(4 * k + 2), ALU.add).then_inc(xt_new, 1)
                for k in range(2):
                    h, o, b = 2 * p + k, k * HD, 4 * k
                    cols = slice(p * P + o, p * P + o + HD)
                    n = n_post * h
                    if not r.decayed:
                        dve.wait_ge(z_full, h + 1)
                        dve.tensor_copy(z[:, k], ps[:, b, 0:TT * HD].rearrange("p (t n) -> p t n", t=TT)).then_inc(z_kept, 1)
                        dve.wait_ge(post_full, n + 1)
                        dve.tensor_copy(r.y_t[o:o + HD, p, :], ps[o:o + HD, b + 3, :]).then_inc(post_kept, 1)
                        n += 1
                    dve.wait_ge(post_full, n + 1)
                    dve.tensor_copy(r.w_t[o:o + HD, p, :], ps[o:o + HD, b + 2, :]).then_inc(post_kept, 1)
                    dve.wait_ge(post_full, n + 2)
                    dve.tensor_copy(r.tz_tok[:, :, cols], ps[:, b + 1, 0:TT * HD].rearrange("p (t n) -> p t n", t=TT)).then_inc(post_kept, 1)


def scan_phase(m, r):
    nc = m.nc
    H, pairs = r.heads, r.heads // 2
    with Phase(m, "scan") as ph:
        ps = ph.banks()
        u_full, u_new, s_full, s_dec, s_new = (ph.sem(s) for s in ("u_full", "u_new", "s_full", "s_dec", "s_new"))
        held = ph.sb("held", [P, pairs, HD])
        block = ph.enter_context(nc.Block())

        @block.tensor
        def _(pe):
            for c in range(NCH):
                t, o = c // 2, (c % 2) * CH
                b = 4 * (c % 2)
                if c:
                    pe.wait_ge(s_new, c + 1)
                    for k in range(2):
                        for p in range(pairs):
                            rows = slice(k * HD, (k + 1) * HD)
                            last = pe.matmul(ps[o:o + CH, b + k, p * HD:(p + 1) * HD], r.w_t[rows, p, c * CH:(c + 1) * CH],
                                             r.states[rows, c, p, :], start=True, stop=True)
                    last.then_inc(u_full, 1)
                if c == NCH - 1:
                    break
                if not r.decayed:
                    for k in range(2):
                        for p in range(pairs):
                            cols = slice(p * P + k * HD, p * P + (k + 1) * HD)
                            pe.matmul(ps[k * HD:(k + 1) * HD, b + 2, p * HD:(p + 1) * HD], r.kd_tok[o:o + CH, t, cols],
                                      r.v_tok[o:o + CH, t, cols], start=p == 0, stop=False, skip_group_check=True)
                pe.wait_ge(u_new, c + 1)
                for k in range(2):
                    for p in range(pairs):
                        cols = slice(p * P + k * HD, p * P + (k + 1) * HD)
                        last = pe.matmul(ps[k * HD:(k + 1) * HD, b + 2, p * HD:(p + 1) * HD], r.bd_tok[o:o + CH, t, cols],
                                         r.u_tok[o:o + CH, t, cols], start=r.decayed and p == 0, stop=p == pairs - 1,
                                         skip_group_check=True)
                last.then_inc(s_full, 1)

        @block.vector
        def _(dve):
            dve.memset(r.states[:, 0], 0.0).then_inc(s_new, 1)
            for c in range(NCH):
                t, o = c // 2, (c % 2) * CH
                b = 4 * (c % 2)
                pair_view = lambda ap: ap.rearrange("p (a k d) -> p k a d", k=2, d=HD)
                if c:
                    dve.wait_ge(u_full, c)
                    dve.tensor_tensor(pair_view(r.u_tok[o:o + CH, t, :]),
                                      ps[o:o + CH, b:b + 2, 0:pairs * HD].rearrange("p k (a d) -> p k a d", d=HD),
                                      pair_view(r.tz_tok[o:o + CH, t, :]), ALU.add).then_inc(u_new, 1)
                else:
                    dve.tensor_copy(r.u_tok[o:o + CH, t, :], r.tz_tok[o:o + CH, t, :]).then_inc(u_new, 1)
                if c == NCH - 1:
                    break
                dve.wait_ge(s_new, c + 1)
                dve.tensor_tensor(held[:, :, :], r.states[:, c], r.last[:, :, c:c + 1].to_broadcast([P, pairs, HD]),
                                  ALU.mult).then_inc(s_dec, 1)
                dve.wait_ge(s_dec, c + 1)
                dve.wait_ge(s_full, c + 1)
                dve.tensor_tensor(r.states[:, c + 1], held[:, :, :],
                                  ps[:, b + 2, 0:pairs * HD].rearrange("p (a d) -> p a d", d=HD), ALU.add).then_inc(s_new, 1)


def read_phase(m, r):
    nc = m.nc
    pairs = r.heads // 2
    with Phase(m, "read") as ph:
        ps = ph.banks()
        full, kept = ph.sem("full"), ph.sem("kept")
        block = ph.enter_context(nc.Block())

        @block.tensor
        def _(pe):
            for h in range(r.heads):
                p, k = h // 2, h % 2
                rows, cols = slice(k * HD, (k + 1) * HD), slice(p * P + k * HD, p * P + (k + 1) * HD)
                if h >= 8:
                    pe.wait_ge(kept, h - 7)
                for t in range(TT):
                    pe.matmul(ps[rows, h % 8, t * P:(t + 1) * P], r.u_tok[:, t, cols], r.qb[:, h, t, :], start=t == 0, stop=False,
                              skip_group_check=True)
                for c in range(1, NCH):
                    last = pe.matmul(ps[rows, h % 8, c * CH:(c + 1) * CH], r.states[rows, c, p, :],
                                     r.r_t[rows, p, c * CH:(c + 1) * CH], start=False, stop=c == NCH - 1, skip_group_check=True)
                last.then_inc(full, 1)

        @block.vector
        def _(dve):
            for h in range(r.heads):
                p, k = h // 2, h % 2
                rows = slice(k * HD, (k + 1) * HD)
                dve.wait_ge(full, h + 1)
                if r.decayed:
                    dve.tensor_copy(r.y_t[rows, p, :], ps[rows, h % 8, :]).then_inc(kept, 1)
                else:
                    dve.tensor_tensor(r.y_t[rows, p, :], r.y_t[rows, p, :], ps[rows, h % 8, :], ALU.add).then_inc(kept, 1)




def dn_conv_phase(m, l, dn, cv):
    nc = m.nc
    with Phase(m, "dn_conv") as ph:
        sq = ph.sb("sq", [P, 6, T])
        ps = ph.banks()
        conv, silu, squared, summed, root, scaled = (ph.sem(s) for s in ("conv", "silu", "squared", "summed", "root", "scaled"))
        block = ph.enter_context(nc.Block())

        @block.vector
        def _(dve):
            for t in range(9):
                dve.tensor_scalar(cv[:, t, :], dn[:, t, :], col(m, f"dn_conv_{l}_3", t), None, ALU.mult).then_inc(conv, 1)
            for s in range(1, 4):
                for t in range(9):
                    dve.wait_ge(conv, 9 * (s - 1) + t + 1)
                    dve.scalar_tensor_tensor(out=cv[:, t, s:T], in0=dn[:, t, 0:T - s], scalar=col(m, f"dn_conv_{l}_{3 - s}", t),
                                             in1=cv[:, t, s:T], op0=ALU.mult, op1=ALU.add).then_inc(conv, 1)
            dve.wait_ge(root, 2)
            for t in range(6):
                dve.scalar_tensor_tensor(out=cv[:, t, :], in0=cv[:, t, :], scalar=HD ** -0.5 if t < 3 else 1.0, in1=sq[:, t, :],
                                         op0=ALU.mult, op1=ALU.mult).then_inc(scaled, 1)

        @block.scalar
        def _(act):
            for t in range(9):
                act.wait_ge(conv, 27 + t + 1)
                act.activation(cv[:, t, :], cv[:, t, :], ACT.Silu).then_inc(silu, 1)
            for t in range(6):
                act.wait_ge(silu, t + 1)
                act.activation(sq[:, t, :], cv[:, t, :], ACT.Square).then_inc(squared, 1)
            act.wait_ge(summed, 6)
            act.activation(sq[:, :, :], ps[:, 0:6, :], ACT.Ln, bias=m.eps[:, 0:1]).then_inc(root, 1)
            act.wait_ge(root, 1)
            act.activation(sq[:, :, :], sq[:, :, :], ACT.Exp, scale=-0.5).then_inc(root, 1)

        @block.tensor
        def _(pe):
            for t in range(6):
                pe.wait_ge(squared, t + 1)
                pe.matmul(ps[:, t, :], m.pair_ones[:, :], sq[:, t, :], start=True, stop=True).then_inc(summed, 1)


def dn_gates_phase(m, l, ab, small, r):
    nc = m.nc
    R = slice(0, 6)
    with Phase(m, "dn_gates") as ph:
        e = ph.sb("e", [P, T])
        t2 = ph.sb("t2", [P, T])
        g = ph.sb("g", [P, T])
        ea = ph.sb("ea", [P, 1])
        bt = ph.sb("bt", [P, T])
        a_done, v_done, rows_done = ph.sem("a_done"), ph.sem("v_done"), ph.sem("rows_done")
        block = ph.enter_context(nc.Block())

        @block.scalar
        def _(act):
            act.activation(e[R, :], ab[R, 0, :], ACT.Abs, bias=col(m, f"dt_bias_{l}")[R]).then_inc(a_done, 1)
            act.wait_ge(a_done, 1)
            act.activation(e[R, :], e[R, :], ACT.Exp, scale=-1.0).then_inc(a_done, 1)
            act.activation(ea[R, :], col(m, f"a_log_{l}")[R], ACT.Exp).then_inc(a_done, 1)
            act.wait_ge(a_done, 3)
            act.activation(e[R, :], e[R, :], ACT.Ln, bias=m.ones[R, 0:1]).then_inc(a_done, 1)
            act.activation(bt[R, :], ab[R, 1, :], ACT.Tanh, scale=0.5).then_inc(a_done, 1)
            act.wait_ge(v_done, 4)
            act.activation(small[R, 1, :], g[R, :], ACT.Exp).then_inc(a_done, 1)
            act.wait_ge(v_done, 5)
            act.activation(small[R, 2, :], t2[R, :], ACT.Exp).then_inc(a_done, 1)

        @block.vector
        def _(dve):
            dve.tensor_scalar(t2[R, :], ab[R, 0, :], col(m, f"dt_bias_{l}")[R], 0.0, ALU.add, ALU.max).then_inc(v_done, 1)
            dve.wait_ge(v_done, 1)
            dve.wait_ge(a_done, 4)
            dve.tensor_tensor(t2[R, :], t2[R, :], e[R, :], ALU.add).then_inc(v_done, 1)
            dve.wait_ge(v_done, 2)
            dve.tensor_scalar(t2[R, :], t2[R, :], ea[R, :], -1.0, ALU.mult, ALU.mult).then_inc(v_done, 1)
            dve.wait_ge(v_done, 3)
            dve.tensor_tensor_scan(g[R, :], m.reset[R, :], t2[R, :], 0.0, ALU.mult, ALU.add).then_inc(v_done, 1)
            dve.wait_ge(v_done, 4)
            chunks = g[R, :].rearrange("p (c t) -> p c t", t=CH)
            dve.tensor_tensor(t2[R, :].rearrange("p (c t) -> p c t", t=CH), chunks[:, :, CH - 1:CH].to_broadcast([6, NCH, CH]),
                              chunks, ALU.subtract).then_inc(v_done, 1)
            dve.wait_ge(a_done, 5)
            dve.tensor_scalar(small[R, 0, :], bt[R, :], 0.5, 0.5, ALU.mult, ALU.add).then_inc(v_done, 1)
            dve.memset(r.lhs_rows[0:HD, :], 0.0).then_inc(rows_done, 1)
            dve.memset(r.rhs_rows[0:HD, :], 0.0).then_inc(rows_done, 1)
            dve.wait_ge(rows_done, 2)
            dve.memset(r.lhs_rows[R, :], 1.0).then_inc(rows_done, 1)
            dve.tensor_scalar(r.lhs_rows[32:38, :], g[R, :], -1.0, None, ALU.mult).then_inc(rows_done, 1)
            dve.tensor_copy(r.rhs_rows[R, :], g[R, :]).then_inc(rows_done, 1)
            dve.memset(r.rhs_rows[32:38, :], 1.0).then_inc(rows_done, 1)
            dve.tensor_copy(r.row_of_head[0:32, :], m.ident[0:32, 0:6]).then_inc(rows_done, 1)
            dve.tensor_copy(r.row_of_head[32:64, :], m.ident[32:64, 32:38]).then_inc(rows_done, 1)


def dn_expand_phase(m, cv, small, az, zb, kd, kb, qd, r):
    nc = m.nc
    with Phase(m, "dn_expand") as ph:
        ps = ph.banks()
        spread, made, turned, kept = (ph.sem(s) for s in ("spread", "made", "turned", "kept"))
        block = ph.enter_context(nc.Block())

        @block.tensor
        def _(pe):
            for p in range(3):
                if p == 2:
                    pe.wait_ge(made, 6)
                for q in range(3):
                    pe.matmul(ps[:, 3 * (p % 2) + q, :], m.head_rows[0:6, p * P:(p + 1) * P], small[0:6, q, :],
                              start=True, stop=True).then_inc(spread, 1)
            for n in range(9):
                p, src = n // 3, (az, zb, kd)[n % 3]
                pe.wait_ge(made, 6 * (p + 1))
                if n >= 2:
                    pe.wait_ge(kept, n - 1)
                for t in range(TT):
                    last = pe.transpose(ps[:, 6 + n % 2, t * P:(t + 1) * P], src[:, p, t * P:(t + 1) * P], m.ident[:, :])
                last.then_inc(turned, 1)

        @block.vector
        def _(dve):
            for p in range(3):
                b = 3 * (p % 2)
                dve.wait_ge(spread, 3 * p + 1)
                dve.scalar_tensor_tensor(out=kb[:, p, :], in0=cv[:, 3 + p, :], scalar=-1.0, in1=ps[:, b, :], op0=ALU.mult,
                                         op1=ALU.mult).then_inc(made, 1)
                dve.tensor_tensor(zb[:, p, :], cv[:, 6 + p, :], ps[:, b, :], ALU.mult).then_inc(made, 1)
                dve.wait_ge(spread, 3 * p + 2)
                dve.wait_ge(made, 6 * p + 2)
                dve.tensor_tensor(az[:, p, :], kb[:, p, :], ps[:, b + 1, :], ALU.mult).then_inc(made, 1)
                dve.tensor_tensor(qd[:, p, :], cv[:, p, :], ps[:, b + 1, :], ALU.mult).then_inc(made, 1)
                dve.tensor_copy(r.last[:, p, :], ps[:, b + 1, CH - 1:T:CH]).then_inc(made, 1)
                dve.wait_ge(spread, 3 * p + 3)
                dve.tensor_tensor(kd[:, p, :], cv[:, 3 + p, :], ps[:, b + 2, :], ALU.mult).then_inc(made, 1)

        @block.scalar
        def _(act):
            for n in range(9):
                p, dst = n // 3, (r.a_tok, r.z_tok, r.bd_tok)[n % 3]
                act.wait_ge(turned, n + 1)
                act.activation(dst[:, :, p * P:(p + 1) * P], ps[:, 6 + n % 2, :].rearrange("p (t n) -> p t n", t=TT),
                               ACT.Copy).then_inc(kept, 1)


def head_norm_phase(m, jobs):
    nc = m.nc
    n = sum(tiles for _, tiles, _, _, _ in jobs)
    assert n <= 8
    with Phase(m, "head_norm") as ph:
        sq = ph.sb("sq", [P, n, T])
        ps = ph.banks()
        squared, summed, root, scaled = (ph.sem(s) for s in ("squared", "summed", "root", "scaled"))
        block = ph.enter_context(nc.Block())
        tiles = [(x[:, t, :], out[:, t, :], c, f) for x, k, out, c, f in jobs for t in range(k)]

        @block.scalar
        def _(act):
            for i, (x, _, _, _) in enumerate(tiles):
                act.activation(sq[:, i, :], x, ACT.Square).then_inc(squared, 1)
            act.wait_ge(summed, n)
            act.activation(sq[:, :, :], ps[:, 0:n, :], ACT.Ln, bias=m.eps[:, 0:1], scale=1.0 / HD).then_inc(root, 1)
            act.wait_ge(root, 1)
            act.activation(sq[:, :, :], sq[:, :, :], ACT.Exp, scale=-0.5).then_inc(root, 1)

        @block.tensor
        def _(pe):
            for i in range(n):
                pe.wait_ge(squared, i + 1)
                pe.matmul(ps[:, i, :], m.pair_ones[:, :], sq[:, i, :], start=True, stop=True).then_inc(summed, 1)

        @block.vector
        def _(dve):
            dve.wait_ge(root, 2)
            for i, (x, out, c, f) in enumerate(tiles):
                if f != 1.0:
                    dve.tensor_scalar(sq[:, i, :], sq[:, i, :], f, None, ALU.mult).then_inc(scaled, 1)
                else:
                    dve.nop().then_inc(scaled, 1)
                dve.wait_ge(scaled, 2 * i + 1)
                dve.scalar_tensor_tensor(out=out, in0=x, scalar=col(m, c), in1=sq[:, i, :], op0=ALU.mult,
                                         op1=ALU.mult).then_inc(scaled, 1)


def gate_split_phase(m, y, z, func, tiles, hi, lo):
    nc = m.nc
    with Phase(m, "gate") as ph:
        gated, times, rounded, rest = (ph.sem(s) for s in ("gated", "times", "rounded", "rest"))
        block = ph.enter_context(nc.Block())

        @block.scalar
        def _(act):
            if z is not None:
                for t in range(tiles):
                    act.activation(z[:, t, :], z[:, t, :], func).then_inc(gated, 1)
            for t in range(tiles):
                if z is not None:
                    act.wait_ge(times, t + 1)
                act.activation(hi[:, t, :], y[:, t, :], ACT.Copy).then_inc(rounded, 1)

        @block.vector
        def _(dve):
            if z is not None:
                for t in range(tiles):
                    dve.wait_ge(gated, t + 1)
                    dve.tensor_tensor(y[:, t, :], y[:, t, :], z[:, t, :], ALU.mult).then_inc(times, 1)
            for t in range(tiles):
                dve.wait_ge(rounded, t + 1)
                dve.tensor_tensor(lo[:, t, :], y[:, t, :], hi[:, t, :].bitcast(F32), ALU.subtract).then_inc(rest, 1)


def fx_rows_phase(m, l, f, r):
    nc = m.nc
    R = slice(0, 6)
    with Phase(m, "fx_rows") as ph:
        e, t2, c = ph.sb("e", [P, T]), ph.sb("t2", [P, T]), ph.sb("c", [P, T])
        one = ph.sb("one", [P, T])
        a_done, v_done, rows_done = ph.sem("a_done"), ph.sem("v_done"), ph.sem("rows_done")
        block = ph.enter_context(nc.Block())

        @block.scalar
        def _(act):
            act.activation(e[R, :], f[R, 0, :], ACT.Abs, bias=col(m, f"f_bias_{l}")[R]).then_inc(a_done, 1)
            act.wait_ge(a_done, 1)
            act.activation(e[R, :], e[R, :], ACT.Exp, scale=-1.0).then_inc(a_done, 1)
            act.wait_ge(a_done, 2)
            act.activation(e[R, :], e[R, :], ACT.Ln, bias=m.ones[R, 0:1]).then_inc(a_done, 1)

        @block.vector
        def _(dve):
            dve.tensor_scalar(t2[R, :], f[R, 0, :], col(m, f"f_bias_{l}")[R], 0.0, ALU.add, ALU.min).then_inc(v_done, 1)
            dve.memset(one[R, :], 1.0).then_inc(v_done, 1)
            dve.wait_ge(v_done, 2)
            dve.wait_ge(a_done, 3)
            dve.tensor_tensor(t2[R, :], t2[R, :], e[R, :], ALU.subtract).then_inc(v_done, 1)
            dve.wait_ge(v_done, 3)
            dve.tensor_tensor_scan(c[R, :], one[R, :], t2[R, :], 0.0, ALU.mult, ALU.add).then_inc(v_done, 1)
            dve.memset(r.key_rows[:, :], 0.0).then_inc(rows_done, 1)
            dve.memset(r.query_rows[:, :], 0.0).then_inc(rows_done, 1)
            dve.wait_ge(rows_done, 2)
            dve.wait_ge(v_done, 4)
            for o in (0, HD):
                dve.tensor_scalar(r.key_rows[o:o + 6, :], c[R, :], -1.0, None, ALU.mult).then_inc(rows_done, 1)
                dve.memset(r.key_rows[o + 32:o + 38, :], 1.0).then_inc(rows_done, 1)
                dve.memset(r.query_rows[o:o + 6, :], 1.0).then_inc(rows_done, 1)
                dve.tensor_copy(r.query_rows[o + 32:o + 38, :], c[R, :]).then_inc(rows_done, 1)
            for o in range(0, P, 32):
                dve.tensor_copy(r.row_of_head[o:o + 32, :], m.ident[o:o + 32, o:o + 6]).then_inc(rows_done, 1)


def turn_phase(m, src, dst, tiles, n=T, dst_tiles=None):
    nc = m.nc
    nt = n // P
    with Phase(m, "turn") as ph:
        ps = ph.banks()
        turned, kept = ph.sem("turned"), ph.sem("kept")
        block = ph.enter_context(nc.Block())

        @block.tensor
        def _(pe):
            for k in range(tiles):
                if k >= 8:
                    pe.wait_ge(kept, k - 7)
                for t in range(nt):
                    last = pe.transpose(ps[:, k % 8, t * P:(t + 1) * P], src[:, k, t * P:(t + 1) * P], m.ident[:, :])
                last.then_inc(turned, 1)

        @block.vector
        def _(dve):
            for k in range(tiles):
                dve.wait_ge(turned, k + 1)
                dve.tensor_copy(dst[:, :, k * P:(k + 1) * P],
                                ps[:, k % 8, 0:n].rearrange("p (t n) -> p t n", t=nt)).then_inc(kept, 1)


def fx_attention_phase(m, q, k, v_tok, r, o_t):
    nc = m.nc
    H = 6
    with Phase(m, "fx") as ph:
        own = ph.sb("own", [P, 2, T])
        prob = ph.sb("prob", [P, 2, TT, T])
        prob_t = ph.sb("prob_t", [P, 2, TT, T])
        top, total = ph.sb("top", [P, 2, TT]), ph.sb("total", [P, 2, TT])
        ps = ph.banks()
        own_ready, scored, masked, topped, exped, inverse, normed, turned, kept, out_full, out_kept = (
            ph.sem(s) for s in ("own", "scored", "masked", "topped", "exped", "inverse", "normed", "turned", "kept",
                                "out_full", "out_kept"))
        block = ph.enter_context(nc.Block())

        @block.gpsimd
        def _(pool):
            for h in range(H):
                o = (h % 2) * HD
                if h >= 2:
                    pool.wait_ge(scored, TT * (h - 1))
                pool.tensor_scalar(own[o:o + HD, h % 2, :], r.query_rows[o:o + HD, :], r.row_of_head[o:o + HD, h:h + 1], None,
                                   ALU.mult).then_inc(own_ready, 1)

        def scores(pe, h):
            p, o = h // 2, (h % 2) * HD
            rows = slice(o, o + HD)
            pe.wait_ge(own_ready, h + 1)
            for i in range(TT):
                if h:
                    pe.wait_ge(exped, TT * (h - 1) + i + 1)
                n = (i + 1) * P
                pe.matmul(ps[:, i, 0:n], q[rows, p, i * P:(i + 1) * P], k[rows, p, 0:n], start=True, stop=False)
                pe.matmul(ps[:, i, 0:n], own[rows, h % 2, i * P:(i + 1) * P], r.key_rows[rows, 0:n],
                          start=False, stop=True).then_inc(scored, 1)

        @block.tensor
        def _(pe):
            scores(pe, 0)
            for h in range(H):
                p, o = h // 2, (h % 2) * HD
                if h + 1 < H:
                    scores(pe, h + 1)
                for j in range(TT):
                    pe.wait_ge(normed, TT * (h + 1))
                    s = TT * h + j
                    if s >= 2:
                        pe.wait_ge(kept, s - 1)
                    for i in range(j, TT):
                        last = pe.transpose(ps[:, 4 + s % 2, i * P:(i + 1) * P], prob[:, h % 2, i, j * P:(j + 1) * P], m.ident[:, :])
                    last.then_inc(turned, 1)
                if h >= 2:
                    pe.wait_ge(out_kept, h - 1)
                for j in range(TT):
                    pe.wait_ge(kept, TT * h + j + 1)
                    last = pe.matmul(ps[o:o + HD, 6 + h % 2, j * P:T], v_tok[:, j, h * HD:(h + 1) * HD], prob_t[:, h % 2, j, j * P:T],
                                     start=j == 0, stop=j == TT - 1, skip_group_check=True)
                last.then_inc(out_full, 1)

        @block.vector
        def _(dve):
            def after(h):
                for i in range(TT):
                    n = TT * h + i
                    dve.wait_ge(exped, n + 1)
                    dve.reciprocal(total[:, h % 2, i:i + 1], total[:, h % 2, i:i + 1]).then_inc(inverse, 1)
                    dve.wait_ge(inverse, n + 1)
                    w = (i + 1) * P
                    dve.tensor_scalar(prob[:, h % 2, i, 0:w], prob[:, h % 2, i, 0:w], total[:, h % 2, i:i + 1], None,
                                      ALU.mult).then_inc(normed, 1)

            def finish(h):
                o = (h % 2) * HD
                dve.wait_ge(out_full, h + 1)
                dve.tensor_copy(o_t[o:o + HD, h // 2, :], ps[o:o + HD, 6 + h % 2, :]).then_inc(out_kept, 1)

            for h in range(H):
                for i in range(TT):
                    n = TT * h + i
                    dve.wait_ge(scored, n + 1)
                    last = ps[:, i, i * P:(i + 1) * P]
                    dve.tensor_tensor(last, last, m.causal[:, :], ALU.add).then_inc(masked, 1)
                    dve.wait_ge(masked, n + 1)
                    if n >= 2 * TT:
                        dve.wait_ge(exped, n - 2 * TT + 1)
                    dve.tensor_reduce(top[:, h % 2, i:i + 1], ps[:, i, 0:(i + 1) * P], AX.X, ALU.max, negate=True).then_inc(topped, 1)
                after(h)
                if h:
                    finish(h - 1)
            finish(H - 1)

        @block.scalar
        def _(act):
            for h in range(H):
                for i in range(TT):
                    n = TT * h + i
                    act.wait_ge(topped, n + 1)
                    if h >= 2:
                        act.wait_ge(turned, TT * (h - 1))
                        act.wait_ge(normed, TT * (h - 1))
                    w = (i + 1) * P
                    act.activation(prob[:, h % 2, i, 0:w], ps[:, i, 0:w], ACT.Exp, bias=top[:, h % 2, i:i + 1],
                                   accum_out=total[:, h % 2, i:i + 1]).then_inc(exped, 1)
                for j in range(TT):
                    s = TT * h + j
                    act.wait_ge(turned, s + 1)
                    if h >= 2:
                        act.wait_ge(out_full, h - 1)
                    act.activation(prob_t[:, h % 2, j, j * P:T], ps[:, 4 + s % 2, j * P:T], ACT.Copy).then_inc(kept, 1)


def pool_phase(m, l, xp, o_t):
    nc = m.nc
    with Phase(m, "pool") as ph:
        w = ph.sb("w", [P, 2, HD])
        inv = ph.sb("inv", [P, 2, T])
        s1, s2 = ph.sb("s1", [P, 2, T]), ph.sb("s2", [P, 2, T])
        ps = ph.banks(4)
        landed, inv_done, summed, full, kept = (ph.sem(s) for s in ("landed", "inv_done", "summed", "full", "kept"))
        block = ph.enter_context(nc.Block())
        groups = [(g // 2, (g % 2) * HD, 2 << g) for g in range(4)]

        @block.sync
        def _(sp):
            sp.dma_start(w[:, :, :], m.ins["pool_w"][l].rearrange("(j k) c d -> (k c) j d", k=2)).then_inc(landed, 16)

        @block.gpsimd
        def _(pool):
            n = 0
            for j, o, win in groups:
                pool.memset(inv[o:o + HD, j, :], 1.0 / win).then_inc(inv_done, 1)
                n += 1
                pool.wait_ge(inv_done, n)
                for t in range(win - 1):
                    pool.memset(inv[o:o + HD, j, t:t + 1], 1.0 / (t + 1)).then_inc(inv_done, 1)
                    n += 1

        n_inv = sum(win for _, _, win in groups)

        @block.vector
        def _(dve):
            n = 0

            def step(ins):
                nonlocal n
                n += 1
                ins.then_inc(summed, 1)
                dve.wait_ge(summed, n)

            for g, (j, o, win) in enumerate(groups):
                rows = slice(o, o + HD)
                src = xp
                a, b = s1, s2
                for k in range(g + 1):
                    d = 1 << k
                    step(dve.tensor_copy(a[rows, j, 0:d], src[rows, j, 0:d]))
                    step(dve.tensor_tensor(a[rows, j, d:T], src[rows, j, d:T], src[rows, j, 0:T - d], ALU.add))
                    src = a
                    a, b = b, a
                if g == 0:
                    dve.wait_ge(inv_done, n_inv)
                step(dve.tensor_tensor(a[rows, j, :], src[rows, j, :], inv[rows, j, :], ALU.mult))
                step(dve.tensor_tensor(xp[rows, j, :], a[rows, j, :], xp[rows, j, :], ALU.subtract))
            for j in range(2):
                for k in range(2):
                    dve.wait_ge(full, 2 * j + k + 1)
                    rows = slice(k * HD, (k + 1) * HD)
                    dve.tensor_scalar(o_t[rows, j, :], ps[rows, 2 * j + k, :], col(m, f"pool_scale_{l}", j)[rows], None,
                                      ALU.mult).then_inc(kept, 1)

        steps = sum(2 * (g + 1) + 2 for g in range(4))

        @block.tensor
        def _(pe):
            pe.wait_ge(landed, 16)
            pe.wait_ge(summed, steps)
            for j, o, _ in groups:
                pe.matmul(ps[o:o + HD, 2 * j + o // HD, :], w[o:o + HD, j, :], xp[o:o + HD, j, :], start=True, stop=True).then_inc(full, 1)


def plain_job(m, w, first, groups, nf, dst, hi=None, lo=None, **more):
    def load(g, c):
        return [(0, nf * P, k_major(w)[:, :, bass.ds(g * (nf * P) + first, nf * P)])]

    def dve(eng, g, b, n):
        size = more.get("n", T)
        return eng.tensor_copy(dst[:, bass.ds(g * nf, nf), :], more["ps"][:, b:b + nf, 0:size])

    return Job(groups, nf, load, hi if hi is not None else m.act_hi, lo if lo is not None else m.act_lo, dve, n=more.get("n", T))


def add_job(m, w, ps, nf=2):
    def load(g, c):
        return [(0, nf * P, k_major(w)[:, :, bass.ds(g * (nf * P), nf * P)])]

    def dve(eng, g, b, n):
        dst = m.xT[:, bass.ds(g * nf, nf), :]
        return eng.tensor_tensor(dst, dst, ps[:, b:b + nf, :], ALU.add)

    return Job(DT // nf, nf, load, m.act_hi, m.act_lo, dve)


def mixer(m, l):
    w = m.ins["w_in"][l]
    norm_phase(m, m.xT, f"norm1_{l}", m.act_hi, m.act_lo)
    with Phase(m, "mix") as mix:
        dn = mix.sb("dn", [P, 12, T])
        fxp = mix.sb("fxp", [P, 9, T])
        xp = mix.sb("xp", [P, 2, T])
        abf = mix.sb("abf", [P, 3, T])

        def jobs(ph, ps):
            q, z = plain_job(m, w, 0, 4, 3, dn, ps=ps), plain_job(m, w, 1548, 3, 3, fxp, ps=ps)

            def load_ab(g, c):
                return [(0, P, k_major(w)[:, :, 1536:1536 + P]), (P, P, k_major(w)[:, :, 1542:1542 + P]),
                        (2 * P, P, k_major(w)[:, :, 2700:2700 + P])]

            def dve_ab(eng, g, b, n):
                return eng.tensor_copy(abf[:, :, :], ps[:, b:b + 3, :])

            ab = Job(1, 3, load_ab, m.act_hi, m.act_lo, dve_ab, loads=3)
            return [q, z, ab, plain_job(m, w, 2706, 1, 2, xp, ps=ps)]

        dense_phase(m, jobs, "proj")
        with Phase(m, "dn") as s:
            r = Rule()
            r.heads, r.decayed = 6, True
            r.qb = s.sb("qb", [P, 6, TT, P])
            r.a_tok, r.z_tok, r.bd_tok = (s.sb(n, [P, TT, 3 * P]) for n in ("a_tok", "z_tok", "bd_tok"))
            r.tz_tok, r.u_tok = r.z_tok, r.a_tok
            r.last = s.sb("last", [P, 3, NCH])
            r.states = s.sb("states", [P, NCH, 3, HD])
            y = dn[:, 3:6]
            with Phase(m, "dn2") as s2:
                cv = s2.sb("cv", [P, 9, T])
                kb = s2.sb("kb", [P, 3, T])
                qd = cv[:, 6:9]
                r.lhs_rows, r.rhs_rows = s2.sb("lhs_rows", [P, T]), s2.sb("rhs_rows", [P, T])
                r.row_of_head = s2.sb("row_of_head", [P, 6])
                dn_conv_phase(m, l, dn, cv)
                with Phase(m, "dn3") as s3:
                    small = s3.sb("small", [P, 3, T])
                    dn_gates_phase(m, l, abf, small, r)
                    dn_expand_phase(m, cv, small, dn[:, 0:3], dn[:, 3:6], dn[:, 6:9], kb, qd, r)
                r.k_t, r.a_t, r.q_t = cv[:, 3:6], kb, cv[:, 0:3]
                r.w_t, r.r_t, r.y_t = dn[:, 0:3], qd, y
                chunk_phase(m, r)
                scan_phase(m, r)
                read_phase(m, r)
            head_norm_phase(m, [(y, 3, y, f"dn_onorm_{l}", 1.0)])
            gate_split_phase(m, y, dn[:, 9:12], ACT.Silu, 3, m.act_hi[:, 0:3], m.act_lo[:, 0:3])
        with Phase(m, "fxs") as s:
            r = Rule()
            r.key_rows, r.query_rows = s.sb("key_rows", [P, T]), s.sb("query_rows", [P, T])
            r.row_of_head = s.sb("row_of_head", [P, 6])
            v_tok = s.sb("v_tok", [P, TT, 3 * P])
            o = s.sb("o", [P, 5, T])
            turn_phase(m, fxp[:, 6:9], v_tok, 3)
            head_norm_phase(m, [(fxp[:, 0:3], 3, fxp[:, 0:3], f"fx_qnorm_{l}", HD ** -0.5),
                                (fxp[:, 3:6], 3, fxp[:, 3:6], f"fx_knorm_{l}", 1.0)])
            fx_rows_phase(m, l, abf[:, 2:3], r)
            fx_attention_phase(m, fxp[:, 0:3], fxp[:, 3:6], v_tok, r, o)
            pool_phase(m, l, xp, o[:, 3:5])
            gate_split_phase(m, o, None, None, 5, m.act_hi[:, 3:8], m.act_lo[:, 3:8])
    dense_phase(m, lambda ph, ps: [add_job(m, m.ins["w_out"][l], ps)], "w_out")



EXPERTS = 8


def router_phase(m, prob, chosen):
    nc = m.nc
    E = EXPERTS
    with Phase(m, "router") as ph:
        w = ph.sb("w", [P, DT, E])
        w_hi, w_lo = ph.sb("w_hi", [P, DT, E], F32R), ph.sb("w_lo", [P, DT, E], F32R)
        logits = ph.sb("logits", [P, TT, E])
        top = ph.sb("top", [P, TT])
        above, ties, lower = (ph.sb(n, [P, TT, E, E]) for n in ("above", "ties", "lower"))
        ps = ph.banks()
        landed, lower_done, parts, full, centred, exped, v_done = (
            ph.sem(s) for s in ("landed", "lower_done", "parts", "full", "centred", "exped", "v_done"))
        block = ph.enter_context(nc.Block())

        @block.sync
        def _(sp):
            sp.dma_start(w[:, :, :], k_major(m.ins["router"][0])).then_inc(landed, 16)

        @block.gpsimd
        def _(pool):
            pool.memset(lower[:, :, :, :], 1.0).then_inc(lower_done, 1)
            pool.wait_ge(lower_done, 1)
            pool.affine_select(out=lower[:, :, :, :], in_=lower[:, :, :, :], compare_op=ALU.is_ge, fill=0.0, base=-1,
                               pattern=[[0, TT], [1, E], [-1, E]], channel_multiplier=0).then_inc(lower_done, 1)

        @block.scalar
        def _(act):
            act.wait_ge(landed, 16)
            act.activation(w_hi[:, :, :], w[:, :, :], ACT.Copy).then_inc(parts, 1)
            act.wait_ge(centred, 1)
            act.activation(prob[:, :, :], prob[:, :, :], ACT.Exp).then_inc(exped, 1)

        @block.tensor
        def _(pe):
            pe.wait_ge(parts, 2)
            for t in range(TT):
                cols = slice(t * P, (t + 1) * P)
                out = ps[:, t, 0:E]
                for k in range(DT):
                    pe.matmul(out, m.act_lo[:, k, cols], w_hi[:, k, :], start=k == 0, stop=False)
                    pe.matmul(out, m.act_hi[:, k, cols], w_lo[:, k, :], start=False, stop=False)
                    last = pe.matmul(out, m.act_hi[:, k, cols], w_hi[:, k, :], start=False, stop=k == DT - 1)
            last.then_inc(full, 1)

        @block.vector
        def _(dve):
            n = 0

            def step(ins):
                nonlocal n
                n += 1
                ins.then_inc(v_done, 1)
                dve.wait_ge(v_done, n)

            dve.wait_ge(parts, 1)
            dve.tensor_tensor(w_lo[:, :, :], w[:, :, :], w_hi[:, :, :].bitcast(F32), ALU.subtract).then_inc(parts, 1)
            dve.wait_ge(full, 1)
            step(dve.tensor_copy(logits[:, :, :], ps[:, 0:TT, 0:E]))
            step(dve.tensor_reduce(top[:, :], logits[:, :, :], AX.X, ALU.max))
            dve.tensor_tensor(prob[:, :, :], logits[:, :, :], top[:, :].unsqueeze(2).to_broadcast([P, TT, E]),
                              ALU.subtract).then_inc(centred, 1)
            for t in range(TT):
                own = logits[:, t, :].unsqueeze(2).to_broadcast([P, E, E])
                other = logits[:, t, :].unsqueeze(1).to_broadcast([P, E, E])
                step(dve.tensor_tensor(above[:, t], other, own, ALU.is_gt))
                step(dve.tensor_tensor(ties[:, t], other, own, ALU.is_equal))
            dve.wait_ge(lower_done, 2)
            step(dve.tensor_tensor(ties[:, :, :, :], ties[:, :, :, :], lower[:, :, :, :], ALU.mult))
            step(dve.tensor_tensor(above[:, :, :, :], above[:, :, :, :], ties[:, :, :, :], ALU.add))
            step(dve.tensor_reduce(chosen[:, :, :], above[:, :, :, :], AX.X, ALU.add))
            step(dve.tensor_scalar(chosen[:, :, :], chosen[:, :, :], 2.0, None, ALU.is_lt))
            dve.wait_ge(exped, 1)
            step(dve.tensor_tensor(prob[:, :, :], prob[:, :, :], chosen[:, :, :], ALU.mult))
            step(dve.tensor_reduce(top[:, :], prob[:, :, :], AX.X, ALU.add))
            step(dve.reciprocal(top[:, :], top[:, :]))
            step(dve.tensor_tensor(prob[:, :, :], prob[:, :, :], top[:, :].unsqueeze(2).to_broadcast([P, TT, E]), ALU.mult))


ITEMS = (2 * T + EXPERTS * (P - 1)) // P
ITEM_COLS = 16


def items_phase(m, prob, chosen, place, weight, table, slots):
    nc = m.nc
    E, N = EXPERTS, ITEM_COLS
    assert ITEMS <= N
    with Phase(m, "items") as ph:
        ints = ph.sb("ints", [P, P], mybir.dt.int32)
        rows_i, first_i = ph.sb("rows_i", [P, N], mybir.dt.int32), ph.sb("first_i", [P, 1], mybir.dt.int32)
        item, expert = ph.sb("item", [P, N]), ph.sb("expert", [P, 1])
        chosen_t, prob_t, run, one = (ph.sb(n, [P, T]) for n in ("chosen_t", "prob_t", "run", "one"))
        tiles, more, begin, end = (ph.sb(n, [P, 1]) for n in ("tiles", "more", "begin", "end"))
        mine, before, shift = (ph.sb(n, [P, N]) for n in ("mine", "before", "shift"))
        ps = ph.banks()
        counted, turned, v_done, ended, made = (ph.sem(s) for s in ("counted", "turned", "v_done", "ended", "made"))
        block = ph.enter_context(nc.Block())

        ENDS = 8 + 2 * (TT - 1) + 1

        @block.gpsimd
        def _(pool):
            pool.iota(ints[:, :], [[1, P]], base=1, channel_multiplier=0).then_inc(counted, 1)
            pool.iota(rows_i[:, :], [[1, N]], base=0, channel_multiplier=0).then_inc(counted, 1)
            pool.iota(first_i[:, :], [[0, 1]], base=0, channel_multiplier=1).then_inc(counted, 1)

        @block.tensor
        def _(pe):
            for b, src in enumerate((chosen, prob)):
                for t in range(TT):
                    last = pe.transpose(ps[0:E, b, t * P:(t + 1) * P], src[:, t, :], m.ident[:, :])
                last.then_inc(turned, 1)
            pe.wait_ge(v_done, ENDS)
            pe.matmul(ps[0:E, 2, 0:1], m.upto[0:E, 0:E], tiles[0:E, :], start=True, stop=True).then_inc(ended, 1)
            pe.wait_ge(v_done, ENDS + 7)
            for t in range(TT):
                cols = slice(t * P, (t + 1) * P)
                pe.matmul(ps[:, 3, t * N:(t + 1) * N], run[0:E, cols], mine[0:E, :], start=True, stop=False)
                pe.matmul(ps[:, 3, t * N:(t + 1) * N], m.ones[0:E, :], shift[0:E, :], start=False, stop=True)
            for t in range(TT):
                last = pe.matmul(ps[:, 4, t * N:(t + 1) * N], prob_t[0:E, t * P:(t + 1) * P], mine[0:E, :], start=True, stop=True)
            last.then_inc(made, 1)
            pe.matmul(ps[0:1, 5, 0:N], expert[0:E, :], mine[0:E, :], start=True, stop=True)
            pe.matmul(ps[0:1, 6, 0:1], m.ones[0:E, 0:1], tiles[0:E, :], start=True, stop=True).then_inc(made, 1)

        @block.vector
        def _(dve):
            n = 0

            def step(ins):
                nonlocal n
                n += 1
                ins.then_inc(v_done, 1)
                dve.wait_ge(v_done, n)

            dve.wait_ge(counted, 3)
            step(dve.tensor_copy(slots[:, :], ints[:, :]))
            step(dve.tensor_copy(item[:, :], rows_i[:, :]))
            step(dve.tensor_copy(expert[:, :], first_i[:, :]))
            step(dve.memset(one[0:E, :], 1.0))
            dve.wait_ge(turned, 2)
            step(dve.tensor_copy(chosen_t[0:E, :], ps[0:E, 0, :]))
            step(dve.tensor_copy(prob_t[0:E, :], ps[0:E, 1, :]))
            step(dve.tensor_tensor_scan(run[0:E, :], one[0:E, :], chosen_t[0:E, :], 0.0, ALU.mult, ALU.add))
            step(dve.tensor_scalar(tiles[0:E, :], run[0:E, T - 1:T], 0.0, None, ALU.is_gt))
            for q in range(1, TT):
                step(dve.tensor_scalar(more[0:E, :], run[0:E, T - 1:T], float(q * P), None, ALU.is_gt))
                step(dve.tensor_tensor(tiles[0:E, :], tiles[0:E, :], more[0:E, :], ALU.add))
            step(dve.tensor_tensor(run[0:E, :], run[0:E, :], chosen_t[0:E, :], ALU.mult))
            assert n == ENDS
            dve.wait_ge(ended, 1)
            step(dve.tensor_copy(end[0:E, :], ps[0:E, 2, 0:1]))
            step(dve.tensor_tensor(begin[0:E, :], end[0:E, :], tiles[0:E, :], ALU.subtract))
            step(dve.tensor_scalar(mine[0:E, :], item[0:E, :], end[0:E, :], None, ALU.is_lt))
            step(dve.tensor_scalar(before[0:E, :], item[0:E, :], begin[0:E, :], None, ALU.is_ge))
            step(dve.tensor_tensor(mine[0:E, :], mine[0:E, :], before[0:E, :], ALU.mult))
            step(dve.tensor_scalar(shift[0:E, :], item[0:E, :], begin[0:E, :], -float(P), ALU.subtract, ALU.mult))
            step(dve.tensor_tensor(shift[0:E, :], shift[0:E, :], mine[0:E, :], ALU.mult))
            dve.wait_ge(made, 1)
            step(dve.tensor_copy(place[:, :, :], ps[:, 3, 0:TT * N].rearrange("p (t n) -> p t n", t=TT)))
            step(dve.tensor_copy(weight[:, :, :], ps[:, 4, 0:TT * N].rearrange("p (t n) -> p t n", t=TT)))
            dve.wait_ge(made, 2)
            step(dve.tensor_copy(table[0:1, 0:N], ps[0:1, 5, 0:N]))
            step(dve.tensor_copy(table[0:1, N:N + 1], ps[0:1, 6, 0:1]))


def experts_phase(m, x_tok, place, weight, table, slots):
    nc = m.nc
    A, B = 6, 4
    U = A + B
    SLOT_A, SLOT_B = DT * BANK, 6 * BANK
    halves = lambda v: SLOT_A // 2 if v < A else SLOT_B // 2
    i_ = m.ins
    gate, up = (i_[n].rearrange("o e (k p) f -> p (o e) k f", p=P) for n in ("moe_gate", "moe_up"))
    down = i_["moe_down"].rearrange("o e (c k p) d -> p (o e) c k d", p=P, k=6)
    down_units = [(0, 0), (1, 0), (0, 1), (1, 1)]
    with Phase(m, "experts") as ph:
        raw = [ph.sb(f"raw{s}", [P, SLOT_A]) for s in range(2)]
        w_hi = [ph.sb(f"w_hi{s}", [P, SLOT_A], F32R) for s in range(2)]
        w_lo = [ph.sb(f"w_lo{s}", [P, SLOT_A], F32R) for s in range(2)]
        pick, pick_w = ph.sb("pick", [P, TT, P]), ph.sb("pick_w", [P, TT, P])
        back = ph.sb("back", [P, T])
        xg_hi, xg_lo = ph.sb("xg_hi", [P, DT, P], F32R), ph.sb("xg_lo", [P, DT, P], F32R)
        silu, h = ph.sb("silu", [P, 2 * P]), [ph.sb(f"h{k}", [P, 2 * P]) for k in range(2)]
        ht_hi, ht_lo = ph.sb("ht_hi", [P, 2 * A, P], F32R), ph.sb("ht_lo", [P, 2 * A, P], F32R)
        y = ph.sb("y", [P, 2, BANK])
        ps = ph.banks()
        landed = [ph.sem("landed0"), ph.sem("landed1")]
        (rounded, split, used, picked, gathered, xg_rounded, xg_done, back_full, back_kept, silu_done, h_done, h_turned,
         ht_rounded, ht_done, y_kept, added_full, added) = (
            ph.sem(s) for s in ("rounded", "split", "used", "picked", "gathered", "xg_rounded", "xg_done", "back_full",
                                "back_kept", "silu_done", "h_done", "h_turned", "ht_rounded", "ht_done", "y_kept",
                                "added_full", "added"))
        block = ph.enter_context(nc.Block())

        def items(eng):
            return eng.value_load(table[0:1, ITEM_COLS:ITEM_COLS + 1], min_val=1, max_val=ITEMS)

        @block.sync
        def _(sp):
            with sp.Fori(0, items(sp)) as i:
                e = sp.value_load(table[0:1, bass.ds(i, 1)], min_val=0, max_val=EXPERTS - 1)
                for v in range(U):
                    sp.wait_ge(split, i * (2 * U) + (2 * v + 2))
                    slot = v % 2
                    if v < A:
                        dst = raw[slot][:, :].rearrange("p (o k w n) -> p o k w n", o=1, k=DT, w=2)
                        for w, src in enumerate((gate, up)):
                            sp.dma_start(dst[:, :, :, w, :], src[:, bass.ds(e, 1), :, v * 2 * P:(v + 1) * 2 * P]).then_inc(landed[slot], 16)
                    else:
                        half, part = down_units[v - A]
                        dst = raw[slot][:, 0:SLOT_B].rearrange("p (o k n) -> p o k n", o=1, k=6)
                        sp.dma_start(dst, down[:, bass.ds(e, 1), part, :, half * BANK:(half + 1) * BANK]).then_inc(landed[slot], 16)

        LANDED = 16 * (A + B // 2)

        def landed_by(i, v):
            return i * LANDED + 16 * sum(2 if u < A else 1 for u in range(v % 2, v + 1, 2))

        @block.scalar
        def _(act):
            with act.Fori(0, items(act)) as i:
                def round_unit(v):
                    n = halves(v)
                    act.wait_ge(landed[v % 2], landed_by(i, v))
                    act.wait_ge(used, i * U + (v + 1))
                    for q in range(2):
                        s = slice(q * n, (q + 1) * n)
                        act.activation(w_hi[v % 2][:, s], raw[v % 2][:, s], ACT.Copy).then_inc(rounded, 1)

                def turned_part(v):
                    act.wait_ge(h_turned, i * A + (v + 1) + 2)
                    act.activation(ht_hi[:, 2 * v:2 * v + 2, :], ps[:, 2 + v % 2, 0:2 * P].rearrange("p (a n) -> p a n", a=2),
                                   ACT.Copy).then_inc(ht_rounded, 1)

                round_unit(0)
                for b in range(2):
                    act.wait_ge(gathered, i * 2 + (b + 1))
                    act.activation(xg_hi[:, 4 * b:4 * b + 4, :], ps[:, 4 + b, :].rearrange("p (a n) -> p a n", a=4),
                                   ACT.Copy).then_inc(xg_rounded, 1)
                act.wait_ge(back_full, i + 2)
                act.activation(back[:, :], ps[:, 3, :], ACT.Copy).then_inc(back_kept, 1)
                for v in range(U):
                    if v + 1 < U:
                        round_unit(v + 1)
                    if v < A:
                        act.wait_ge(used, i * U + (v + 3))
                        act.wait_ge(h_done, i * A + (v + 2))
                        act.activation(silu[:, :], ps[:, v % 2, 0:2 * P], ACT.Silu).then_inc(silu_done, 1)
                    if 1 <= v <= A:
                        turned_part(v - 1)
                    if v >= U - 2:
                        half = v - (U - 2)
                        act.wait_ge(used, i * U + (v + 3))
                        act.activation(y[:, half, :], ps[:, 6 + half, :], ACT.Copy).then_inc(y_kept, 1)

        @block.vector
        def _(dve):
            dve.nop().then_inc(split, 4)
            dve.nop().then_inc(h_done, 2)
            dve.nop().then_inc(ht_done, 2)
            dve.nop().then_inc(added, 8)
            with dve.Fori(0, items(dve)) as i:
                def rest_unit(v):
                    n = halves(v)
                    for q in range(2):
                        s = slice(q * n, (q + 1) * n)
                        dve.wait_ge(rounded, i * (2 * U) + (2 * v + q + 1))
                        dve.tensor_tensor(w_lo[v % 2][:, s], raw[v % 2][:, s], w_hi[v % 2][:, s].bitcast(F32),
                                          ALU.subtract).then_inc(split, 1)

                def turned_part(v):
                    dve.wait_ge(ht_rounded, i * A + (v + 1))
                    dve.tensor_tensor(ht_lo[:, 2 * v:2 * v + 2, :], ps[:, 2 + v % 2, 0:2 * P].rearrange("p (a n) -> p a n", a=2),
                                      ht_hi[:, 2 * v:2 * v + 2, :].bitcast(F32), ALU.subtract).then_inc(ht_done, 1)

                dve.wait_ge(back_full, i + 1)
                for t in range(TT):
                    dve.tensor_scalar(pick[:, t, :], slots[:, :], place[:, t, bass.ds(i, 1)], None, ALU.is_equal).then_inc(picked, 1)
                for t in range(TT):
                    dve.tensor_scalar(pick_w[:, t, :], slots[:, :], place[:, t, bass.ds(i, 1)], weight[:, t, bass.ds(i, 1)],
                                      ALU.is_equal, ALU.mult).then_inc(picked, 1)
                rest_unit(0)
                for b in range(2):
                    dve.wait_ge(xg_rounded, i * 2 + (b + 1))
                    dve.tensor_tensor(xg_lo[:, 4 * b:4 * b + 4, :], ps[:, 4 + b, :].rearrange("p (a n) -> p a n", a=4),
                                      xg_hi[:, 4 * b:4 * b + 4, :].bitcast(F32), ALU.subtract).then_inc(xg_done, 1)
                for v in range(U):
                    if v + 1 < U:
                        rest_unit(v + 1)
                    if v < A:
                        dve.wait_ge(silu_done, i * A + (v + 1))
                        dve.wait_ge(h_turned, i * A + (v + 1))
                        dve.tensor_tensor(h[v % 2][:, :], silu[:, :], ps[:, v % 2, 2 * P:4 * P], ALU.mult).then_inc(h_done, 1)
                    if 1 <= v <= A:
                        turned_part(v - 1)
                for d in range(DT):
                    dve.wait_ge(added_full, i * DT + (d + 1))
                    dve.wait_ge(added, i * DT + (d + 1))
                    dve.tensor_tensor(m.xT[:, d, :], m.xT[:, d, :], ps[:, d % 4, :], ALU.add).then_inc(added, 1)

        @block.tensor
        def _(pe):
            pe.nop().then_inc(used, 2)
            pe.nop().then_inc(h_turned, 2)
            pe.nop().then_inc(back_full, 1)
            with pe.Fori(0, items(pe)) as i:
                def turn(v):
                    pe.wait_ge(h_done, i * A + (v + 3))
                    pe.wait_ge(ht_done, i * A + (v + 1))
                    if v == 1:
                        pe.wait_ge(back_kept, i + 1)
                    for a in range(2):
                        last = pe.transpose(ps[:, 2 + v % 2, a * P:(a + 1) * P], h[v % 2][:, a * P:(a + 1) * P], m.ident[:, :])
                    last.then_inc(h_turned, 1)

                pe.wait_ge(picked, i * (2 * TT) + TT)
                for b in range(2):
                    for d in range(4 * b, 4 * b + 4):
                        for t in range(TT):
                            last = pe.matmul(ps[:, 4 + b, (d % 4) * P:(d % 4 + 1) * P], x_tok[:, t, d * P:(d + 1) * P], pick[:, t, :],
                                             start=t == 0, stop=t == TT - 1)
                    last.then_inc(gathered, 1)
                pe.wait_ge(picked, i * (2 * TT) + 2 * TT)
                pe.wait_ge(added, i * DT + DT)
                for t in range(TT):
                    last = pe.transpose(ps[:, 3, t * P:(t + 1) * P], pick_w[:, t, :], m.ident[:, :])
                last.then_inc(back_full, 1)
                for v in range(U):
                    slot = v % 2
                    kt = DT if v < A else 6
                    if v == 0:
                        pe.wait_ge(xg_done, i * 2 + 2)
                    if v < A:
                        pe.wait_ge(h_done, i * A + (v + 1))
                        out, lhs, first, begin, end = ps[:, v % 2, :], (xg_hi, xg_lo), 0, True, True
                    else:
                        half, part = down_units[v - A]
                        if part == 0:
                            pe.wait_ge(ht_done, i * A + 5)
                        else:
                            pe.wait_ge(ht_done, i * A + A + 2)
                        out, lhs, first, begin, end = ps[:, 6 + half, :], (ht_hi, ht_lo), 6 * part, part == 0, part == 1
                    for k in range(kt):
                        if k % (kt // 2) == 0:
                            pe.wait_ge(split, i * (2 * U) + (2 * v + k // (kt // 2) + 5))
                        cols = slice(k * BANK, (k + 1) * BANK)
                        pe.matmul(out, lhs[1][:, first + k, :], w_hi[slot][:, cols], start=begin and k == 0, stop=False)
                        pe.matmul(out, lhs[0][:, first + k, :], w_lo[slot][:, cols], start=False, stop=False)
                        last = pe.matmul(out, lhs[0][:, first + k, :], w_hi[slot][:, cols], start=False, stop=end and k == kt - 1)
                    last.then_inc(used, 1)
                    if 1 <= v <= A:
                        turn(v - 1)
                for d in range(DT):
                    if d % 4 == 0:
                        pe.wait_ge(y_kept, i * 2 + (d // 4 + 1))
                    pe.wait_ge(added, i * DT + (d + 5))
                    pe.matmul(ps[:, d % 4, :], y[:, d // 4, (d % 4) * P:(d % 4 + 1) * P], back[:, :], start=True, stop=True).then_inc(added_full, 1)


def moe_phase(m):
    with Phase(m, "moe") as s:
        x_tok = s.sb("x_tok", [P, TT, D])
        place, weight = (s.sb(n, [P, TT, ITEM_COLS]) for n in ("place", "weight"))
        table, slots = s.sb("table", [1, ITEM_COLS + 1], mybir.dt.int32), s.sb("slots", [P, P])
        with Phase(m, "moe2") as s2:
            h = s2.sb("h", [P, DT, T])
            prob, chosen = (s2.sb(n, [P, TT, EXPERTS]) for n in ("prob", "chosen"))
            norm_phase(m, m.xT, "norm2_1", m.act_hi, m.act_lo, full=h)
            turn_phase(m, h, x_tok, DT)
            router_phase(m, prob, chosen)
            items_phase(m, prob, chosen, place, weight, table, slots)
        experts_phase(m, x_tok, place, weight, table, slots)




def rg_phase(m, px, py, hi, lo):
    nc = m.nc
    i = m.ins
    N = 4
    with Phase(m, "rg") as ph:
        wa, wx = ph.sb("wa", [P, N, HD]), ph.sb("wx", [P, N, HD])
        xb, ga, gx, mult = (ph.sb(n, [P, N, T]) for n in ("xb", "ga", "gx", "mult"))
        lam, neg = ph.sb("lam", [P, N]), ph.sb("neg", [P, N])
        ps = ph.banks()
        landed, conv, lam_a, lam_v, full, sig, v_done, a_done = (
            ph.sem(s) for s in ("landed", "conv", "lam_a", "lam_v", "full", "sig", "v_done", "a_done"))
        block = ph.enter_context(nc.Block())
        lam_cols = m.params[:, m.columns["lru_lambda"]:m.columns["lru_lambda"] + N]

        @block.sync
        def _(sp):
            for w, src in ((wa, "w_rg_a_2"), (wx, "w_rg_x_2")):
                sp.dma_start(w[:, :, :], i[src][0].rearrange("(j k) c d -> (k c) j d", k=2)).then_inc(landed, 16)

        @block.tensor
        def _(pe):
            pe.wait_ge(landed, 32)
            for w, b in ((wa, 0), (wx, 4)):
                for j in range(N):
                    pe.wait_ge(conv, 3 * N + j + 1)
                    pe.matmul(ps[0:HD, b + j, :], w[0:HD, j, :], xb[0:HD, j, :], start=True, stop=True).then_inc(full, 1)
                    pe.wait_ge(full, 2 * (b + j) + 1)
                    pe.matmul(ps[HD:P, b + j, :], w[HD:P, j, :], xb[HD:P, j, :], start=True, stop=True).then_inc(full, 1)

        @block.scalar
        def _(act):
            act.activation(lam[:, :], lam_cols, ACT.Abs).then_inc(lam_a, 1)
            act.wait_ge(lam_a, 1)
            act.activation(lam[:, :], lam[:, :], ACT.Exp, scale=-1.0).then_inc(lam_a, 1)
            act.wait_ge(lam_a, 2)
            act.activation(lam[:, :], lam[:, :], ACT.Ln, bias=m.ones[:, 0:1]).then_inc(lam_a, 1)
            for j in range(N):
                act.wait_ge(full, 2 * j + 2)
                act.activation(ga[:, j, :], ps[:, j, :], ACT.Sigmoid, bias=col(m, "b_rg_a", j)).then_inc(sig, 1)
            for j in range(N):
                act.wait_ge(full, 2 * (4 + j) + 2)
                act.activation(gx[:, j, :], ps[:, 4 + j, :], ACT.Sigmoid, bias=col(m, "b_rg_x", j)).then_inc(sig, 1)
            act.wait_ge(lam_v, 3)
            act.wait_ge(sig, 2 * N)
            for j in range(N):
                act.activation(mult[:, j, :], ga[:, j, :], ACT.Tanh, scale=neg[:, j:j + 1]).then_inc(a_done, 1)
            act.wait_ge(lam_v, 4)
            act.wait_ge(a_done, N)
            for j in range(N):
                act.activation(ga[:, j, :], ga[:, j, :], ACT.Exp, scale=lam[:, j:j + 1]).then_inc(a_done, 1)
            act.wait_ge(v_done, 3)
            act.activation(mult[:, :, :], mult[:, :, :], ACT.Sqrt).then_inc(a_done, 1)
            act.activation(py[:, :, :], py[:, :, :], ACT.Gelu_apprx_tanh).then_inc(a_done, 1)
            act.wait_ge(v_done, 11)
            act.activation(hi[:, :, :], xb[:, :, :], ACT.Copy).then_inc(a_done, 1)

        @block.vector
        def _(dve):
            for j in range(N):
                dve.tensor_scalar(xb[:, j, :], px[:, j, :], col(m, "conv_b_w_3", j), col(m, "conv_b_b", j), ALU.mult,
                                  ALU.add).then_inc(conv, 1)
            for s in range(1, 4):
                for j in range(N):
                    dve.wait_ge(conv, N * (s - 1) + j + 1)
                    dve.scalar_tensor_tensor(out=xb[:, j, s:T], in0=px[:, j, 0:T - s], scalar=col(m, f"conv_b_w_{3 - s}", j),
                                             in1=xb[:, j, s:T], op0=ALU.mult, op1=ALU.add).then_inc(conv, 1)
            dve.tensor_scalar(neg[:, :], lam_cols, 0.0, None, ALU.min).then_inc(lam_v, 1)
            dve.wait_ge(lam_v, 1)
            dve.wait_ge(lam_a, 3)
            dve.tensor_tensor(neg[:, :], lam[:, :], neg[:, :], ALU.subtract).then_inc(lam_v, 1)
            dve.wait_ge(lam_v, 2)
            dve.tensor_scalar(neg[:, :], neg[:, :], 8.0, None, ALU.mult).then_inc(lam_v, 1)
            dve.wait_ge(lam_v, 3)
            dve.tensor_scalar(lam[:, :], neg[:, :], -1.0, None, ALU.mult).then_inc(lam_v, 1)
            n = 0

            def step(ins):
                nonlocal n
                n += 1
                ins.then_inc(v_done, 1)
                dve.wait_ge(v_done, n)

            dve.wait_ge(a_done, N)
            step(dve.tensor_scalar(px[:, :, :], mult[:, :, :], 1.0, None, ALU.add))
            step(dve.reciprocal(px[:, :, :], px[:, :, :]))
            step(dve.scalar_tensor_tensor(out=mult[:, :, :], in0=mult[:, :, :], scalar=2.0, in1=px[:, :, :], op0=ALU.mult,
                                          op1=ALU.mult))
            dve.wait_ge(conv, 4 * N)
            dve.wait_ge(a_done, 2 * N + 1)
            step(dve.memset(mult[:, :, 0:1], 1.0))
            step(dve.tensor_tensor(xb[:, :, :], xb[:, :, :], gx[:, :, :], ALU.mult))
            step(dve.tensor_tensor(xb[:, :, :], xb[:, :, :], mult[:, :, :], ALU.mult))
            for j in range(N):
                step(dve.tensor_tensor_scan(px[:, j, :], ga[:, j, :], xb[:, j, :], 0.0, ALU.mult, ALU.add))
            dve.wait_ge(a_done, 2 * N + 2)
            step(dve.tensor_tensor(xb[:, :, :], px[:, :, :], py[:, :, :], ALU.mult))
            dve.wait_ge(a_done, 2 * N + 3)
            step(dve.tensor_tensor(lo[:, :, :], xb[:, :, :], hi[:, :, :].bitcast(F32), ALU.subtract))


def rw_shift_phase(m, rw):
    nc = m.nc
    N = 14
    with Phase(m, "rw_shift") as ph:
        d = ph.sb("d", [P, N, T])
        diff, mixed, a_done = ph.sem("diff"), ph.sem("mixed"), ph.sem("a_done")
        block = ph.enter_context(nc.Block())

        @block.vector
        def _(dve):
            dve.tensor_tensor(d[:, :, 1:T], rw[:, :, 0:T - 1], rw[:, :, 1:T], ALU.subtract).then_inc(diff, 1)
            dve.tensor_scalar(d[:, :, 0:1], rw[:, :, 0:1], -1.0, None, ALU.mult).then_inc(diff, 1)
            dve.wait_ge(diff, 2)
            for j in reversed(range(N)):
                dve.scalar_tensor_tensor(out=rw[:, j, :], in0=d[:, j, :], scalar=col(m, "mu_shift", j), in1=rw[:, j, :],
                                         op0=ALU.mult, op1=ALU.add).then_inc(mixed, 1)

        @block.scalar
        def _(act):
            act.wait_ge(mixed, 1)
            act.activation(rw[:, 13, :], rw[:, 13, :], ACT.Sigmoid).then_inc(a_done, 1)
            act.wait_ge(mixed, 2)
            act.activation(rw[0:HD, 12, :], rw[0:HD, 12, :], ACT.Tanh).then_inc(a_done, 1)


def rw_lora_phase(m, rw, ld, a, g):
    nc = m.nc
    i = m.ins
    with Phase(m, "rw_lora") as ph:
        wa, wg = ph.sb("wa", [P, 4 * P]), ph.sb("wg", [P, 4 * P])
        ps = ph.banks()
        landed, full, kept, scaled = (ph.sem(s) for s in ("landed", "full", "kept", "scaled"))
        block = ph.enter_context(nc.Block())

        @block.sync
        def _(sp):
            sp.dma_start(wa[0:HD, :], i["w_lora_up_2"][0]).then_inc(landed, 16)
            sp.dma_start(wa[HD:P, :], i["a_lora_up_2"][0]).then_inc(landed, 16)
            sp.dma_start(wg[:, :], i["g_lora_up_2"][0]).then_inc(landed, 16)

        @block.tensor
        def _(pe):
            pe.wait_ge(landed, 48)
            for n in range(12):
                q, j = n // 4, n % 4
                cols = slice(j * P, (j + 1) * P)
                if q == 2:
                    pe.wait_ge(kept, j + 1)
                lhs, rhs = ((wa[0:HD, cols], rw[0:HD, 12, :]), (wa[HD:P, cols], rw[HD:P, 12, :]), (wg[:, cols], rw[:, 13, :]))[q]
                pe.matmul(ps[:, n % 8, :], lhs, rhs, start=True, stop=True).then_inc(full, 1)

        @block.scalar
        def _(act):
            for n in range(12):
                q, j = n // 4, n % 4
                act.wait_ge(full, n + 1)
                if q == 2:
                    act.activation(g[:, j, :], ps[:, n % 8, :], ACT.Copy).then_inc(kept, 1)
                else:
                    dst, name = ((ld, "w0"), (a, "a0"))[q]
                    act.activation(dst[:, j, :], ps[:, n % 8, :], ACT.Sigmoid, bias=col(m, name, j)).then_inc(kept, 1)

        @block.vector
        def _(dve):
            for j in range(4):
                dve.wait_ge(kept, j + 1)
                dve.tensor_scalar(ld[:, j, :], ld[:, j, :], -math.exp(-0.5), None, ALU.mult).then_inc(scaled, 1)


def rw_keys_phase(m, rw, a, kk, b, bonus_rows):
    nc = m.nc
    N = 4
    r, k = rw[:, 0:4], rw[:, 4:8]
    with Phase(m, "rw_keys") as ph:
        sq = ph.sb("sq", [P, N, T])
        one_less = ph.sb("one_less", [P, N])
        ps = ph.banks()
        v_done, a_done, summed = ph.sem("v_done"), ph.sem("a_done"), ph.sem("summed")
        block = ph.enter_context(nc.Block())
        ka = m.params[:, m.columns["k_a"]:m.columns["k_a"] + N]
        STEPS = N + 1 + 2 * N + 3 + 1 + N

        @block.scalar
        def _(act):
            act.wait_ge(v_done, N)
            act.activation(sq[:, :, :], kk[:, :, :], ACT.Square).then_inc(a_done, 1)
            act.wait_ge(summed, N)
            act.activation(sq[:, :, :], ps[:, 0:N, :], ACT.Sqrt).then_inc(a_done, 1)

        @block.tensor
        def _(pe):
            pe.wait_ge(a_done, 1)
            for j in range(N):
                pe.matmul(ps[:, j, :], m.pair_ones[:, :], sq[:, j, :], start=True, stop=True).then_inc(summed, 1)
            pe.wait_ge(v_done, STEPS)
            for j in range(N):
                pe.matmul(ps[:, N + j, :], m.pair_ones[:, :], sq[:, j, :], start=True, stop=True).then_inc(summed, 1)

        @block.vector
        def _(dve):
            n = 0

            def step(ins):
                nonlocal n
                n += 1
                ins.then_inc(v_done, 1)
                dve.wait_ge(v_done, n)

            for j in range(N):
                step(dve.tensor_scalar(kk[:, j, :], k[:, j, :], col(m, "k_k", j), None, ALU.mult))
            step(dve.tensor_scalar(one_less[:, :], ka, -1.0, 1.0, ALU.mult, ALU.add))
            for j in range(N):
                step(dve.tensor_scalar(bonus_rows[:, j, :], a[:, j, :], col(m, "k_a", j), one_less[:, j:j + 1], ALU.mult, ALU.add))
                step(dve.tensor_tensor(k[:, j, :], k[:, j, :], bonus_rows[:, j, :], ALU.mult))
            dve.wait_ge(a_done, 2)
            step(dve.tensor_scalar(sq[:, :, :], sq[:, :, :], 1e-12, None, ALU.max))
            step(dve.reciprocal(sq[:, :, :], sq[:, :, :]))
            step(dve.scalar_tensor_tensor(out=kk[:, :, :], in0=kk[:, :, :], scalar=-1.0, in1=sq[:, :, :], op0=ALU.mult, op1=ALU.mult))
            step(dve.scalar_tensor_tensor(out=b[:, :, :], in0=kk[:, :, :], scalar=-1.0, in1=a[:, :, :], op0=ALU.mult, op1=ALU.mult))
            for j in range(N):
                step(dve.scalar_tensor_tensor(out=sq[:, j, :], in0=r[:, j, :], scalar=col(m, "r_k", j), in1=k[:, j, :],
                                              op0=ALU.mult, op1=ALU.mult))
            assert n == STEPS
            for j in range(N):
                dve.wait_ge(summed, N + j + 1)
                step(dve.tensor_copy(bonus_rows[:, j, :], ps[:, N + j, :]))


def rw_scale_phase(m, rw, ld, kk, b, bd, kd, last):
    nc = m.nc
    N = 4
    r, k = rw[:, 0:4], rw[:, 4:8]
    with Phase(m, "rw_scale") as ph:
        run, e = ph.sb("run", [P, N, T]), ph.sb("e", [P, N, T])
        scanned, before, a_done, v_done = (ph.sem(s) for s in ("scanned", "before", "a_done", "v_done"))
        block = ph.enter_context(nc.Block())
        chunks = lambda x: x.rearrange("p j (c t) -> p j c t", t=CH)

        @block.scalar
        def _(act):
            act.wait_ge(scanned, N)
            act.activation(e[:, :, :], run[:, :, :], ACT.Exp).then_inc(a_done, 1)
            act.wait_ge(before, 1)
            act.activation(ld[:, :, :], ld[:, :, :], ACT.Exp).then_inc(a_done, 1)
            act.activation(run[:, :, :], run[:, :, :], ACT.Exp, scale=-1.0).then_inc(a_done, 1)

        @block.vector
        def _(dve):
            n = 0

            def step(ins):
                nonlocal n
                n += 1
                ins.then_inc(v_done, 1)
                dve.wait_ge(v_done, n)

            for j in range(N):
                dve.tensor_tensor_scan(run[:, j, :], m.reset[:, :], ld[:, j, :], 0.0, ALU.mult, ALU.add).then_inc(scanned, 1)
            dve.wait_ge(scanned, N)
            dve.tensor_tensor(ld[:, :, :], run[:, :, :], ld[:, :, :], ALU.subtract).then_inc(before, 1)
            dve.wait_ge(a_done, 1)
            step(dve.tensor_tensor(r[:, :, :], r[:, :, :], e[:, :, :], ALU.mult))
            step(dve.tensor_copy(last[:, :, :], e[:, :, CH - 1:T:CH]))
            dve.wait_ge(a_done, 2)
            step(dve.tensor_tensor(kk[:, :, :], kk[:, :, :], ld[:, :, :], ALU.mult))
            dve.wait_ge(a_done, 3)
            step(dve.tensor_tensor(b[:, :, :], b[:, :, :], run[:, :, :], ALU.mult))
            step(dve.tensor_tensor(k[:, :, :], k[:, :, :], run[:, :, :], ALU.mult))
            for j in range(N):
                end = last[:, j, :].unsqueeze(2).to_broadcast([P, NCH, CH])
                step(dve.tensor_tensor(chunks(bd[:, :, :])[:, j], chunks(b[:, :, :])[:, j], end, ALU.mult))
                step(dve.tensor_tensor(chunks(kd[:, :, :])[:, j], chunks(k[:, :, :])[:, j], end, ALU.mult))


def rw_out_phase(m, y, v, bonus, g, hi, lo):
    nc = m.nc
    N = 4
    with Phase(m, "rw_out") as ph:
        sq = ph.sb("sq", [P, N, T])
        lnx_eps = ph.sb("lnx_eps", [P, 1])
        ps = ph.banks()
        v_done, a_done, summed, eps_done = (ph.sem(s) for s in ("v_done", "a_done", "summed", "eps_done"))
        block = ph.enter_context(nc.Block())

        @block.gpsimd
        def _(pool):
            pool.memset(lnx_eps[:, :], 64e-5).then_inc(eps_done, 1)

        @block.tensor
        def _(pe):
            for j in range(N):
                pe.matmul(ps[:, j, :], m.pair_ones[:, :], y[:, j, :], start=True, stop=True).then_inc(summed, 1)
            pe.wait_ge(a_done, 1)
            for j in range(N):
                pe.matmul(ps[:, N + j, :], m.pair_ones[:, :], sq[:, j, :], start=True, stop=True).then_inc(summed, 1)

        @block.scalar
        def _(act):
            act.wait_ge(v_done, 1)
            act.activation(sq[:, :, :], y[:, :, :], ACT.Square).then_inc(a_done, 1)
            act.wait_ge(summed, 2 * N)
            act.wait_ge(eps_done, 1)
            act.activation(sq[:, :, :], ps[:, N:2 * N, :], ACT.Ln, scale=1.0 / HD, bias=lnx_eps[:, 0:1]).then_inc(a_done, 1)
            act.wait_ge(a_done, 2)
            act.activation(sq[:, :, :], sq[:, :, :], ACT.Exp, scale=-0.5).then_inc(a_done, 1)
            act.wait_ge(v_done, 2 + 2 * N + 1)
            act.activation(hi[:, :, :], y[:, :, :], ACT.Copy).then_inc(a_done, 1)

        @block.vector
        def _(dve):
            n = 0

            def step(ins):
                nonlocal n
                n += 1
                ins.then_inc(v_done, 1)
                dve.wait_ge(v_done, n)

            dve.wait_ge(summed, N)
            step(dve.scalar_tensor_tensor(out=y[:, :, :], in0=ps[:, 0:N, :], scalar=-1.0 / HD, in1=y[:, :, :], op0=ALU.mult, op1=ALU.add))
            step(dve.tensor_tensor(v[:, :, :], v[:, :, :], bonus[:, :, :], ALU.mult))
            dve.wait_ge(a_done, 3)
            for j in range(N):
                step(dve.scalar_tensor_tensor(out=y[:, j, :], in0=y[:, j, :], scalar=col(m, "lnx_g", j), in1=sq[:, j, :],
                                              op0=ALU.mult, op1=ALU.mult))
                step(dve.scalar_tensor_tensor(out=y[:, j, :], in0=y[:, j, :], scalar=col(m, "lnx_b", j), in1=v[:, j, :],
                                              op0=ALU.add, op1=ALU.add))
            step(dve.tensor_tensor(y[:, :, :], y[:, :, :], g[:, :, :], ALU.mult))
            dve.wait_ge(a_done, 4)
            step(dve.tensor_tensor(lo[:, :, :], y[:, :, :], hi[:, :, :].bitcast(F32), ALU.subtract))


def bias_job(m, ps, w, first, groups, nf, dst, name, bias0):
    def load(g, c):
        return [(0, nf * P, k_major(w)[:, :, bass.ds(g * (nf * P) + first, nf * P)])]

    def dve(eng, g, b, n):
        for f in range(nf):
            c = g * nf + (m.columns[name] + bias0 + f)
            last = eng.tensor_scalar(dst[:, bass.ds(g * nf + f, 1), :], ps[:, b + f, :], m.params[:, bass.ds(c, 1)], None, ALU.add)
        return last

    return Job(groups, nf, load, m.act_hi, m.act_lo, dve)


def second_mixer(m):
    i = m.ins
    w = i["w_in_2"][0]
    RW = 14
    norm_phase(m, m.xT, "norm_mix_g", m.act_hi, m.act_lo)
    with Phase(m, "mix2") as s:
        rw = s.sb("rw", [P, RW, T])
        with Phase(m, "pxy") as s2:
            px, py = s2.sb("px", [P, 4, T]), s2.sb("py", [P, 4, T])
            dense_phase(m, lambda ph, ps: [bias_job(m, ps, w, 0, 7, 2, rw, "b_in", 0),
                                           bias_job(m, ps, w, RW * P, 2, 2, px, "b_in", RW),
                                           bias_job(m, ps, w, (RW + 4) * P, 2, 2, py, "b_in", RW + 4)], "proj2")
            rg_phase(m, px, py, m.act_hi[:, 4:8], m.act_lo[:, 4:8])
        rw_shift_phase(m, rw)
        r = Rule()
        r.heads, r.decayed = 8, False
        kk, b, g, bonus = (s.sb(n, [P, 4, T]) for n in ("kk", "b", "g", "bonus"))
        r.last = s.sb("last", [P, 4, NCH])
        r.a_tok, r.v_tok, r.bd_tok, r.kd_tok = (s.sb(n, [P, TT, 4 * P]) for n in ("a_tok", "v_tok", "bd_tok", "kd_tok"))
        with Phase(m, "ld") as s3:
            ld, a = s3.sb("ld", [P, 4, T]), s3.sb("a", [P, 4, T])
            rw_lora_phase(m, rw, ld, a, g)
            rw_keys_phase(m, rw, a, kk, b, bonus)
            with Phase(m, "bdkd") as s4:
                kd = s4.sb("kd", [P, 4, T])
                rw_scale_phase(m, rw, ld, kk, b, a, kd, r.last)
                turn_phase(m, a, r.bd_tok, 4)
                turn_phase(m, kd, r.kd_tok, 4)
        turn_phase(m, kk, r.a_tok, 4)
        turn_phase(m, rw[:, 8:12], r.v_tok, 4)
        with Phase(m, "qb") as s5:
            r.qb = s5.sb("qb", [P, 8, TT, P])
            r.k_t, r.a_t, r.b_t, r.q_t, r.r_t = rw[:, 4:8], kk, b, rw[:, 0:4], rw[:, 0:4]
            r.w_t, r.y_t, r.tz_tok, r.u_tok = kk, rw[:, 4:8], r.a_tok, r.a_tok
            chunk_phase(m, r)
            r.states = s5.sb("states", [P, NCH, 4, HD])
            scan_phase(m, r)
            read_phase(m, r)
        rw_out_phase(m, rw[:, 4:8], rw[:, 8:12], bonus, g, m.act_hi[:, 0:4], m.act_lo[:, 0:4])
    with Phase(m, "merge") as s:
        h_hi, h_lo = s.sb("h_hi", [P, DT, T], F32R), s.sb("h_lo", [P, DT, T], F32R)
        norm_phase(m, m.xT, "norm_mix_g", h_hi, h_lo)
        ga, gb = s.sb("ga", [P, DT, T]), s.sb("gb", [P, DT, T])

        def jobs(ph, ps):
            sig, merged, m_hi, times = ph.sem("sig"), ph.sem("merged"), ph.sem("m_hi"), ph.sem("times")

            def gate_job(dst, n0, tile0):
                def load(g, c):
                    return [(0, 2 * P, k_major(w)[:, :, bass.ds(g * (2 * P) + tile0 * P, 2 * P)])]

                def act(eng, g, b, n):
                    for f in range(2):
                        c = g * 2 + (m.columns["b_in"] + tile0 + f)
                        eng.activation(dst[:, bass.ds(g * 2 + f, 1), :], ps[:, b + f, :], ACT.Sigmoid,
                                       bias=m.params[:, bass.ds(c, 1)]).then_inc(sig, 1)

                def dve(eng, g, b, n):
                    eng.wait_ge(sig, n * 2 + 2 * n0)
                    return eng.nop()

                return Job(4, 2, load, h_hi, h_lo, dve, act)

            def branch_job(w_branch, first, second):
                def load(g, c):
                    return [(0, 4 * P, k_major(w_branch)[:, :, bass.ds(g * (4 * P), 4 * P)])]

                def dve(eng, g, b, n):
                    gate = (gb if second else ga)[:, bass.ds(g * 4, 4), :]
                    if not second:
                        return eng.tensor_tensor(gate, gate, ps[:, b:b + 4, :], ALU.mult)
                    into = ga[:, bass.ds(g * 4, 4), :]
                    eng.tensor_tensor(gate, gate, ps[:, b:b + 4, :], ALU.mult).then_inc(times, 1)
                    eng.wait_ge(times, n)
                    eng.tensor_tensor(into, into, gate, ALU.add).then_inc(merged, 1)
                    eng.wait_ge(m_hi, n)
                    return eng.tensor_tensor(h_lo[:, bass.ds(g * 4, 4), :], into, h_hi[:, bass.ds(g * 4, 4), :].bitcast(F32),
                                             ALU.subtract)

                def act(eng, g, b, n):
                    eng.wait_ge(merged, n)
                    eng.activation(h_hi[:, bass.ds(g * 4, 4), :], ga[:, bass.ds(g * 4, 4), :], ACT.Copy).then_inc(m_hi, 1)

                x = slice(first, first + 4)
                return Job(2, 4, load, m.act_hi[:, x], m.act_lo[:, x], dve, act if second else None, kt=4)

            out = add_job(m, i["w_mix_out_2"][0], ps)
            out.hi, out.lo, out.after = h_hi, h_lo, 3
            return [gate_job(ga, 0, RW + 8), gate_job(gb, 4, RW + 16), branch_job(i["w_branch_a_2"][0], 0, False),
                    branch_job(i["w_branch_b_2"][0], 4, True), out]

        dense_phase(m, jobs, "merge")


def memory_phase(m, mem_t):
    nc = m.nc
    with Phase(m, "memory") as ph:
        rows = ph.sb("rows", [P, 2, D])
        ps = ph.banks()
        landed, turned, kept = ph.sem("landed"), ph.sem("turned"), ph.sem("kept")
        block = ph.enter_context(nc.Block())

        @block.sync
        def _(sp):
            sp.dma_start(rows[:, :, :], m.ins["mem_2"][0].rearrange("(t p) d -> p t d", p=P)).then_inc(landed, 16)

        @block.tensor
        def _(pe):
            pe.wait_ge(landed, 16)
            for k in range(DT):
                for t in range(2):
                    last = pe.transpose(ps[:, k, t * P:(t + 1) * P], rows[:, t, k * P:(k + 1) * P], m.ident[:, :])
                last.then_inc(turned, 1)

        @block.vector
        def _(dve):
            for k in range(DT):
                dve.wait_ge(turned, k + 1)
                dve.tensor_copy(mem_t[:, k, :], ps[:, k, 0:2 * P]).then_inc(kept, 1)


def cross_attention_phase(m, q, k, v_tok, o_t):
    nc = m.nc
    H, M = 4, 256
    with Phase(m, "cross") as ph:
        prob, prob_t = ph.sb("prob", [P, TT, M]), ph.sb("prob_t", [P, 2, T])
        top, total = ph.sb("top", [P, TT]), ph.sb("total", [P, TT])
        ps = ph.banks()
        scored, topped, exped, inverse, normed, turned, kept, out_full, out_kept = (
            ph.sem(s) for s in ("scored", "topped", "exped", "inverse", "normed", "turned", "kept", "out_full", "out_kept"))
        block = ph.enter_context(nc.Block())

        @block.tensor
        def _(pe):
            for h in range(H):
                for i in range(TT):
                    n = TT * h + i
                    if h:
                        pe.wait_ge(exped, n - TT + 1)
                    for d in range(2):
                        last = pe.matmul(ps[:, i, 0:M], q[:, 2 * h + d, i * P:(i + 1) * P], k[:, 2 * h + d, :], start=d == 0, stop=d == 1)
                    last.then_inc(scored, 1)
                pe.wait_ge(normed, TT * (h + 1))
                for j in range(2):
                    if h:
                        pe.wait_ge(kept, 2 * (h - 1) + j + 1)
                    for i in range(TT):
                        last = pe.transpose(ps[:, 4 + j, i * P:(i + 1) * P], prob[:, i, j * P:(j + 1) * P], m.ident[:, :])
                    last.then_inc(turned, 1)
                pe.wait_ge(kept, 2 * (h + 1))
                for d in range(2):
                    if h:
                        pe.wait_ge(out_kept, 2 * (h - 1) + d + 1)
                    for j in range(2):
                        last = pe.matmul(ps[:, 6 + d, :], v_tok[:, j, (2 * h + d) * P:(2 * h + d + 1) * P], prob_t[:, j, :],
                                         start=j == 0, stop=j == 1)
                    last.then_inc(out_full, 1)

        @block.vector
        def _(dve):
            for h in range(H):
                for i in range(TT):
                    n = TT * h + i
                    dve.wait_ge(scored, n + 1)
                    if h:
                        dve.wait_ge(exped, n - TT + 1)
                    dve.tensor_reduce(top[:, i:i + 1], ps[:, i, 0:M], AX.X, ALU.max, negate=True).then_inc(topped, 1)
                for i in range(TT):
                    n = TT * h + i
                    dve.wait_ge(exped, n + 1)
                    dve.reciprocal(total[:, i:i + 1], total[:, i:i + 1]).then_inc(inverse, 1)
                    dve.wait_ge(inverse, n + 1)
                    dve.tensor_scalar(prob[:, i, :], prob[:, i, :], total[:, i:i + 1], None, ALU.mult).then_inc(normed, 1)
                for d in range(2):
                    dve.wait_ge(out_full, 2 * h + d + 1)
                    dve.tensor_copy(o_t[:, 2 * h + d, :], ps[:, 6 + d, :]).then_inc(out_kept, 1)

        @block.scalar
        def _(act):
            for h in range(H):
                for i in range(TT):
                    n = TT * h + i
                    act.wait_ge(topped, n + 1)
                    if h:
                        act.wait_ge(turned, 2 * h)
                        act.wait_ge(normed, n - TT + 1)
                    act.activation(prob[:, i, :], ps[:, i, 0:M], ACT.Exp, bias=top[:, i:i + 1],
                                   accum_out=total[:, i:i + 1]).then_inc(exped, 1)
                for j in range(2):
                    act.wait_ge(turned, 2 * h + j + 1)
                    if h:
                        act.wait_ge(out_full, 2 * h)
                    act.activation(prob_t[:, j, :], ps[:, 4 + j, :], ACT.Copy).then_inc(kept, 1)


def cross_mixer(m):
    i = m.ins
    M = 256
    norm_phase(m, m.xT, "norm_x_g", m.act_hi, m.act_lo)
    with Phase(m, "cr") as s:
        q, k = s.sb("q", [P, DT, T]), s.sb("k", [P, DT, M])
        v_tok = s.sb("v_tok", [P, 2, D])
        with Phase(m, "cr2") as s2:
            mem_t, v = s2.sb("mem_t", [P, DT, M]), s2.sb("v", [P, DT, M])
            mem_hi, mem_lo = s2.sb("mem_hi", [P, DT, M], F32R), s2.sb("mem_lo", [P, DT, M], F32R)
            memory_phase(m, mem_t)
            norm_phase(m, mem_t, "norm_mem_g", mem_hi, mem_lo, DT, M)

            def jobs(ph, ps):
                def dve(eng, g, b, n):
                    return eng.tensor_scalar(q[:, bass.ds(g * 2, 2), :], ps[:, b:b + 2, :], 1.0 / 16, None, ALU.mult)

                q_job = plain_job(m, i["w_cq_2"][0], 0, 4, 2, q, ps=ps)
                q_job.dve = dve
                more = dict(ps=ps, n=M, hi=mem_hi, lo=mem_lo)
                return [q_job, plain_job(m, i["w_ckv_2"][0], 0, 4, 2, k, **more), plain_job(m, i["w_ckv_2"][0], D, 4, 2, v, **more)]

            dense_phase(m, jobs, "cross_proj")
            turn_phase(m, v, v_tok, DT, M)
        o = s.sb("o", [P, DT, T])
        cross_attention_phase(m, q, k, v_tok, o)
        gate_split_phase(m, o, None, None, DT, m.act_hi, m.act_lo)
    dense_phase(m, lambda ph, ps: [add_job(m, i["w_co_2"][0], ps)], "w_co")


def conv_ffn_phase(m):
    i = m.ins
    norm_phase(m, m.xT, "norm_ffn_g", m.act_hi, m.act_lo)
    half = 11
    for s in range(2):
        w = i["w_ffn_in_2"][0]
        f = slice(s * half * P, (s + 1) * half * P)

        def jobs(ph, ps):
            jobs = swiglu_jobs(m, ph, ps, w[:, f], w[:, 22 * P + s * half * P:22 * P + (s + 1) * half * P],
                               i["w_ffn_out_2"][0][f, :], half, half, 1)
            up = jobs[0]
            conv, tap = ph.sb("conv", [P, T]), [ph.sem("tap0"), ph.sem("tap1")]
            act0, dve0 = up.act, up.dve
            param = lambda name, g: m.params[:, bass.ds(g + (m.columns[name] + s * half), 1)]

            def act(eng, g, b, n):
                eng.activation(conv[:, :], ps[:, b, :], ACT.Identity, scale=param("ffn_conv_w_2", g),
                               bias=param("ffn_conv_b", g)).then_inc(tap[0], 1)
                eng.wait_ge(tap[1], n * 2)
                act0(eng, g, b, n, conv[:, :], ACT.Gelu_apprx_tanh)

            def dve(eng, g, b, n):
                eng.wait_ge(tap[0], n)
                for d in (1, 2):
                    if d == 2:
                        eng.wait_ge(tap[1], n * 2 - 1)
                    ins = eng.scalar_tensor_tensor(out=conv[:, d:T], in0=ps[:, b, 0:T - d], scalar=param(f"ffn_conv_w_{2 - d}", g),
                                                   in1=conv[:, d:T], op0=ALU.mult, op1=ALU.add)
                    ins.then_inc(tap[1], 1)
                return dve0(eng, g, b, n)

            up.act, up.dve = act, dve
            return jobs

        dense_phase(m, jobs, "conv_ffn")


def final_norm_phase(m, x, gain):
    nc = m.nc
    with Phase(m, "final") as ph:
        sq = ph.sb("sq", [P, DT, T])
        rstd = ph.sb("rstd", [P, T])
        ps = ph.banks(1)
        squared, summed, root, scaled = (ph.sem(s) for s in ("squared", "summed", "root", "scaled"))
        block = ph.enter_context(nc.Block())

        @block.scalar
        def _(act):
            for k in range(DT):
                act.activation(sq[:, k, :], x[:, k, :], ACT.Square).then_inc(squared, 1)
            act.wait_ge(summed, 1)
            act.activation(rstd[:, :], ps[:, 0, :], ACT.Ln, scale=1.0 / D, bias=m.eps[:, 0:1]).then_inc(root, 1)
            act.wait_ge(root, 1)
            act.activation(rstd[:, :], rstd[:, :], ACT.Exp, scale=-0.5).then_inc(root, 1)

        @block.tensor
        def _(pe):
            for k in range(DT):
                pe.wait_ge(squared, k + 1)
                last = pe.matmul(ps[:, 0, :], m.ones[:, :], sq[:, k, :], start=k == 0, stop=k == DT - 1)
            last.then_inc(summed, 1)

        @block.vector
        def _(dve):
            dve.wait_ge(root, 2)
            for k in range(DT):
                dve.scalar_tensor_tensor(out=x[:, k, :], in0=x[:, k, :], scalar=col(m, gain, k), in1=rstd[:, :],
                                         op0=ALU.mult, op1=ALU.mult).then_inc(scaled, 1)




def program(m):
    with Phase(m, "keep") as keep:
        setup_phase(m, keep)
        masks_phase(m, keep)
        mixer(m, 0)
        norm_phase(m, m.xT, "norm2_0", m.act_hi, m.act_lo)
        ffn_phase(m)
        mixer(m, 1)
        moe_phase(m)
        second_mixer(m)
        cross_mixer(m)
        conv_ffn_phase(m)
        final_norm_phase(m, m.xT, "norm_final_g")
        out_phase(m, m.xT)


def kernel(**inputs):
    import numpy as np

    import concourse.bacc as bacc
    from concourse.bass_utils import run_bass_kernel_spmd

    nc = bacc.Bacc("TRN2", target_bir_lowering=False, num_devices=1)
    arrays, ins = {}, {}
    for name, a in inputs.items():
        a = np.ascontiguousarray(a)
        arrays[f"in_{name}"] = a
        ins[name] = nc.dram_tensor(f"in_{name}", a.shape, mybir.dt.from_np(a.dtype), kind="ExternalInput").ap()
    out = nc.dram_tensor("out", inputs["x"].shape, F32, kind="ExternalOutput").ap()
    program(Machine(nc, ins, out))
    return run_bass_kernel_spmd(nc, [arrays], core_ids=[0]).results[0]["out"]
```

```python
import math
from contextlib import ExitStack

import concourse.bass as bass
from concourse import mybir

F32 = mybir.dt.float32
F32R = mybir.dt.float32r
ALU = mybir.AluOpType
ACT = mybir.ActivationFunctionType
AX = mybir.AxisListType

P = 128
T = 512
D = 1024
DT = D // P
TT = T // P
HD = 64
CH = 64
NCH = T // CH
EPS = 1e-6
BANK = 512
SLOT = 3 * DT * P


class Machine:

    def __init__(self, nc, ins, out):
        self.nc, self.ins, self.out = nc, ins, out
        self.columns = {}
        self.phases = 0
        self.free_sems, self.cleared_sems = [], []

    def name(self, what):
        self.phases += 1
        return f"{what}_{self.phases}"


class Phase(ExitStack):

    def __init__(self, m, what):
        super().__init__()
        self.m, self.nc, self.what, self.sems, self.tensors = m, m.nc, m.name(what), [], 0

    def sb(self, name, shape, dt=F32):
        self.tensors += 1
        return self.enter_context(self.nc.sbuf_tensor(f"{self.what}_{self.tensors}_{name}", shape, dt))

    def banks(self, n=8):
        return self.enter_context(self.nc.psum_tensor(f"{self.what}_psum", [P, n, BANK], F32))

    def sem(self, name):
        s = self.m.free_sems.pop() if self.m.free_sems else self.nc.alloc_semaphore(f"{name}_{self.what}_{len(self.sems)}")
        self.sems.append(s)
        return s

    def __exit__(self, *error):
        result = super().__exit__(*error)
        if error[0] is None and self.sems:
            for s in self.sems:
                self.nc.gpsimd.sem_clear(s)
            self.m.free_sems += self.m.cleared_sems
            self.m.cleared_sems = self.sems
        return result


class Part:

    def __init__(self, sync=None, gpsimd=None, tensor=None, scalar=None, vector=None, start=None, first_tap=None, taps=None,
                 squares=None, sums=None, root=None, scaled=None, steps=None):
        self.sync, self.gpsimd, self.tensor, self.scalar, self.vector = sync, gpsimd, tensor, scalar, vector
        self.start, self.first_tap, self.taps, self.squares, self.sums = start, first_tap, taps, squares, sums
        self.root, self.scaled, self.steps = root, scaled, steps


def k_major(w):
    return w.rearrange("(k p) n -> p k n", p=P)




def row_params(m):
    rows, i = [], m.ins

    def vectors(names, ap, n, width=P, twice=False):
        src = ap.rearrange("(k p) -> k p", p=width)
        rows.append((names, src, n // width, width, twice))

    layers = lambda name: [f"{name}_{l}" for l in range(2)]
    flat = lambda ap: ap.rearrange("a n -> (a n)")
    vectors(layers("norm1"), flat(i["norm1"]), D)
    vectors(layers("norm2"), flat(i["norm2"]), D)
    vectors([f"dn_conv_{l}_{j}" for l in range(2) for j in range(4)], i["dn_conv"].rearrange("l j n -> (l j n)"), 9 * P)
    vectors(layers("dn_onorm"), flat(i["dn_onorm"]), HD, HD, True)
    vectors(layers("fx_qnorm"), flat(i["fx_qnorm"]), HD, HD, True)
    vectors(layers("fx_knorm"), flat(i["fx_knorm"]), HD, HD, True)
    vectors(layers("pool_scale"), flat(i["pool_scale"]), 2 * P)
    vectors(layers("a_log"), flat(i["dn_a_log"]), 6, 6)
    vectors(layers("dt_bias"), flat(i["dn_dt_bias"]), 6, 6)
    vectors(layers("f_bias"), flat(i["fx_f_bias"]), 6, 6)
    for name, n in (("norm_mix_g", D), ("norm_x_g", D), ("norm_mem_g", D), ("norm_ffn_g", D), ("b_in", 4864),
                    ("mu_shift", 1792), ("w0", 512), ("a0", 512), ("k_k", 512), ("k_a", 512), ("lnx_g", 512),
                    ("lnx_b", 512), ("conv_b_b", 512), ("b_rg_a", 512), ("b_rg_x", 512), ("lru_lambda", 512),
                    ("ffn_conv_b", 2816)):
        vectors([name], i[name + "_2"][0], n)
    vectors(["norm_final_g"], i["norm_final_g_2"], D)
    vectors(["r_k"], i["r_k_2"][0].rearrange("h d -> (h d)"), 512)
    vectors([f"conv_b_w_{j}" for j in range(4)], flat(i["conv_b_w_2"][0]), 512)
    vectors([f"ffn_conv_w_{j}" for j in range(3)], flat(i["ffn_conv_w_2"][0]), 2816)
    return rows


def setup_phase(m, persist):
    nc = m.nc
    rows = row_params(m)
    total = sum(len(names) * n for names, _, n, _, _ in rows)
    stages = -(-total // P)
    m.ident = persist.sb("ident", [P, P])
    m.ones = persist.sb("ones", [P, P])
    m.pair_ones = persist.sb("pair_ones", [P, P])
    m.params = persist.sb("params", [P, stages * P])
    m.xT = persist.sb("xT", [P, DT, T])
    m.act_hi = persist.sb("act_hi", [P, DT, T], F32R)
    m.act_lo = persist.sb("act_lo", [P, DT, T], F32R)
    m.eps = persist.sb("eps", [P, 1])
    mask_buffers(m, persist)
    with Phase(m, "setup") as ph:
        stage = ph.sb("stage", [P, stages, P])
        xs = ph.sb("xs", [P, TT, D])
        ps = ph.banks()
        zeroed, filled, const, masked = ph.sem("zeroed"), ph.sem("filled"), ph.sem("const"), ph.sem("masked")
        x_landed, turned, copied = ph.sem("x_landed"), ph.sem("turned"), ph.sem("copied")
        block = ph.enter_context(nc.Block())
        places, at = [], 0
        for names, src, n, width, twice in rows:
            for v, name in enumerate(names):
                m.columns[name] = at + v * n
            done = 0
            while done < len(names) * n:
                k = min(len(names) * n - done, P - at % P)
                for o in (0, HD) if twice else (0,):
                    places.append((at // P, at % P, k, o, width, src[done:done + k, :]))
                at += k
                done += k

        @block.gpsimd
        def _(pool):
            pool.memset(stage[:, :, :], 0.0).then_inc(zeroed, 1)
            pool.memset(m.ident[:, :], 0.0).then_inc(const, 1)
            pool.memset(m.ones[:, :], 1.0).then_inc(const, 1)
            pool.memset(m.eps[:, :], EPS).then_inc(const, 1)
            pool.memset(m.pair_ones[:, :], 0.0).then_inc(const, 1)
            pool.wait_ge(const, 4)
            pool.memset(m.pair_ones[0:HD, 0:HD], 1.0).then_inc(const, 1)
            pool.memset(m.pair_ones[HD:P, HD:P], 1.0).then_inc(const, 1)
            pool.wait_ge(const, 6)
            pool.affine_select(out=m.ident[:, :], in_=m.ident[:, :], compare_op=ALU.not_equal, fill=1.0, base=0,
                               pattern=[[-1, P]], channel_multiplier=1).then_inc(const, 1)
            make_masks(m, pool, masked)

        @block.sync
        def _(sp):
            sp.dma_start(xs[:, :, :], m.ins["x"][0].rearrange("(t p) d -> p t d", p=P)).then_inc(x_landed, 16)
            sp.wait_ge(zeroed, 1)
            for s, r, k, o, width, src in places:
                sp.dma_start(stage[r:r + k, s, o:o + width], src).then_inc(filled, 16)

        jobs = [("x", k) for k in range(DT)] + [("param", s) for s in range(stages)]

        @block.tensor
        def _(pe):
            pe.wait_ge(const, 7)
            pe.wait_ge(x_landed, 16)
            for n, (kind, k) in enumerate(jobs):
                if n >= 8:
                    pe.wait_ge(copied, n - 7)
                if kind == "x":
                    for t in range(TT):
                        last = pe.transpose(ps[:, n % 8, t * P:(t + 1) * P], xs[:, t, k * P:(k + 1) * P], m.ident[:, :])
                else:
                    if k == 0:
                        pe.wait_ge(filled, 16 * len(places))
                    last = pe.transpose(ps[:, n % 8, 0:P], stage[:, k, :], m.ident[:, :])
                last.then_inc(turned, 1)

        @block.vector
        def _(dve):
            for n, (kind, k) in enumerate(jobs):
                dve.wait_ge(turned, n + 1)
                dst, w = (m.xT[:, k, :], T) if kind == "x" else (m.params[:, k * P:(k + 1) * P], P)
                dve.tensor_copy(dst, ps[:, n % 8, 0:w]).then_inc(copied, 1)


def col(m, name, k=0):
    c = m.columns[name] + k
    return m.params[:, c:c + 1]




class Norm:

    def __init__(self, m, ph, ps, x, gain, hi, lo, nt=DT, n=T, full=None):
        self.m, self.x, self.gain, self.hi, self.lo, self.nt, self.n = m, x, gain, hi, lo, nt, n
        self.sq = full if full is not None else ph.sb("sq", [P, nt, n])
        self.rstd = ph.sb("rstd", [P, n])
        self.sums = ps[:, 0, 0:n]
        self.squared, self.summed, self.root, self.done, self.rounded = (
            ph.sem(s) for s in ("squared", "summed", "root", "normed", "norm_rounded"))

    def ready(self, t):
        return self.nt + t + 1

    def roots(self, act):
        for k in range(self.nt):
            act.activation(self.sq[:, k, :], self.x[:, k, :], ACT.Square).then_inc(self.squared, 1)
        act.wait_ge(self.summed, 1)
        act.activation(self.rstd[:, :], self.sums, ACT.Ln, scale=1.0 / D, bias=self.m.eps[:, 0:1]).then_inc(self.root, 1)
        act.wait_ge(self.root, 1)
        act.activation(self.rstd[:, :], self.rstd[:, :], ACT.Exp, scale=-0.5).then_inc(self.root, 1)

    def sum_up(self, pe):
        for k in range(self.nt):
            pe.wait_ge(self.squared, k + 1)
            last = pe.matmul(self.sums, self.m.ones[:, :], self.sq[:, k, :], start=k == 0, stop=k == self.nt - 1)
        last.then_inc(self.summed, 1)

    def scale(self, dve):
        dve.wait_ge(self.root, 2)
        for k in range(self.nt):
            dve.scalar_tensor_tensor(out=self.sq[:, k, :], in0=self.x[:, k, :], scalar=col(self.m, self.gain, k), in1=self.rstd[:, :],
                                     op0=ALU.mult, op1=ALU.mult).then_inc(self.done, 1)

    def round_tiles(self, act):
        for k in range(self.nt):
            act.wait_ge(self.done, k + 1)
            act.activation(self.hi[:, k, :], self.sq[:, k, :], ACT.Copy).then_inc(self.rounded, 1)

    def rest_tiles(self, dve):
        for k in range(self.nt):
            dve.wait_ge(self.rounded, k + 1)
            dve.tensor_tensor(self.lo[:, k, :], self.sq[:, k, :], self.hi[:, k, :].bitcast(F32), ALU.subtract).then_inc(self.done, 1)


class Split:

    def __init__(self, ph, tiles, hi, lo):
        self.tiles, self.hi, self.lo = tiles, hi, lo
        self.rounded, self.done = ph.sem("y_rounded"), ph.sem("y_done")

    def ready(self, t):
        return max(1, t - (DT - len(self.tiles)) + 1)

    def roots(self, act):
        for t, y in enumerate(self.tiles):
            act.activation(self.hi[:, t, :], y, ACT.Copy).then_inc(self.rounded, 1)

    def scale(self, dve):
        for t, y in enumerate(self.tiles):
            dve.wait_ge(self.rounded, t + 1)
            dve.tensor_tensor(self.lo[:, t, :], y, self.hi[:, t, :].bitcast(F32), ALU.subtract).then_inc(self.done, 1)

    def round_tiles(self, act):
        pass

    def rest_tiles(self, dve):
        pass

    def sum_up(self, pe):
        pass


def norm_of(m, gain, hi=None, lo=None, full=None):
    return lambda ph, ps: Norm(m, ph, ps, m.xT, gain, m.act_hi if hi is None else hi, m.act_lo if lo is None else lo, full=full)


def norm_phase(m, x, gain, hi, lo, nt=DT, n=T, full=None):
    nc = m.nc
    with Phase(m, "norm") as ph:
        norm = Norm(m, ph, ph.banks(1), x, gain, hi, lo, nt, n, full)
        block = ph.enter_context(nc.Block())

        @block.scalar
        def _(act):
            norm.roots(act)
            norm.round_tiles(act)

        @block.tensor
        def _(pe):
            norm.sum_up(pe)

        @block.vector
        def _(dve):
            norm.scale(dve)
            norm.rest_tiles(dve)




def halves_of(nf):
    return (nf // 2, nf - nf // 2)


def two_loads(w, first, nf):
    a, b = halves_of(nf)
    return [w[:, :, bass.ds(first, a * P)], w[:, :, bass.ds(first + a * P, b * P)]]


class Job:

    def __init__(self, groups, nf, load, hi, lo, dve, act=None, kt=DT, parts=1, n=T, loads=(1, 1), after=None):
        self.groups, self.nf, self.load, self.hi, self.lo = groups, nf, load, hi, lo
        self.dve, self.act, self.kt, self.parts, self.n, self.loads, self.after = dve, act, kt, parts, n, loads, after
        self.heads = halves_of(nf)[0]
        assert kt * nf * P <= SLOT and 2 <= nf <= 4

    def half(self, q):
        return range(0, self.heads) if q == 0 else range(self.heads, self.nf)

    def view(self, buffer, q):
        tiles = self.half(q)
        return buffer[:, self.kt * P * tiles.start:self.kt * P * tiles.stop].rearrange("p (k n) -> p k n", k=self.kt)


def over_groups(eng, groups, body, peel=False):
    pairs = groups // 2
    if peel or pairs == 1:
        for g in range(2):
            body(0, g)
    if pairs > 1:
        with eng.Fori(int(peel), pairs) as i:
            for k in range(2):
                body(i, k)
    if groups % 2:
        body(pairs, 0)


def dense_phase(m, make_jobs, what="dense", first=None):
    nc = m.nc
    with Phase(m, what) as ph:
        raw = [ph.sb(f"raw{s}", [P, SLOT]) for s in range(2)]
        w_hi = [ph.sb(f"w_hi{s}", [P, SLOT], F32R) for s in range(2)]
        w_lo = [ph.sb(f"w_lo{s}", [P, SLOT], F32R) for s in range(2)]
        ps = ph.banks()
        landed = [[ph.sem(f"landed{s}{q}") for q in range(2)] for s in range(2)]
        first = first and first(ph, ps[:, 7:8])
        rounded, split, used, full, taken = (ph.sem(s) for s in ("rounded", "split", "used", "full", "taken"))
        jobs = make_jobs(ph, ps)
        block = ph.enter_context(nc.Block())
        unit0, group0, land0 = [], [], []
        u = g = 0
        at = [[0, 0], [0, 0]]
        for job in jobs:
            unit0.append(u)
            group0.append(g)
            land0.append([list(x) for x in at])
            for r in range(job.groups * job.parts):
                for q in range(2):
                    at[(u + r) % 2][q] += 16 * job.loads[q]
            u += job.groups * job.parts
            g += job.groups

        def place(j, i, k, c):
            job = jobs[j]
            r = k * job.parts + c
            slot = (unit0[j] + r) % 2
            return slot, i * (2 * job.parts) + (unit0[j] + r), [
                i * (16 * job.loads[q] * job.parts) + (land0[j][slot][q] + 16 * job.loads[q] * (r // 2 + 1)) for q in range(2)]

        def bank(j, k):
            return 4 * ((group0[j] + k) % 2)

        @block.sync
        def _(sp):
            for j, job in enumerate(jobs):
                def body(i, k, j=j, job=job):
                    for c in range(job.parts):
                        slot, unit, _ = place(j, i, k, c)
                        sp.wait_ge(split, unit * 2 + 2)
                        sources = job.load(i * 2 + k, c)
                        assert len(sources) == sum(job.loads)
                        for q in range(2):
                            first = 0
                            for src in sources[:job.loads[0]] if q == 0 else sources[job.loads[0]:]:
                                width = src.shape[2]
                                sp.dma_start(job.view(raw[slot], q)[:, :, first:first + width], src).then_inc(landed[slot][q], 16)
                                first += width

                over_groups(sp, job.groups, body)

        def walk(eng, split_unit, empty, before, then):

            def split_group(j, i, k):
                for c in range(jobs[j].parts):
                    split_unit(j, i, k, c)

            if first:
                before(eng)
            split_group(0, 0, 0)
            if first:
                then(eng)
            for j, job in enumerate(jobs):
                looped = (job.groups - 1) // 2

                def pair(i, j=j):
                    split_group(j, i, 1)
                    empty(j, i, 0)
                    split_group(j, i + 1, 0)
                    empty(j, i, 1)

                if looped > 1:
                    with eng.Fori(0, looped) as i:
                        pair(i)
                elif looped:
                    pair(0)
                for g in range(2 * looped, job.groups):
                    if g + 1 < job.groups:
                        split_group(j, (g + 1) // 2, (g + 1) % 2)
                    elif j + 1 < len(jobs):
                        split_group(j + 1, 0, 0)
                    empty(j, g // 2, g % 2)

        @block.scalar
        def _(act):
            def round_unit(j, i, k, c):
                slot, unit, land = place(j, i, k, c)
                act.wait_ge(used, unit + 1)
                for q in range(2):
                    act.wait_ge(landed[slot][q], land[q])
                    act.activation(jobs[j].view(w_hi[slot], q), jobs[j].view(raw[slot], q), ACT.Copy).then_inc(rounded, 1)

            def empty(j, i, k):
                if jobs[j].act:
                    act.wait_ge(full, i * 2 + (group0[j] + k + 1))
                    jobs[j].act(act, i * 2 + k, bank(j, k), i * 2 + (k + 1))

            walk(act, round_unit, empty, first and first.roots, first and first.round_tiles)

        @block.vector
        def _(dve):
            dve.nop().then_inc(split, 4)
            dve.nop().then_inc(taken, 2)

            def rest_unit(j, i, k, c):
                slot, unit, _ = place(j, i, k, c)
                for q in range(2):
                    dve.wait_ge(rounded, unit * 2 + (q + 1))
                    dve.tensor_tensor(jobs[j].view(w_lo[slot], q), jobs[j].view(raw[slot], q), jobs[j].view(w_hi[slot], q).bitcast(F32),
                                      ALU.subtract).then_inc(split, 1)

            def empty(j, i, k):
                dve.wait_ge(full, i * 2 + (group0[j] + k + 1))
                dve.wait_ge(taken, i * 2 + (group0[j] + k + 2))
                jobs[j].dve(dve, i * 2 + k, bank(j, k), i * 2 + (k + 1)).then_inc(taken, 1)

            walk(dve, rest_unit, empty, first and first.scale, first and first.rest_tiles)

        @block.tensor
        def _(pe):
            pe.nop().then_inc(used, 2)
            if first:
                first.sum_up(pe)
            for j, job in enumerate(jobs):
                if job.after is not None:
                    pe.wait_ge(taken, 2 + group0[job.after] + jobs[job.after].groups)

                def body(i, k, j=j, job=job):
                    pe.wait_ge(taken, i * 2 + (group0[j] + k + 1))
                    for c in range(job.parts):
                        slot, unit, _ = place(j, i, k, c)
                        for f in range(job.nf):
                            q = int(f >= job.heads)
                            if f in (0, job.heads):
                                pe.wait_ge(split, unit * 2 + (q + 5))
                            hi, lo = job.view(w_hi[slot], q), job.view(w_lo[slot], q)
                            out = ps[:, bank(j, k) + f, 0:job.n]
                            for t in range(job.kt):
                                x_hi, x_lo = (x[:, c * job.kt + t, :] for x in (job.hi, job.lo))
                                if j == 0 and first and k == 0 and f == 0 and isinstance(i, int):
                                    pe.wait_ge(first.done, first.ready(t))
                                at = f - job.half(q).start
                                cols = slice(at * P, (at + 1) * P)
                                begin, end = c == 0 and t == 0, c == job.parts - 1 and t == job.kt - 1
                                pe.matmul(out, lo[:, t, cols], x_hi, start=begin, stop=False)
                                pe.matmul(out, hi[:, t, cols], x_lo, start=False, stop=False)
                                last = pe.matmul(out, hi[:, t, cols], x_hi, start=False, stop=end)
                        if c == job.parts - 1:
                            last.then_inc(full, 1)
                            pe.wait_ge(full, i * 2 + (group0[j] + k + 1))
                            pe.nop().then_inc(used, 1)
                        else:
                            last.then_inc(used, 1)

                over_groups(pe, job.groups, body, peel=j == 0 and bool(first))


def swiglu_buffers(ph, ft):
    return (ph.sb("hid_hi", [P, ft, T], F32R), ph.sb("hid_lo", [P, ft, T], F32R), ph.sb("s", [P, T]), ph.sb("h", [P, T]))


def swiglu_jobs(m, ph, ps, buffers, gate, up, down, ft, first):
    hid_hi, hid_lo, s, h = buffers
    silu_done, h_done, h_rounded = (ph.sem(n) for n in ("silu_done", "h_done", "h_rounded"))

    def load(g, c):
        return [k_major(gate)[:, :, bass.ds(g * P, P)], k_major(up)[:, :, bass.ds(g * P, P)]]

    def act(eng, g, b, n, src=None, func=ACT.Silu):
        eng.activation(s[:, :], ps[:, b, :] if src is None else src, func).then_inc(silu_done, 1)
        eng.wait_ge(h_done, n)
        eng.activation(hid_hi[:, bass.ds(g, 1), :], h[:, :], ACT.Copy).then_inc(h_rounded, 1)

    def dve(eng, g, b, n):
        eng.wait_ge(silu_done, n)
        eng.tensor_tensor(h[:, :], s[:, :], ps[:, b + 1, :], ALU.mult).then_inc(h_done, 1)
        eng.wait_ge(h_rounded, n)
        return eng.tensor_tensor(hid_lo[:, bass.ds(g, 1), :], h[:, :], hid_hi[:, bass.ds(g, 1), :].bitcast(F32), ALU.subtract)

    nf = 2

    def load_down(g, c):
        return two_loads(down.rearrange("(k p) n -> p k n", p=P), g * (nf * P), nf)

    def dve_down(eng, g, b, n):
        dst = m.xT[:, bass.ds(g * nf, nf), :]
        return eng.tensor_tensor(dst, dst, ps[:, b:b + nf, :], ALU.add)

    return [Job(ft, 2, load, m.act_hi, m.act_lo, dve, act),
            Job(DT // nf, nf, load_down, hid_hi, hid_lo, dve_down, kt=ft, after=first)]


def ffn_phase(m):
    gate, up, down = m.ins["ffn_gate"][0], m.ins["ffn_up"][0], m.ins["ffn_down"][0]
    half = 11

    def jobs(ph, ps):
        buffers, jobs = swiglu_buffers(ph, half), []
        for s in range(2):
            f = slice(s * half * P, (s + 1) * half * P)
            jobs += swiglu_jobs(m, ph, ps, buffers, gate[:, f], up[:, f], down[f, :], half, 2 * s)
        return jobs

    dense_phase(m, jobs, "ffn", norm_of(m, "norm2_0"))




def mask_buffers(m, persist):
    m.upto = persist.sb("upto", [P, P])
    m.before = persist.sb("before", [P, P])
    m.level = persist.sb("level", [P, 6, P])
    m.reset = persist.sb("reset", [P, T])
    m.head_rows = persist.sb("head_rows", [P, 3 * P])
    m.causal = persist.sb("causal", [P, P])


def make_masks(m, pool, done):
    n = 0

    def step(ins):
        nonlocal n
        n += 1
        ins.then_inc(done, 1)
        pool.wait_ge(done, n)

    def keep(view, base, pattern, mult, op=ALU.is_ge, fill=0.0):
        step(pool.affine_select(out=view, in_=view, compare_op=op, fill=fill, base=base, pattern=pattern,
                                channel_multiplier=mult))

    for mask, base in ((m.upto, 0), (m.before, -1)):
        step(pool.memset(mask[:, :], 0.0))
        for o in (0, CH):
            step(pool.memset(mask[o:o + CH, o:o + CH], 1.0))
            keep(mask[o:o + CH, o:o + CH], base, [[1, CH]], -1)
    for l in range(6):
        b = 1 << l
        blocks = P // (2 * b)
        mask = m.level[:, l, :]
        step(pool.memset(mask, 1.0))
        keep(mask, 0, [[-2 * b, blocks], [0, 2], [0, b]], 1)
        keep(mask, b - 1, [[2 * b, blocks], [0, 2], [0, b]], -1)
        step(pool.memset(mask.rearrange("p (j h b) -> p j h b", h=2, b=b)[:, :, 0, :], 0.0))
    step(pool.memset(m.reset[:, :], 1.0))
    step(pool.memset(m.reset[:, :].rearrange("p (c t) -> p c t", t=CH)[:, :, 0:1], 0.0))
    step(pool.memset(m.head_rows[:, :], 1.0))
    keep(m.head_rows[:, :], 0, [[1, 3 * P]], -HD)
    keep(m.head_rows[:, :], HD - 1, [[-1, 3 * P]], HD)
    step(pool.memset(m.causal[:, :], 0.0))
    keep(m.causal[:, :], 0, [[-1, P]], 1, fill=-1e30)




class Rule:
    pass


def chunk_phase(m, r):
    nc = m.nc
    H, pairs = r.heads, r.heads // 2
    L = 6
    with Phase(m, "chunk") as ph:
        nt = ph.sb("nt", [P, 2, TT, P])
        nb = ph.sb("nb", [P, 2, TT, P])
        x = ph.sb("x", [P, 2, TT, P])
        xt = ph.sb("xt", [P, 2, TT, P])
        p1 = ph.sb("p1", [P, 2, TT, P])
        if r.decayed:
            dec = ph.sb("dec", [P, 2, TT, P])
            own = ph.sb("own", [HD, 2, T])
        else:
            ak = ph.sb("ak", [P, 2, TT, P])
            qk = ph.sb("qk", [P, 2, TT, P])
            z = ph.sb("z", [P, 2, TT, HD])
        ps = ph.banks()
        own_ready, raw, low, low2, exped, formed, masked = (ph.sem(s) for s in ("own", "raw", "low", "low2", "exped", "formed", "masked"))
        p1_full, p1_kept, x_full, xt_full, x_new, xt_new = (
            ph.sem(s) for s in ("p1_full", "p1_kept", "x_full", "xt_full", "x_new", "xt_new"))
        z_full, z_kept, post_full, post_kept = (ph.sem(s) for s in ("z_full", "z_kept", "post_full", "post_kept"))
        block = ph.enter_context(nc.Block())
        heads = [(p, k, 2 * p + k, k * HD) for p in range(pairs) for k in range(2)]
        tile = lambda t: slice(t * P, (t + 1) * P)
        n_forms = 2 if r.decayed else 4
        n_post = 2 if r.decayed else 3
        four = lambda mask: mask[:, :].unsqueeze(1).to_broadcast([P, TT, P])

        def every(p, l, k):
            return (p * L + l) * 2 + k + 1

        def from_1(p, l, k):
            return (p * (L - 1) + (l - 1)) * 2 + k + 1

        def inner(p, l, k):
            return (p * (L - 2) + (l - 1)) * 2 + k + 1

        def to_last(p, l, k):
            return (p * (L - 1) + l) * 2 + k + 1

        @block.gpsimd
        def _(pool):
            for p in range(pairs):
                if r.decayed:
                    for k in range(2):
                        h = 2 * p + k
                        if p:
                            pool.wait_ge(raw, 3 * (h - 1))
                        pool.tensor_scalar(own[:, k, :], r.rhs_rows[0:HD, :], r.row_of_head[0:HD, h:h + 1], None,
                                           ALU.mult).then_inc(own_ready, 1)
                for l in range(L):
                    for k in range(2):
                        s = (p * L + l) * 2 + k
                        pool.wait_ge(formed, n_forms * (2 * p + k + 1))
                        if s >= 2:
                            pool.wait_ge(p1_full, s - 1)
                        if l == 1:
                            pool.wait_ge(xt_new, every(p, 0, k))
                        pool.tensor_tensor(nb[:, k], nt[:, k], four(m.level[:, l, :]), ALU.mult).then_inc(masked, 1)

        @block.tensor
        def _(pe):
            for p in range(pairs):
                for k in range(2):
                    h, o, b = 2 * p + k, k * HD, 4 * k
                    if p:
                        pe.wait_ge(post_kept, n_post * (h - 1))
                    rows = slice(o, o + HD)
                    if r.decayed:
                        pe.wait_ge(own_ready, h + 1)
                        products = [(b, None, None), (b + 1, r.k_t, r.a_t), (b + 2, r.k_t, r.q_t)]
                    else:
                        products = [(b, r.k_t, r.a_t), (b + 1, r.b_t, r.a_t), (b + 2, r.b_t, r.q_t), (b + 3, r.k_t, r.q_t)]
                    for bank, lhs, rhs in products:
                        for t in range(TT):
                            if lhs is None:
                                last = pe.matmul(ps[:, bank, tile(t)], r.lhs_rows[0:HD, tile(t)], own[:, k, tile(t)],
                                                 start=True, stop=True)
                            else:
                                last = pe.matmul(ps[:, bank, tile(t)], lhs[rows, p, tile(t)], rhs[rows, p, tile(t)],
                                                 start=True, stop=True)
                        last.then_inc(raw, 1)
                for l in range(L):
                    for k in range(2):
                        pe.wait_ge(masked, every(p, l, k))
                        if l:
                            pe.wait_ge(x_new, to_last(p, l - 1, k))
                        for t in range(TT):
                            last = pe.matmul(ps[:, 4 * k, tile(t)], nb[:, k, t, :], x[:, k, t, :] if l else m.ident[:, :],
                                             start=True, stop=True)
                        last.then_inc(p1_full, 1)
                    if not l:
                        continue
                    for k in range(2):
                        pe.wait_ge(p1_kept, from_1(p, l, k))
                        pe.wait_ge(xt_new, every(p, l - 1, k))
                        if l < L - 1:
                            for t in range(TT):
                                last = pe.matmul(ps[:, 4 * k + 1, tile(t)], xt[:, k, t, :], p1[:, k, t, :], start=True, stop=True)
                            last.then_inc(x_full, 1)
                        for t in range(TT):
                            last = pe.matmul(ps[:, 4 * k + 2, tile(t)], p1[:, k, t, :], xt[:, k, t, :], start=True, stop=True)
                        last.then_inc(xt_full, 1)
                for k in range(2):
                    h, o, b = 2 * p + k, k * HD, 4 * k
                    cols = slice(p * P + o, p * P + o + HD)
                    if not r.decayed:
                        for t in range(TT):
                            last = pe.matmul(ps[:, b, t * HD:(t + 1) * HD], ak[:, k, t, :], r.v_tok[:, t, cols], start=True, stop=True)
                        last.then_inc(z_full, 1)
                        for t in range(TT):
                            last = pe.matmul(ps[o:o + HD, b + 3, tile(t)], r.v_tok[:, t, cols], qk[:, k, t, :], start=True, stop=True)
                        last.then_inc(post_full, 1)
                    pe.wait_ge(xt_new, every(p, L - 1, k))
                    for t in range(TT):
                        last = pe.matmul(ps[o:o + HD, b + 2, tile(t)], r.a_tok[:, t, cols], xt[:, k, t, :], start=True, stop=True)
                    last.then_inc(post_full, 1)
                    if not r.decayed:
                        pe.wait_ge(z_kept, h + 1)
                    for t in range(TT):
                        last = pe.matmul(ps[:, b + 1, t * HD:(t + 1) * HD], xt[:, k, t, :],
                                         r.z_tok[:, t, cols] if r.decayed else z[:, k, t, :], start=True, stop=True)
                    last.then_inc(post_full, 1)

        @block.scalar
        def _(act):
            for p in range(pairs):
                if r.decayed:
                    for k in range(2):
                        h = 2 * p + k
                        act.wait_ge(low, h + 1)
                        act.activation(dec[:, k], dec[:, k], ACT.Exp).then_inc(exped, 1)
                for l in range(1, L):
                    for k in range(2):
                        n = from_1(p, l, k)
                        act.wait_ge(p1_full, every(p, l, k))
                        if n > 2:
                            act.wait_ge(xt_full, n - 2)
                        act.activation(p1[:, k], ps[:, 4 * k, :].rearrange("p (t n) -> p t n", t=TT), ACT.Copy).then_inc(p1_kept, 1)

        @block.vector
        def _(dve):
            view = lambda b: ps[:, b, :].rearrange("p (t n) -> p t n", t=TT)
            for p in range(pairs):
                for k in range(2):
                    h, b = 2 * p + k, 4 * k
                    if p:
                        dve.wait_ge(masked, p * L * 2)
                        dve.wait_ge(post_kept, n_post * (h - 1))
                    if r.decayed:
                        dve.wait_ge(raw, 3 * h + 1)
                        dve.wait_ge(formed, n_forms * h) if h else None
                        dve.tensor_scalar(dec[:, k], view(b), 0.0, None, ALU.min).then_inc(low, 1)
                        dve.wait_ge(exped, h + 1)
                        dve.tensor_tensor(dec[:, k], dec[:, k], four(m.upto), ALU.mult).then_inc(low2, 1)
                        dve.wait_ge(low2, h + 1)
                        dve.wait_ge(raw, 3 * h + 3)
                        dve.tensor_tensor(nt[:, k], view(b + 1), dec[:, k], ALU.mult).then_inc(formed, 1)
                        dve.tensor_tensor(r.qb[:, h], view(b + 2), dec[:, k], ALU.mult).then_inc(formed, 1)
                    else:
                        for n, (dst, mask) in enumerate(((ak[:, k], m.before), (nt[:, k], m.before), (r.qb[:, h], m.upto),
                                                         (qk[:, k], m.upto))):
                            dve.wait_ge(raw, 4 * h + n + 1)
                            dve.tensor_tensor(dst, view(b + n), four(mask), ALU.mult).then_inc(formed, 1)
                for k in range(2):
                    dve.wait_ge(masked, every(p, 0, k))
                    dve.tensor_tensor(xt[:, k], four(m.ident), nb[:, k], ALU.add).then_inc(xt_new, 1)
                    dve.wait_ge(p1_full, every(p, 0, k))
                    dve.tensor_tensor(x[:, k], four(m.ident), view(4 * k), ALU.add).then_inc(x_new, 1)
                for l in range(1, L):
                    for k in range(2):
                        if l < L - 1:
                            dve.wait_ge(x_full, inner(p, l, k))
                            dve.wait_ge(x_new, to_last(p, l - 1, k))
                            dve.tensor_tensor(x[:, k], x[:, k], view(4 * k + 1), ALU.add).then_inc(x_new, 1)
                        dve.wait_ge(xt_full, from_1(p, l, k))
                        dve.wait_ge(xt_new, every(p, l - 1, k))
                        dve.tensor_tensor(xt[:, k], xt[:, k], view(4 * k + 2), ALU.add).then_inc(xt_new, 1)
                for k in range(2):
                    h, o, b = 2 * p + k, k * HD, 4 * k
                    cols = slice(p * P + o, p * P + o + HD)
                    n = n_post * h
                    if not r.decayed:
                        dve.wait_ge(z_full, h + 1)
                        dve.tensor_copy(z[:, k], ps[:, b, 0:TT * HD].rearrange("p (t n) -> p t n", t=TT)).then_inc(z_kept, 1)
                        dve.wait_ge(post_full, n + 1)
                        dve.tensor_copy(r.y_t[o:o + HD, p, :], ps[o:o + HD, b + 3, :]).then_inc(post_kept, 1)
                        n += 1
                    dve.wait_ge(post_full, n + 1)
                    dve.tensor_copy(r.w_t[o:o + HD, p, :], ps[o:o + HD, b + 2, :]).then_inc(post_kept, 1)
                    dve.wait_ge(post_full, n + 2)
                    dve.tensor_copy(r.tz_tok[:, :, cols], ps[:, b + 1, 0:TT * HD].rearrange("p (t n) -> p t n", t=TT)).then_inc(post_kept, 1)


def scan_phase(m, r):
    nc = m.nc
    H, pairs = r.heads, r.heads // 2
    with Phase(m, "scan") as ph:
        ps = ph.banks()
        u_full, u_new, s_full, s_dec, s_new = (ph.sem(s) for s in ("u_full", "u_new", "s_full", "s_dec", "s_new"))
        held = ph.sb("held", [P, pairs, HD])
        block = ph.enter_context(nc.Block())

        @block.tensor
        def _(pe):
            for c in range(NCH):
                t, o = c // 2, (c % 2) * CH
                b = 4 * (c % 2)
                if c:
                    pe.wait_ge(s_new, c + 1)
                    for k in range(2):
                        for p in range(pairs):
                            rows = slice(k * HD, (k + 1) * HD)
                            last = pe.matmul(ps[o:o + CH, b + k, p * HD:(p + 1) * HD], r.w_t[rows, p, c * CH:(c + 1) * CH],
                                             r.states[rows, c, p, :], start=True, stop=True)
                    last.then_inc(u_full, 1)
                if c == NCH - 1:
                    break
                if not r.decayed:
                    for k in range(2):
                        for p in range(pairs):
                            cols = slice(p * P + k * HD, p * P + (k + 1) * HD)
                            pe.matmul(ps[k * HD:(k + 1) * HD, b + 2, p * HD:(p + 1) * HD], r.kd_tok[o:o + CH, t, cols],
                                      r.v_tok[o:o + CH, t, cols], start=p == 0, stop=False, skip_group_check=True)
                pe.wait_ge(u_new, c + 1)
                for k in range(2):
                    for p in range(pairs):
                        cols = slice(p * P + k * HD, p * P + (k + 1) * HD)
                        last = pe.matmul(ps[k * HD:(k + 1) * HD, b + 2, p * HD:(p + 1) * HD], r.bd_tok[o:o + CH, t, cols],
                                         r.u_tok[o:o + CH, t, cols], start=r.decayed and p == 0, stop=p == pairs - 1,
                                         skip_group_check=True)
                last.then_inc(s_full, 1)

        @block.vector
        def _(dve):
            dve.memset(r.states[:, 0], 0.0).then_inc(s_new, 1)
            for c in range(NCH):
                t, o = c // 2, (c % 2) * CH
                b = 4 * (c % 2)
                pair_view = lambda ap: ap.rearrange("p (a k d) -> p k a d", k=2, d=HD)
                if c:
                    dve.wait_ge(u_full, c)
                    dve.tensor_tensor(pair_view(r.u_tok[o:o + CH, t, :]),
                                      ps[o:o + CH, b:b + 2, 0:pairs * HD].rearrange("p k (a d) -> p k a d", d=HD),
                                      pair_view(r.tz_tok[o:o + CH, t, :]), ALU.add).then_inc(u_new, 1)
                else:
                    dve.tensor_copy(r.u_tok[o:o + CH, t, :], r.tz_tok[o:o + CH, t, :]).then_inc(u_new, 1)
                if c == NCH - 1:
                    break
                dve.wait_ge(s_new, c + 1)
                dve.tensor_tensor(held[:, :, :], r.states[:, c], r.last[:, :, c:c + 1].to_broadcast([P, pairs, HD]),
                                  ALU.mult).then_inc(s_dec, 1)
                dve.wait_ge(s_dec, c + 1)
                dve.wait_ge(s_full, c + 1)
                dve.tensor_tensor(r.states[:, c + 1], held[:, :, :],
                                  ps[:, b + 2, 0:pairs * HD].rearrange("p (a d) -> p a d", d=HD), ALU.add).then_inc(s_new, 1)


def read_phase(m, r):
    nc = m.nc
    pairs = r.heads // 2
    with Phase(m, "read") as ph:
        ps = ph.banks()
        full, kept = ph.sem("full"), ph.sem("kept")
        block = ph.enter_context(nc.Block())

        @block.tensor
        def _(pe):
            for h in range(r.heads):
                p, k = h // 2, h % 2
                rows, cols = slice(k * HD, (k + 1) * HD), slice(p * P + k * HD, p * P + (k + 1) * HD)
                if h >= 8:
                    pe.wait_ge(kept, h - 7)
                for t in range(TT):
                    pe.matmul(ps[rows, h % 8, t * P:(t + 1) * P], r.u_tok[:, t, cols], r.qb[:, h, t, :], start=t == 0, stop=False,
                              skip_group_check=True)
                for c in range(1, NCH):
                    last = pe.matmul(ps[rows, h % 8, c * CH:(c + 1) * CH], r.states[rows, c, p, :],
                                     r.r_t[rows, p, c * CH:(c + 1) * CH], start=False, stop=c == NCH - 1, skip_group_check=True)
                last.then_inc(full, 1)

        @block.vector
        def _(dve):
            for h in range(r.heads):
                p, k = h // 2, h % 2
                rows = slice(k * HD, (k + 1) * HD)
                dve.wait_ge(full, h + 1)
                if r.decayed:
                    dve.tensor_copy(r.y_t[rows, p, :], ps[rows, h % 8, :]).then_inc(kept, 1)
                else:
                    dve.tensor_tensor(r.y_t[rows, p, :], r.y_t[rows, p, :], ps[rows, h % 8, :], ALU.add).then_inc(kept, 1)




def dn_conv_part(m, ph, ps, l, dn, cv):
    sq = ph.sb("sq", [P, 6, T])
    tap, conv, silu, squared, summed, root, scaled = (ph.sem(s) for s in ("tap", "conv", "silu", "squared", "summed", "root", "scaled"))

    def taps(dve):
        for w in range(3):
            for s in range(1, 4):
                for t in range(3 * w, 3 * w + 3):
                    if s == 1:
                        dve.wait_ge(tap, t + 1)
                    else:
                        dve.wait_ge(conv, 9 * w + 3 * (s - 2) + (t - 3 * w) + 1)
                    dve.scalar_tensor_tensor(out=cv[:, t, s:T], in0=dn[:, t, 0:T - s], scalar=col(m, f"dn_conv_{l}_{3 - s}", t),
                                             in1=cv[:, t, s:T], op0=ALU.mult, op1=ALU.add).then_inc(conv, 1)

    def vector(dve):
        dve.wait_ge(root, 2)
        for t in range(6):
            dve.scalar_tensor_tensor(out=cv[:, t, :], in0=cv[:, t, :], scalar=HD ** -0.5 if t < 3 else 1.0, in1=sq[:, t, :],
                                     op0=ALU.mult, op1=ALU.mult).then_inc(scaled, 1)

    def first_tap(act):
        for t in range(9):
            act.activation(cv[:, t, :], dn[:, t, :], ACT.Identity, scale=col(m, f"dn_conv_{l}_3", t)).then_inc(tap, 1)

    def scalar(act):
        for t in range(9):
            act.wait_ge(conv, 9 * (t // 3) + 6 + t % 3 + 1)
            act.activation(cv[:, t, :], cv[:, t, :], ACT.Silu).then_inc(silu, 1)
        for t in range(6):
            act.wait_ge(silu, t + 1)
            act.activation(sq[:, t, :], cv[:, t, :], ACT.Square).then_inc(squared, 1)
        act.wait_ge(summed, 6)
        act.activation(sq[:, :, :], ps[:, 0:6, :], ACT.Ln, bias=m.eps[:, 0:1]).then_inc(root, 1)
        act.wait_ge(root, 1)
        act.activation(sq[:, :, :], sq[:, :, :], ACT.Exp, scale=-0.5).then_inc(root, 1)

    def tensor(pe):
        for t in range(6):
            pe.wait_ge(squared, t + 1)
            pe.matmul(ps[:, t, :], m.pair_ones[:, :], sq[:, t, :], start=True, stop=True).then_inc(summed, 1)

    return Part(first_tap=first_tap, taps=taps, scalar=scalar, tensor=tensor, vector=vector, root=root)


def dn_gates_part(m, ph, l, ab, small, r):
    R = slice(0, 6)
    e = ph.sb("e", [P, T])
    t2 = ph.sb("t2", [P, T])
    g = ph.sb("g", [P, T])
    ea = ph.sb("ea", [P, 1])
    bt = ph.sb("bt", [P, T])
    a_done, v_done, rows_done = ph.sem("a_done"), ph.sem("v_done"), ph.sem("rows_done")

    def start(act):
        act.activation(e[R, :], ab[R, 0, :], ACT.Abs, bias=col(m, f"dt_bias_{l}")[R]).then_inc(a_done, 1)
        act.wait_ge(a_done, 1)
        act.activation(e[R, :], e[R, :], ACT.Exp, scale=-1.0).then_inc(a_done, 1)
        act.activation(ea[R, :], col(m, f"a_log_{l}")[R], ACT.Exp).then_inc(a_done, 1)
        act.wait_ge(a_done, 3)
        act.activation(e[R, :], e[R, :], ACT.Ln, bias=m.ones[R, 0:1]).then_inc(a_done, 1)
        act.activation(bt[R, :], ab[R, 1, :], ACT.Tanh, scale=0.5).then_inc(a_done, 1)

    def scalar(act):
        act.wait_ge(a_done, 5)
        act.wait_ge(v_done, 4)
        act.activation(small[R, 1, :], g[R, :], ACT.Exp).then_inc(a_done, 1)
        act.wait_ge(v_done, 5)
        act.activation(small[R, 2, :], t2[R, :], ACT.Exp).then_inc(a_done, 1)

    def vector(dve):
        dve.tensor_scalar(t2[R, :], ab[R, 0, :], col(m, f"dt_bias_{l}")[R], 0.0, ALU.add, ALU.max).then_inc(v_done, 1)
        dve.wait_ge(v_done, 1)
        dve.wait_ge(a_done, 4)
        dve.tensor_tensor(t2[R, :], t2[R, :], e[R, :], ALU.add).then_inc(v_done, 1)
        dve.wait_ge(v_done, 2)
        dve.tensor_scalar(t2[R, :], t2[R, :], ea[R, :], -1.0, ALU.mult, ALU.mult).then_inc(v_done, 1)
        dve.wait_ge(v_done, 3)
        dve.tensor_tensor_scan(g[R, :], m.reset[R, :], t2[R, :], 0.0, ALU.mult, ALU.add).then_inc(v_done, 1)
        dve.wait_ge(v_done, 4)
        chunks = g[R, :].rearrange("p (c t) -> p c t", t=CH)
        dve.tensor_tensor(t2[R, :].rearrange("p (c t) -> p c t", t=CH), chunks[:, :, CH - 1:CH].to_broadcast([6, NCH, CH]),
                          chunks, ALU.subtract).then_inc(v_done, 1)
        dve.wait_ge(a_done, 5)
        dve.tensor_scalar(small[R, 0, :], bt[R, :], 0.5, 0.5, ALU.mult, ALU.add).then_inc(v_done, 1)
        dve.memset(r.lhs_rows[0:HD, :], 0.0).then_inc(rows_done, 1)
        dve.memset(r.rhs_rows[0:HD, :], 0.0).then_inc(rows_done, 1)
        dve.wait_ge(rows_done, 2)
        dve.memset(r.lhs_rows[R, :], 1.0).then_inc(rows_done, 1)
        dve.tensor_scalar(r.lhs_rows[32:38, :], g[R, :], -1.0, None, ALU.mult).then_inc(rows_done, 1)
        dve.tensor_copy(r.rhs_rows[R, :], g[R, :]).then_inc(rows_done, 1)
        dve.memset(r.rhs_rows[32:38, :], 1.0).then_inc(rows_done, 1)
        dve.tensor_copy(r.row_of_head[0:32, :], m.ident[0:32, 0:6]).then_inc(rows_done, 1)
        dve.tensor_copy(r.row_of_head[32:64, :], m.ident[32:64, 32:38]).then_inc(rows_done, 1)

    return Part(start=start, scalar=scalar, vector=vector)


def dn_expand_phase(m, cv, small, az, zb, kd, kb, qd, r):
    nc = m.nc
    with Phase(m, "dn_expand") as ph:
        ps = ph.banks()
        spread, made, turned, kept = (ph.sem(s) for s in ("spread", "made", "turned", "kept"))
        block = ph.enter_context(nc.Block())

        @block.tensor
        def _(pe):
            for p in range(3):
                if p == 2:
                    pe.wait_ge(made, 6)
                for q in range(3):
                    pe.matmul(ps[:, 3 * (p % 2) + q, :], m.head_rows[0:6, p * P:(p + 1) * P], small[0:6, q, :],
                              start=True, stop=True).then_inc(spread, 1)
            for n in range(9):
                p, src = n // 3, (az, zb, kd)[n % 3]
                pe.wait_ge(made, 6 * (p + 1))
                if n >= 2:
                    pe.wait_ge(kept, n - 1)
                for t in range(TT):
                    last = pe.transpose(ps[:, 6 + n % 2, t * P:(t + 1) * P], src[:, p, t * P:(t + 1) * P], m.ident[:, :])
                last.then_inc(turned, 1)

        @block.vector
        def _(dve):
            for p in range(3):
                b = 3 * (p % 2)
                dve.wait_ge(spread, 3 * p + 1)
                dve.scalar_tensor_tensor(out=kb[:, p, :], in0=cv[:, 3 + p, :], scalar=-1.0, in1=ps[:, b, :], op0=ALU.mult,
                                         op1=ALU.mult).then_inc(made, 1)
                dve.tensor_tensor(zb[:, p, :], cv[:, 6 + p, :], ps[:, b, :], ALU.mult).then_inc(made, 1)
                dve.wait_ge(spread, 3 * p + 2)
                dve.wait_ge(made, 6 * p + 2)
                dve.tensor_tensor(az[:, p, :], kb[:, p, :], ps[:, b + 1, :], ALU.mult).then_inc(made, 1)
                dve.tensor_tensor(qd[:, p, :], cv[:, p, :], ps[:, b + 1, :], ALU.mult).then_inc(made, 1)
                dve.tensor_copy(r.last[:, p, :], ps[:, b + 1, CH - 1:T:CH]).then_inc(made, 1)
                dve.wait_ge(spread, 3 * p + 3)
                dve.tensor_tensor(kd[:, p, :], cv[:, 3 + p, :], ps[:, b + 2, :], ALU.mult).then_inc(made, 1)

        @block.scalar
        def _(act):
            for n in range(9):
                p, dst = n // 3, (r.a_tok, r.z_tok, r.bd_tok)[n % 3]
                act.wait_ge(turned, n + 1)
                act.activation(dst[:, :, p * P:(p + 1) * P], ps[:, 6 + n % 2, :].rearrange("p (t n) -> p t n", t=TT),
                               ACT.Copy).then_inc(kept, 1)


def head_norm_part(m, ph, ps, jobs):
    n = sum(tiles for _, tiles, _, _, _ in jobs)
    assert n <= 8
    sq = ph.sb("sq", [P, n, T])
    squared, summed, root, scaled = (ph.sem(s) for s in ("squared", "summed", "root", "scaled"))
    tiles = [(x[:, t, :], out[:, t, :], c, f) for x, k, out, c, f in jobs for t in range(k)]

    def squares(act):
        for i, (x, _, _, _) in enumerate(tiles):
            act.activation(sq[:, i, :], x, ACT.Square).then_inc(squared, 1)

    def scalar(act):
        act.wait_ge(summed, n)
        act.activation(sq[:, :, :], ps[:, 0:n, :], ACT.Ln, bias=m.eps[:, 0:1], scale=1.0 / HD).then_inc(root, 1)
        act.wait_ge(root, 1)
        act.activation(sq[:, :, :], sq[:, :, :], ACT.Exp, scale=-0.5).then_inc(root, 1)

    def tensor(pe):
        for i in range(n):
            pe.wait_ge(squared, i + 1)
            pe.matmul(ps[:, i, :], m.pair_ones[:, :], sq[:, i, :], start=True, stop=True).then_inc(summed, 1)

    def vector(dve):
        dve.wait_ge(root, 2)
        for i, (x, out, c, f) in enumerate(tiles):
            if f != 1.0:
                dve.tensor_scalar(sq[:, i, :], sq[:, i, :], f, None, ALU.mult).then_inc(scaled, 1)
            else:
                dve.nop().then_inc(scaled, 1)
            dve.wait_ge(scaled, 2 * i + 1)
            dve.scalar_tensor_tensor(out=out, in0=x, scalar=col(m, c), in1=sq[:, i, :], op0=ALU.mult,
                                     op1=ALU.mult).then_inc(scaled, 1)

    return Part(squares=squares, scalar=scalar, tensor=tensor, vector=vector, root=root, scaled=scaled, steps=2 * n)


def gate_part(m, ph, y, z, tiles, hi, lo):
    times, rounded, rest = (ph.sem(s) for s in ("times", "rounded", "rest"))

    def scalar(act):
        for t in range(tiles):
            act.wait_ge(times, t + 1)
            act.activation(hi[:, t, :], y[:, t, :], ACT.Copy).then_inc(rounded, 1)

    def vector(dve):
        for t in range(tiles):
            dve.tensor_tensor(y[:, t, :], y[:, t, :], z[:, t, :], ALU.mult).then_inc(times, 1)
        for t in range(tiles):
            dve.wait_ge(rounded, t + 1)
            dve.tensor_tensor(lo[:, t, :], y[:, t, :], hi[:, t, :].bitcast(F32), ALU.subtract).then_inc(rest, 1)

    return Part(scalar=scalar, vector=vector)


def fx_rows_part(m, ph, l, f, r):
    R = slice(0, 6)
    e, t2, c = ph.sb("e", [P, T]), ph.sb("t2", [P, T]), ph.sb("c", [P, T])
    one = ph.sb("one", [P, T])
    a_done, v_done, rows_done = ph.sem("a_done"), ph.sem("v_done"), ph.sem("rows_done")

    def scalar(act):
        act.activation(e[R, :], f[R, 0, :], ACT.Abs, bias=col(m, f"f_bias_{l}")[R]).then_inc(a_done, 1)
        act.wait_ge(a_done, 1)
        act.activation(e[R, :], e[R, :], ACT.Exp, scale=-1.0).then_inc(a_done, 1)
        act.wait_ge(a_done, 2)
        act.activation(e[R, :], e[R, :], ACT.Ln, bias=m.ones[R, 0:1]).then_inc(a_done, 1)

    def vector(dve):
        dve.tensor_scalar(t2[R, :], f[R, 0, :], col(m, f"f_bias_{l}")[R], 0.0, ALU.add, ALU.min).then_inc(v_done, 1)
        dve.memset(one[R, :], 1.0).then_inc(v_done, 1)
        dve.wait_ge(v_done, 2)
        dve.wait_ge(a_done, 3)
        dve.tensor_tensor(t2[R, :], t2[R, :], e[R, :], ALU.subtract).then_inc(v_done, 1)
        dve.wait_ge(v_done, 3)
        dve.tensor_tensor_scan(c[R, :], one[R, :], t2[R, :], 0.0, ALU.mult, ALU.add).then_inc(v_done, 1)
        dve.memset(r.key_rows[:, :], 0.0).then_inc(rows_done, 1)
        dve.memset(r.query_rows[:, :], 0.0).then_inc(rows_done, 1)
        dve.wait_ge(rows_done, 2)
        dve.wait_ge(v_done, 4)
        for o in (0, HD):
            dve.tensor_scalar(r.key_rows[o:o + 6, :], c[R, :], -1.0, None, ALU.mult).then_inc(rows_done, 1)
            dve.memset(r.key_rows[o + 32:o + 38, :], 1.0).then_inc(rows_done, 1)
            dve.memset(r.query_rows[o:o + 6, :], 1.0).then_inc(rows_done, 1)
            dve.tensor_copy(r.query_rows[o + 32:o + 38, :], c[R, :]).then_inc(rows_done, 1)
        for o in range(0, P, 32):
            dve.tensor_copy(r.row_of_head[o:o + 32, :], m.ident[o:o + 32, o:o + 6]).then_inc(rows_done, 1)

    return Part(scalar=scalar, vector=vector)


def turn_part(m, ph, ps, pairs, n=T, banks=8):
    nt = n // P
    tiles = [(src, dst, tile) for src, dst, k in pairs for tile in range(k)]
    turned, kept = ph.sem("turned"), ph.sem("kept")

    def tensor(pe):
        for k, (src, _, tile) in enumerate(tiles):
            if k >= banks:
                pe.wait_ge(kept, k - banks + 1)
            for t in range(nt):
                last = pe.transpose(ps[:, k % banks, t * P:(t + 1) * P], src[:, tile, t * P:(t + 1) * P], m.ident[:, :])
            last.then_inc(turned, 1)

    def vector(dve):
        for k, (_, dst, tile) in enumerate(tiles):
            dve.wait_ge(turned, k + 1)
            dve.tensor_copy(dst[:, :, tile * P:(tile + 1) * P],
                            ps[:, k % banks, 0:n].rearrange("p (t n) -> p t n", t=nt)).then_inc(kept, 1)

    return Part(tensor=tensor, vector=vector)


def turn_phase(m, pairs, n=T):
    with Phase(m, "turn") as ph:
        turn = turn_part(m, ph, ph.banks(), pairs, n)
        block = ph.enter_context(m.nc.Block())

        @block.tensor
        def _(pe):
            turn.tensor(pe)

        @block.vector
        def _(dve):
            turn.vector(dve)


def fx_attention_phase(m, q, k, v_tok, r, o_t, make_gate):
    nc = m.nc
    H = 6
    with Phase(m, "fx") as ph:
        own = ph.sb("own", [P, 2, T])
        prob = ph.sb("prob", [P, 2, TT, T])
        prob_t = ph.sb("prob_t", [P, 2, TT, T])
        top, total = ph.sb("top", [P, 2, TT]), ph.sb("total", [P, 2, TT])
        ps = ph.banks()
        own_ready, scored, masked, topped, exped, inverse, normed, turned, kept, out_full, out_kept = (
            ph.sem(s) for s in ("own", "scored", "masked", "topped", "exped", "inverse", "normed", "turned", "kept",
                                "out_full", "out_kept"))
        block = ph.enter_context(nc.Block())
        gate = make_gate(ph)

        @block.gpsimd
        def _(pool):
            for h in range(H):
                o = (h % 2) * HD
                if h >= 2:
                    pool.wait_ge(scored, TT * (h - 1))
                pool.tensor_scalar(own[o:o + HD, h % 2, :], r.query_rows[o:o + HD, :], r.row_of_head[o:o + HD, h:h + 1], None,
                                   ALU.mult).then_inc(own_ready, 1)

        def scores(pe, h):
            p, o = h // 2, (h % 2) * HD
            rows = slice(o, o + HD)
            pe.wait_ge(own_ready, h + 1)
            for i in range(TT):
                if h:
                    pe.wait_ge(exped, TT * (h - 1) + i + 1)
                n = (i + 1) * P
                pe.matmul(ps[:, i, 0:n], q[rows, p, i * P:(i + 1) * P], k[rows, p, 0:n], start=True, stop=False)
                pe.matmul(ps[:, i, 0:n], own[rows, h % 2, i * P:(i + 1) * P], r.key_rows[rows, 0:n],
                          start=False, stop=True).then_inc(scored, 1)

        @block.tensor
        def _(pe):
            scores(pe, 0)
            for h in range(H):
                p, o = h // 2, (h % 2) * HD
                if h + 1 < H:
                    scores(pe, h + 1)
                for j in range(TT):
                    pe.wait_ge(normed, TT * (h + 1))
                    s = TT * h + j
                    if s >= 2:
                        pe.wait_ge(kept, s - 1)
                    for i in range(j, TT):
                        last = pe.transpose(ps[:, 4 + s % 2, i * P:(i + 1) * P], prob[:, h % 2, i, j * P:(j + 1) * P], m.ident[:, :])
                    last.then_inc(turned, 1)
                if h >= 2:
                    pe.wait_ge(out_kept, h - 1)
                for j in range(TT):
                    pe.wait_ge(kept, TT * h + j + 1)
                    last = pe.matmul(ps[o:o + HD, 6 + h % 2, j * P:T], v_tok[:, j, h * HD:(h + 1) * HD], prob_t[:, h % 2, j, j * P:T],
                                     start=j == 0, stop=j == TT - 1, skip_group_check=True)
                last.then_inc(out_full, 1)

        @block.vector
        def _(dve):
            def after(h):
                for i in range(TT):
                    n = TT * h + i
                    dve.wait_ge(exped, n + 1)
                    dve.reciprocal(total[:, h % 2, i:i + 1], total[:, h % 2, i:i + 1]).then_inc(inverse, 1)
                    dve.wait_ge(inverse, n + 1)
                    w = (i + 1) * P
                    dve.tensor_scalar(prob[:, h % 2, i, 0:w], prob[:, h % 2, i, 0:w], total[:, h % 2, i:i + 1], None,
                                      ALU.mult).then_inc(normed, 1)

            def finish(h):
                o = (h % 2) * HD
                dve.wait_ge(out_full, h + 1)
                dve.tensor_copy(o_t[o:o + HD, h // 2, :], ps[o:o + HD, 6 + h % 2, :]).then_inc(out_kept, 1)

            for h in range(H):
                for i in range(TT):
                    n = TT * h + i
                    dve.wait_ge(scored, n + 1)
                    last = ps[:, i, i * P:(i + 1) * P]
                    dve.tensor_tensor(last, last, m.causal[:, :], ALU.add).then_inc(masked, 1)
                    dve.wait_ge(masked, n + 1)
                    if n >= 2 * TT:
                        dve.wait_ge(exped, n - 2 * TT + 1)
                    dve.tensor_reduce(top[:, h % 2, i:i + 1], ps[:, i, 0:(i + 1) * P], AX.X, ALU.max, negate=True).then_inc(topped, 1)
                after(h)
                if h:
                    finish(h - 1)
            gate.vector(dve)
            finish(H - 1)

        @block.scalar
        def _(act):
            for h in range(H):
                for i in range(TT):
                    n = TT * h + i
                    act.wait_ge(topped, n + 1)
                    if h >= 2:
                        act.wait_ge(turned, TT * (h - 1))
                        act.wait_ge(normed, TT * (h - 1))
                    w = (i + 1) * P
                    act.activation(prob[:, h % 2, i, 0:w], ps[:, i, 0:w], ACT.Exp, bias=top[:, h % 2, i:i + 1],
                                   accum_out=total[:, h % 2, i:i + 1]).then_inc(exped, 1)
                for j in range(TT):
                    s = TT * h + j
                    act.wait_ge(turned, s + 1)
                    if h >= 2:
                        act.wait_ge(out_full, h - 1)
                    act.activation(prob_t[:, h % 2, j, j * P:T], ps[:, 4 + s % 2, j * P:T], ACT.Copy).then_inc(kept, 1)
            gate.scalar(act)


def pool_part(m, ph, ps, l, xp):
    w = ph.sb("w", [P, 2, HD])
    inv = ph.sb("inv", [P, 2, T])
    s1, s2 = ph.sb("s1", [P, 2, T]), ph.sb("s2", [P, 2, T])
    landed, inv_done, summed, full, kept = (ph.sem(s) for s in ("landed", "inv_done", "summed", "full", "kept"))
    groups = [(g // 2, (g % 2) * HD, 2 << g) for g in range(4)]

    def sync(sp):
        sp.dma_start(w[:, :, :], m.ins["pool_w"][l].rearrange("(j k) c d -> (k c) j d", k=2)).then_inc(landed, 16)

    def gpsimd(pool):
        n = 0
        for j, o, win in groups:
            pool.memset(inv[o:o + HD, j, :], 1.0 / win).then_inc(inv_done, 1)
            n += 1
            pool.wait_ge(inv_done, n)
            for t in range(win - 1):
                pool.memset(inv[o:o + HD, j, t:t + 1], 1.0 / (t + 1)).then_inc(inv_done, 1)
                n += 1

    n_inv = sum(win for _, _, win in groups)
    steps = sum(2 * (2 * j + 2) + 4 for j in range(2))

    def sums(dve):
        n = 0

        def step(ins):
            nonlocal n
            n += 1
            ins.then_inc(summed, 1)
            dve.wait_ge(summed, n)

        for j in range(2):
            src, into, other = xp, s1, s2
            for k in range(2 * j + 2):
                d = 1 << k
                rows = slice(0, P) if k < 2 * j + 1 else slice(HD, P)
                step(dve.tensor_copy(into[rows, j, 0:d], src[rows, j, 0:d]))
                step(dve.tensor_tensor(into[rows, j, d:T], src[rows, j, d:T], src[rows, j, 0:T - d], ALU.add))
                src, into, other = into, other, into
            if j == 0:
                dve.wait_ge(inv_done, n_inv)
            for rows, total in ((slice(0, HD), into), (slice(HD, P), src)):
                step(dve.tensor_tensor(total[rows, j, :], total[rows, j, :], inv[rows, j, :], ALU.mult))
                step(dve.tensor_tensor(xp[rows, j, :], total[rows, j, :], xp[rows, j, :], ALU.subtract))
        assert n == steps

    def vector(dve):
        for j in range(2):
            for k in range(2):
                dve.wait_ge(full, 2 * j + k + 1)
                rows = slice(k * HD, (k + 1) * HD)
                dve.tensor_scalar(xp[rows, j, :], ps[rows, 2 * j + k, :], col(m, f"pool_scale_{l}", j)[rows], None,
                                  ALU.mult).then_inc(kept, 1)

    def tensor(pe):
        pe.wait_ge(landed, 16)
        pe.wait_ge(summed, steps)
        for j, o, _ in groups:
            pe.matmul(ps[o:o + HD, 2 * j + o // HD, :], w[o:o + HD, j, :], xp[o:o + HD, j, :], start=True, stop=True).then_inc(full, 1)

    return Part(sync=sync, gpsimd=gpsimd, sums=sums, vector=vector, tensor=tensor)


def plain_job(m, w, first, groups, nf, dst, hi=None, lo=None, **more):
    def load(g, c):
        return two_loads(k_major(w), g * (nf * P) + first, nf)

    def dve(eng, g, b, n):
        size = more.get("n", T)
        return eng.tensor_copy(dst[:, bass.ds(g * nf, nf), :], more["ps"][:, b:b + nf, 0:size])

    return Job(groups, nf, load, hi if hi is not None else m.act_hi, lo if lo is not None else m.act_lo, dve, n=more.get("n", T))


def add_job(m, w, ps, nf=2):
    def load(g, c):
        return two_loads(k_major(w), g * (nf * P), nf)

    def dve(eng, g, b, n):
        dst = m.xT[:, bass.ds(g * nf, nf), :]
        return eng.tensor_tensor(dst, dst, ps[:, b:b + nf, :], ALU.add)

    return Job(DT // nf, nf, load, m.act_hi, m.act_lo, dve)


def dn_and_fx_start_phase(m, l, dn, cv, ab, small, r, q, k, xp):
    with Phase(m, "start") as ph:
        ps = ph.banks()
        conv = dn_conv_part(m, ph, ps, l, dn, cv)
        gates = dn_gates_part(m, ph, l, ab, small, r)
        norm = head_norm_part(m, ph, ps, [(q, 3, q, f"fx_qnorm_{l}", HD ** -0.5), (k, 3, k, f"fx_knorm_{l}", 1.0)])
        means = pool_part(m, ph, ps, l, xp)
        block = ph.enter_context(m.nc.Block())

        @block.sync
        def _(sp):
            means.sync(sp)

        @block.gpsimd
        def _(pool):
            means.gpsimd(pool)

        @block.scalar
        def _(act):
            conv.first_tap(act)
            norm.squares(act)
            gates.start(act)
            conv.scalar(act)
            norm.scalar(act)
            gates.scalar(act)

        @block.tensor
        def _(pe):
            conv.tensor(pe)
            pe.wait_ge(conv.root, 1)
            norm.tensor(pe)
            pe.wait_ge(norm.root, 1)
            means.tensor(pe)

        @block.vector
        def _(dve):
            conv.taps(dve)
            gates.vector(dve)
            means.sums(dve)
            conv.vector(dve)
            norm.vector(dve)
            means.vector(dve)


def dn_norm_and_fx_rows_phase(m, l, y, z, f, v, v_tok, r):
    with Phase(m, "between") as ph:
        ps = ph.banks()
        norm = head_norm_part(m, ph, ps, [(y, 3, y, f"dn_onorm_{l}", 1.0)])
        rows = fx_rows_part(m, ph, l, f, r)
        turn = turn_part(m, ph, ps[:, 3:6], [(v, v_tok, 3)], banks=3)
        gated = ph.sem("gated")
        block = ph.enter_context(m.nc.Block())

        @block.scalar
        def _(act):
            norm.squares(act)
            rows.scalar(act)
            norm.scalar(act)
            act.activation(z[:, :, :], z[:, :, :], ACT.Silu).then_inc(gated, 1)

        @block.tensor
        def _(pe):
            norm.tensor(pe)
            turn.tensor(pe)

        @block.vector
        def _(dve):
            turn.vector(dve)
            rows.vector(dve)
            norm.vector(dve)


def mixer(m, l):
    w = m.ins["w_in"][l]
    with Phase(m, "mix") as mix:
        dn = mix.sb("dn", [P, 12, T])
        fxp = mix.sb("fxp", [P, 9, T])
        xp = mix.sb("xp", [P, 2, T])
        fab = mix.sb("fab", [P, 4, T])

        def jobs(ph, ps):
            q, z = plain_job(m, w, 0, 4, 3, dn, ps=ps), plain_job(m, w, 1548, 3, 3, fxp, ps=ps)

            def load_ab(g, c):
                return [k_major(w)[:, :, c:c + P] for c in (2700, 1536, 1542)]

            def dve_ab(eng, g, b, n):
                return eng.tensor_copy(fab[:, 0:3, :], ps[:, b:b + 3, :])

            ab = Job(1, 3, load_ab, m.act_hi, m.act_lo, dve_ab, loads=(1, 2))
            return [q, z, ab, plain_job(m, w, 2706, 1, 2, xp, ps=ps)]

        dense_phase(m, jobs, "proj", norm_of(m, f"norm1_{l}"))
        r = Rule()
        r.heads, r.decayed = 6, True
        y, small = dn[:, 3:6], fab[:, 1:4]
        with Phase(m, "dn") as s:
            cv = s.sb("cv", [P, 9, T])
            kb = s.sb("kb", [P, 3, T])
            qd = cv[:, 6:9]
            r.lhs_rows, r.rhs_rows = s.sb("lhs_rows", [P, T]), s.sb("rhs_rows", [P, T])
            r.row_of_head = s.sb("row_of_head", [P, 6])
            dn_and_fx_start_phase(m, l, dn, cv, fab[:, 1:3], small, r, fxp[:, 0:3], fxp[:, 3:6], xp)
            r.qb = s.sb("qb", [P, 6, TT, P])
            r.a_tok, r.z_tok, r.bd_tok = (s.sb(n, [P, TT, 3 * P]) for n in ("a_tok", "z_tok", "bd_tok"))
            r.tz_tok, r.u_tok = r.z_tok, r.a_tok
            r.last = s.sb("last", [P, 3, NCH])
            dn_expand_phase(m, cv, small, dn[:, 0:3], dn[:, 3:6], dn[:, 6:9], kb, qd, r)
            r.k_t, r.a_t, r.q_t = cv[:, 3:6], kb, cv[:, 0:3]
            r.w_t, r.r_t, r.y_t = dn[:, 0:3], qd, y
            chunk_phase(m, r)
            r.states = s.sb("states", [P, NCH, 3, HD])
            scan_phase(m, r)
            read_phase(m, r)
        with Phase(m, "fxs") as s:
            o = s.sb("o", [P, 3, T])
            with Phase(m, "fxr") as s2:
                r = Rule()
                r.key_rows, r.query_rows = s2.sb("key_rows", [P, T]), s2.sb("query_rows", [P, T])
                r.row_of_head = s2.sb("row_of_head", [P, 6])
                v_tok = s2.sb("v_tok", [P, TT, 3 * P])
                dn_norm_and_fx_rows_phase(m, l, y, dn[:, 9:12], fab[:, 0:1], fxp[:, 6:9], v_tok, r)
                fx_attention_phase(m, fxp[:, 0:3], fxp[:, 3:6], v_tok, r, o,
                                   lambda ph: gate_part(m, ph, y, dn[:, 9:12], 3, m.act_hi[:, 0:3], m.act_lo[:, 0:3]))
            tiles = [o[:, t, :] for t in range(3)] + [xp[:, t, :] for t in range(2)]
            dense_phase(m, lambda ph, ps: [add_job(m, m.ins["w_out"][l], ps)], "w_out",
                        lambda ph, ps: Split(ph, tiles, m.act_hi[:, 3:8], m.act_lo[:, 3:8]))



EXPERTS = 8


def router_phase(m, prob, chosen, h, x_tok):
    nc = m.nc
    E = EXPERTS
    with Phase(m, "router") as ph:
        w = ph.sb("w", [P, DT, E])
        w_hi, w_lo = ph.sb("w_hi", [P, DT, E], F32R), ph.sb("w_lo", [P, DT, E], F32R)
        logits = ph.sb("logits", [P, TT, E])
        top = ph.sb("top", [P, TT])
        above, ties, lower = (ph.sb(n, [P, TT, E, E]) for n in ("above", "ties", "lower"))
        ps = ph.banks()
        landed, lower_done, parts, full, centred, exped, v_done, turned, kept = (
            ph.sem(s) for s in ("landed", "lower_done", "parts", "full", "centred", "exped", "v_done", "turned", "kept"))
        block = ph.enter_context(nc.Block())

        @block.sync
        def _(sp):
            sp.dma_start(w[:, :, :], k_major(m.ins["router"][0])).then_inc(landed, 16)

        @block.gpsimd
        def _(pool):
            pool.memset(lower[:, :, :, :], 1.0).then_inc(lower_done, 1)
            pool.wait_ge(lower_done, 1)
            pool.affine_select(out=lower[:, :, :, :], in_=lower[:, :, :, :], compare_op=ALU.is_ge, fill=0.0, base=-1,
                               pattern=[[0, TT], [1, E], [-1, E]], channel_multiplier=0).then_inc(lower_done, 1)

        @block.scalar
        def _(act):
            act.wait_ge(landed, 16)
            act.activation(w_hi[:, :, :], w[:, :, :], ACT.Copy).then_inc(parts, 1)

            def keep(tiles):
                for k in tiles:
                    act.wait_ge(turned, k + 1)
                    act.activation(x_tok[:, :, k * P:(k + 1) * P], ps[:, 4 + k % 4, :].rearrange("p (t n) -> p t n", t=TT),
                                   ACT.Copy).then_inc(kept, 1)

            keep(range(0, 4))
            act.wait_ge(centred, 1)
            act.activation(prob[:, :, :], prob[:, :, :], ACT.Exp).then_inc(exped, 1)
            keep(range(4, DT))

        @block.tensor
        def _(pe):
            def turn(tiles):
                for k in tiles:
                    if k >= 4:
                        pe.wait_ge(kept, k - 3)
                    for t in range(TT):
                        last = pe.transpose(ps[:, 4 + k % 4, t * P:(t + 1) * P], h[:, k, t * P:(t + 1) * P], m.ident[:, :])
                    last.then_inc(turned, 1)

            turn(range(0, 4))
            pe.wait_ge(parts, 2)
            for t in range(TT):
                cols = slice(t * P, (t + 1) * P)
                out = ps[:, t, 0:E]
                for k in range(DT):
                    pe.matmul(out, m.act_lo[:, k, cols], w_hi[:, k, :], start=k == 0, stop=False)
                    pe.matmul(out, m.act_hi[:, k, cols], w_lo[:, k, :], start=False, stop=False)
                    last = pe.matmul(out, m.act_hi[:, k, cols], w_hi[:, k, :], start=False, stop=k == DT - 1)
            last.then_inc(full, 1)
            turn(range(4, DT))

        @block.vector
        def _(dve):
            n = 0

            def step(ins):
                nonlocal n
                n += 1
                ins.then_inc(v_done, 1)
                dve.wait_ge(v_done, n)

            dve.wait_ge(parts, 1)
            dve.tensor_tensor(w_lo[:, :, :], w[:, :, :], w_hi[:, :, :].bitcast(F32), ALU.subtract).then_inc(parts, 1)
            dve.wait_ge(full, 1)
            step(dve.tensor_copy(logits[:, :, :], ps[:, 0:TT, 0:E]))
            step(dve.tensor_reduce(top[:, :], logits[:, :, :], AX.X, ALU.max))
            dve.tensor_tensor(prob[:, :, :], logits[:, :, :], top[:, :].unsqueeze(2).to_broadcast([P, TT, E]),
                              ALU.subtract).then_inc(centred, 1)
            for t in range(TT):
                own = logits[:, t, :].unsqueeze(2).to_broadcast([P, E, E])
                other = logits[:, t, :].unsqueeze(1).to_broadcast([P, E, E])
                step(dve.tensor_tensor(above[:, t], other, own, ALU.is_gt))
                step(dve.tensor_tensor(ties[:, t], other, own, ALU.is_equal))
            dve.wait_ge(lower_done, 2)
            step(dve.tensor_tensor(ties[:, :, :, :], ties[:, :, :, :], lower[:, :, :, :], ALU.mult))
            step(dve.tensor_tensor(above[:, :, :, :], above[:, :, :, :], ties[:, :, :, :], ALU.add))
            step(dve.tensor_reduce(chosen[:, :, :], above[:, :, :, :], AX.X, ALU.add))
            step(dve.tensor_scalar(chosen[:, :, :], chosen[:, :, :], 2.0, None, ALU.is_lt))
            dve.wait_ge(exped, 1)
            step(dve.tensor_tensor(prob[:, :, :], prob[:, :, :], chosen[:, :, :], ALU.mult))
            step(dve.tensor_reduce(top[:, :], prob[:, :, :], AX.X, ALU.add))
            step(dve.reciprocal(top[:, :], top[:, :]))
            step(dve.tensor_tensor(prob[:, :, :], prob[:, :, :], top[:, :].unsqueeze(2).to_broadcast([P, TT, E]), ALU.mult))


ITEMS = (2 * T + EXPERTS * (P - 1)) // P
ITEM_COLS = 16


def items_phase(m, prob, chosen, place, weight, table, slots):
    nc = m.nc
    E, N = EXPERTS, ITEM_COLS
    assert ITEMS <= N
    with Phase(m, "items") as ph:
        ints = ph.sb("ints", [P, P], mybir.dt.int32)
        rows_i, first_i = ph.sb("rows_i", [P, N], mybir.dt.int32), ph.sb("first_i", [P, 1], mybir.dt.int32)
        item, expert = ph.sb("item", [P, N]), ph.sb("expert", [P, 1])
        chosen_t, prob_t, run, one = (ph.sb(n, [P, T]) for n in ("chosen_t", "prob_t", "run", "one"))
        tiles, more, begin, end = (ph.sb(n, [P, 1]) for n in ("tiles", "more", "begin", "end"))
        mine, before, shift = (ph.sb(n, [P, N]) for n in ("mine", "before", "shift"))
        ps = ph.banks()
        counted, turned, v_done, ended, made = (ph.sem(s) for s in ("counted", "turned", "v_done", "ended", "made"))
        block = ph.enter_context(nc.Block())

        ENDS = 8 + 2 * (TT - 1) + 1

        @block.gpsimd
        def _(pool):
            pool.iota(ints[:, :], [[1, P]], base=1, channel_multiplier=0).then_inc(counted, 1)
            pool.iota(rows_i[:, :], [[1, N]], base=0, channel_multiplier=0).then_inc(counted, 1)
            pool.iota(first_i[:, :], [[0, 1]], base=0, channel_multiplier=1).then_inc(counted, 1)

        @block.tensor
        def _(pe):
            for b, src in enumerate((chosen, prob)):
                for t in range(TT):
                    last = pe.transpose(ps[0:E, b, t * P:(t + 1) * P], src[:, t, :], m.ident[:, :])
                last.then_inc(turned, 1)
            pe.wait_ge(v_done, ENDS)
            pe.matmul(ps[0:E, 2, 0:1], m.upto[0:E, 0:E], tiles[0:E, :], start=True, stop=True).then_inc(ended, 1)
            pe.wait_ge(v_done, ENDS + 7)
            for t in range(TT):
                cols = slice(t * P, (t + 1) * P)
                pe.matmul(ps[:, 3, t * N:(t + 1) * N], run[0:E, cols], mine[0:E, :], start=True, stop=False)
                pe.matmul(ps[:, 3, t * N:(t + 1) * N], m.ones[0:E, :], shift[0:E, :], start=False, stop=True)
            for t in range(TT):
                last = pe.matmul(ps[:, 4, t * N:(t + 1) * N], prob_t[0:E, t * P:(t + 1) * P], mine[0:E, :], start=True, stop=True)
            last.then_inc(made, 1)
            pe.matmul(ps[0:1, 5, 0:N], expert[0:E, :], mine[0:E, :], start=True, stop=True)
            pe.matmul(ps[0:1, 6, 0:1], m.ones[0:E, 0:1], tiles[0:E, :], start=True, stop=True).then_inc(made, 1)

        @block.vector
        def _(dve):
            n = 0

            def step(ins):
                nonlocal n
                n += 1
                ins.then_inc(v_done, 1)
                dve.wait_ge(v_done, n)

            dve.wait_ge(counted, 3)
            step(dve.tensor_copy(slots[:, :], ints[:, :]))
            step(dve.tensor_copy(item[:, :], rows_i[:, :]))
            step(dve.tensor_copy(expert[:, :], first_i[:, :]))
            step(dve.memset(one[0:E, :], 1.0))
            dve.wait_ge(turned, 2)
            step(dve.tensor_copy(chosen_t[0:E, :], ps[0:E, 0, :]))
            step(dve.tensor_copy(prob_t[0:E, :], ps[0:E, 1, :]))
            step(dve.tensor_tensor_scan(run[0:E, :], one[0:E, :], chosen_t[0:E, :], 0.0, ALU.mult, ALU.add))
            step(dve.tensor_scalar(tiles[0:E, :], run[0:E, T - 1:T], 0.0, None, ALU.is_gt))
            for q in range(1, TT):
                step(dve.tensor_scalar(more[0:E, :], run[0:E, T - 1:T], float(q * P), None, ALU.is_gt))
                step(dve.tensor_tensor(tiles[0:E, :], tiles[0:E, :], more[0:E, :], ALU.add))
            step(dve.tensor_tensor(run[0:E, :], run[0:E, :], chosen_t[0:E, :], ALU.mult))
            assert n == ENDS
            dve.wait_ge(ended, 1)
            step(dve.tensor_copy(end[0:E, :], ps[0:E, 2, 0:1]))
            step(dve.tensor_tensor(begin[0:E, :], end[0:E, :], tiles[0:E, :], ALU.subtract))
            step(dve.tensor_scalar(mine[0:E, :], item[0:E, :], end[0:E, :], None, ALU.is_lt))
            step(dve.tensor_scalar(before[0:E, :], item[0:E, :], begin[0:E, :], None, ALU.is_ge))
            step(dve.tensor_tensor(mine[0:E, :], mine[0:E, :], before[0:E, :], ALU.mult))
            step(dve.tensor_scalar(shift[0:E, :], item[0:E, :], begin[0:E, :], -float(P), ALU.subtract, ALU.mult))
            step(dve.tensor_tensor(shift[0:E, :], shift[0:E, :], mine[0:E, :], ALU.mult))
            dve.wait_ge(made, 1)
            step(dve.tensor_copy(place[:, :, :], ps[:, 3, 0:TT * N].rearrange("p (t n) -> p t n", t=TT)))
            step(dve.tensor_copy(weight[:, :, :], ps[:, 4, 0:TT * N].rearrange("p (t n) -> p t n", t=TT)))
            dve.wait_ge(made, 2)
            step(dve.tensor_copy(table[0:1, 0:N], ps[0:1, 5, 0:N]))
            step(dve.tensor_copy(table[0:1, N:N + 1], ps[0:1, 6, 0:1]))


def experts_phase(m, x_tok, place, weight, table, slots):
    nc = m.nc
    PAIRS = 3
    A, B = 2 * PAIRS, 4
    U = A + B
    SLOT_A, SLOT_B = DT * BANK, 6 * BANK
    halves = lambda v: SLOT_A // 2 if v % U < A else SLOT_B // 2
    i_ = m.ins
    gate, up = (i_[n].rearrange("o e (k p) f -> p (o e) k f", p=P) for n in ("moe_gate", "moe_up"))
    down = i_["moe_down"].rearrange("o e (c k p) d -> p (o e) c k d", p=P, k=6)
    down_units = [(0, 0), (1, 0), (0, 1), (1, 1)]
    add_bank = [2, 3, 4, 5, 6, 7, 2, 3]
    assert ITEMS < ITEM_COLS
    with Phase(m, "experts") as ph:
        raw = [ph.sb(f"raw{s}", [P, SLOT_A]) for s in range(2)]
        w_hi = [ph.sb(f"w_hi{s}", [P, SLOT_A], F32R) for s in range(2)]
        w_lo = [ph.sb(f"w_lo{s}", [P, SLOT_A], F32R) for s in range(2)]
        pick, back, slot_weight = ph.sb("pick", [P, TT, P]), ph.sb("back", [P, T], F32R), ph.sb("slot_weight", [P, 1])
        xg_hi, xg_lo = ph.sb("xg_hi", [P, DT, P], F32R), ph.sb("xg_lo", [P, DT, P], F32R)
        h = ph.sb("h", [P, BANK])
        ht_hi, ht_lo = ph.sb("ht_hi", [P, 2 * A, P], F32R), ph.sb("ht_lo", [P, 2 * A, P], F32R)
        y_hi, y_lo = ph.sb("y_hi", [P, 2, BANK], F32R), ph.sb("y_lo", [P, 2, BANK], F32R)
        ps = ph.banks()
        landed = [[ph.sem(f"landed{s}{q}") for q in range(2)] for s in range(2)]
        (rounded, split, used, picked, gathered, xg_rounded, xg_done, back_full, back_kept, silu_done, h_done, h_turned,
         ht_rounded, ht_done, y_rounded, y_done, added_full, added) = (
            ph.sem(s) for s in ("rounded", "split", "used", "picked", "gathered", "xg_rounded", "xg_done", "back_full",
                                "back_kept", "silu_done", "h_done", "h_turned", "ht_rounded", "ht_done", "y_rounded", "y_done",
                                "added_full", "added"))
        block = ph.enter_context(nc.Block())
        four = lambda bank: ps[:, bank, :].rearrange("p (a n) -> p a n", a=4)

        def items(eng):
            return eng.value_load(table[0:1, ITEM_COLS:ITEM_COLS + 1], min_val=1, max_val=ITEMS)

        @block.sync
        def _(sp):
            def load(i, v, e):
                slot = v % 2
                c = v % U
                for q in range(2):
                    sp.wait_ge(split, i * (2 * U) + (2 * v + (2 if c < 2 else q + 1)))
                    if c < A:
                        dst = raw[slot][:, :].rearrange("p (o k n) -> p o k n", o=1, k=DT)
                        rows = slice(q * (DT // 2), (q + 1) * (DT // 2))
                        sp.dma_start(dst[:, :, rows, :], (gate, up)[c % 2][:, bass.ds(e, 1), rows, c // 2 * BANK:(c // 2 + 1) * BANK]
                                     ).then_inc(landed[slot][q], 16)
                    else:
                        half, part = down_units[c - A]
                        dst = raw[slot][:, 0:SLOT_B].rearrange("p (o k n) -> p o k n", o=1, k=6)
                        rows = slice(3 * q, 3 * q + 3)
                        sp.dma_start(dst[:, :, rows, :],
                                     down[:, bass.ds(e, 1), part, rows, half * BANK:(half + 1) * BANK]).then_inc(landed[slot][q], 16)

            load(0, 0, sp.value_load(table[0:1, 0:1], min_val=0, max_val=EXPERTS - 1))
            with sp.Fori(0, items(sp)) as i:
                expert = lambda: sp.value_load(table[0:1, bass.ds(i, 1)], min_val=0, max_val=EXPERTS - 1)
                e = expert()
                for v in range(1, A):
                    load(i, v, e)
                e = expert()
                for v in range(A, U):
                    load(i, v, e)
                load(i, U, sp.value_load(table[0:1, 1:][:, bass.ds(i, 1)], min_val=0, max_val=EXPERTS - 1))

        def landed_by(i, v):
            return i * (16 * U // 2) + 16 * (v // 2 + 1)

        @block.scalar
        def _(act):
            def round_half(i, v, q):
                n = halves(v)
                act.wait_ge(landed[v % 2][q], landed_by(i, v))
                if q == 0:
                    act.wait_ge(used, i * U + (v + 1))
                s = slice(q * n, (q + 1) * n)
                act.activation(w_hi[v % 2][:, s], raw[v % 2][:, s], ACT.Copy).then_inc(rounded, 1)

            def round_gathered(n):
                for b in range(2):
                    act.wait_ge(gathered, n + (b + 1))
                    act.activation(xg_hi[:, 4 * b:4 * b + 4, :], four(4 + b), ACT.Copy).then_inc(xg_rounded, 1)

            round_half(0, 0, 0)
            round_half(0, 0, 1)
            round_gathered(0)
            with act.Fori(0, items(act)) as i:
                def round_result(half):
                    act.wait_ge(used, i * U + (U - 2 + half + 3))
                    act.activation(y_hi[:, half, :], ps[:, 6 + half, :], ACT.Copy, scale=slot_weight[:, 0:1]).then_inc(y_rounded, 1)

                for v in range(U):
                    round_half(i, v + 1, 0)
                    if v == U - 1:
                        round_result(1)
                    round_half(i, v + 1, 1)
                    if v < A and v % 2 == 0:
                        act.wait_ge(used, i * U + (v + 3))
                        act.wait_ge(h_turned, i * PAIRS + (v // 2 + 1))
                        act.activation(h[:, :], ps[:, 0, :], ACT.Silu).then_inc(silu_done, 1)
                    if v == 0:
                        act.wait_ge(back_full, i + 1)
                        act.activation(back[:, :], ps[:, 3, :], ACT.Copy).then_inc(back_kept, 1)
                        act.activation(slot_weight[:, :], ps[:, 6, 0:1], ACT.Copy).then_inc(back_kept, 1)
                    if v in (2, 4, 6):
                        j = v // 2 - 1
                        act.wait_ge(h_turned, i * PAIRS + (j + 2))
                        act.activation(ht_hi[:, 4 * j:4 * j + 4, :], four(2 + j % 2), ACT.Copy).then_inc(ht_rounded, 1)
                    if v == U - 2:
                        round_gathered(i * 2 + 2)
                        act.wait_ge(back_kept, i * 2 + 2)
                        round_result(0)

        @block.vector
        def _(dve):
            def rest_half(i, v, q):
                n = halves(v)
                s = slice(q * n, (q + 1) * n)
                dve.wait_ge(rounded, i * (2 * U) + (2 * v + q + 1))
                dve.tensor_tensor(w_lo[v % 2][:, s], raw[v % 2][:, s], w_hi[v % 2][:, s].bitcast(F32),
                                  ALU.subtract).then_inc(split, 1)

            def rest_gathered(n):
                for b in range(2):
                    dve.wait_ge(xg_rounded, n + (b + 1))
                    dve.tensor_tensor(xg_lo[:, 4 * b:4 * b + 4, :], four(4 + b), xg_hi[:, 4 * b:4 * b + 4, :].bitcast(F32),
                                      ALU.subtract).then_inc(xg_done, 1)

            def picks(column):
                for t in range(TT):
                    dve.tensor_scalar(pick[:, t, :], slots[:, :], place[:, t, column], None, ALU.is_equal).then_inc(picked, 1)

            dve.nop().then_inc(split, 4)
            dve.nop().then_inc(h_done, 1)
            dve.nop().then_inc(ht_done, 2)
            dve.nop().then_inc(added, DT)
            picks(slice(0, 1))
            rest_half(0, 0, 0)
            rest_half(0, 0, 1)
            rest_gathered(0)
            with dve.Fori(0, items(dve)) as i:
                def rest_result(half):
                    dve.wait_ge(y_rounded, i * 2 + (half + 1))
                    dve.scalar_tensor_tensor(out=y_lo[:, half, :], in0=ps[:, 6 + half, :], scalar=slot_weight[:, 0:1],
                                             in1=y_hi[:, half, :].bitcast(F32), op0=ALU.mult, op1=ALU.subtract).then_inc(y_done, 1)

                def add(tiles):
                    for d in tiles:
                        dve.wait_ge(added_full, i * DT + (d + 1))
                        dve.tensor_tensor(m.xT[:, d, :], m.xT[:, d, :], ps[:, add_bank[d], :], ALU.add).then_inc(added, 1)

                for v in range(U):
                    rest_half(i, v + 1, 0)
                    if v == U - 1:
                        rest_result(1)
                        dve.wait_ge(added, i * DT + DT)
                        add(range(0, 2))
                    rest_half(i, v + 1, 1)
                    if v < A and v % 2:
                        j = v // 2
                        dve.wait_ge(used, i * U + (v + 3))
                        dve.wait_ge(silu_done, i * PAIRS + (j + 2))
                        dve.tensor_tensor(h[:, :], h[:, :], ps[:, 1, :], ALU.mult).then_inc(h_done, 1)
                    if v in (2, 4, 6):
                        j = v // 2 - 1
                        dve.wait_ge(ht_rounded, i * PAIRS + (j + 1))
                        dve.tensor_tensor(ht_lo[:, 4 * j:4 * j + 4, :], four(2 + j % 2), ht_hi[:, 4 * j:4 * j + 4, :].bitcast(F32),
                                          ALU.subtract).then_inc(ht_done, 1)
                    if v == A:
                        dve.wait_ge(back_full, i + 1)
                        picks(bass.ds(i + 1, 1))
                    if v == U - 2:
                        rest_gathered(i * 2 + 2)
                        rest_result(0)
                add(range(2, DT))

        @block.tensor
        def _(pe):
            def gather(n):
                pe.wait_ge(picked, n * TT + TT)
                for b in range(2):
                    for d in range(4 * b, 4 * b + 4):
                        for t in range(TT):
                            last = pe.matmul(ps[:, 4 + b, (d % 4) * P:(d % 4 + 1) * P], x_tok[:, t, d * P:(d + 1) * P], pick[:, t, :],
                                             start=t == 0, stop=t == TT - 1)
                    last.then_inc(gathered, 1)

            pe.nop().then_inc(used, 2)
            pe.nop().then_inc(h_turned, 1)
            pe.nop().then_inc(silu_done, 1)
            gather(0)
            with pe.Fori(0, items(pe)) as i:
                def turn(j):
                    pe.wait_ge(h_done, i * PAIRS + (j + 2))
                    pe.wait_ge(ht_done, i * PAIRS + (j + 1))
                    if j == 1:
                        pe.wait_ge(back_kept, i * 2 + 2)
                    for a in range(4):
                        last = pe.transpose(ps[:, 2 + j % 2, a * P:(a + 1) * P], h[:, a * P:(a + 1) * P], m.ident[:, :])
                    last.then_inc(h_turned, 1)

                for v in range(U):
                    slot = v % 2
                    kt = DT if v < A else 6
                    if v == 0:
                        pe.wait_ge(xg_done, i * 2 + 2)
                    if v < A:
                        pe.wait_ge(h_done if v % 2 else silu_done, i * PAIRS + (v // 2 + 1))
                        out, lhs, first, begin, end = ps[:, v % 2, :], (xg_hi, xg_lo), 0, True, True
                    else:
                        half, part = down_units[v - A]
                        if part == 0:
                            pe.wait_ge(ht_done, i * PAIRS + 4)
                        else:
                            pe.wait_ge(ht_done, i * PAIRS + PAIRS + 2)
                        out, lhs, first, begin, end = ps[:, 6 + half, :], (ht_hi, ht_lo), 6 * part, part == 0, part == 1
                    for k in range(kt):
                        if k % (kt // 2) == 0:
                            pe.wait_ge(split, i * (2 * U) + (2 * v + k // (kt // 2) + 5))
                        cols = slice(k * BANK, (k + 1) * BANK)
                        pe.matmul(out, lhs[1][:, first + k, :], w_hi[slot][:, cols], start=begin and k == 0, stop=False)
                        pe.matmul(out, lhs[0][:, first + k, :], w_lo[slot][:, cols], start=False, stop=False)
                        last = pe.matmul(out, lhs[0][:, first + k, :], w_hi[slot][:, cols], start=False, stop=end and k == kt - 1)
                    last.then_inc(used, 1)
                    if v == 0:
                        pe.wait_ge(added, i * DT + DT)
                        for t in range(TT):
                            pe.matmul(ps[:, 6, 0:1], pick[:, t, :], weight[:, t, bass.ds(i, 1)], start=t == 0, stop=t == TT - 1)
                        for t in range(TT):
                            last = pe.transpose(ps[:, 3, t * P:(t + 1) * P], pick[:, t, :], m.ident[:, :])
                        last.then_inc(back_full, 1)
                    if v in (2, 4, 6):
                        turn(v // 2 - 1)
                    if v == A + 1:
                        gather(i + 1)
                for d in range(DT):
                    if d % 4 == 0:
                        pe.wait_ge(y_done, i * 2 + (d // 4 + 1))
                    if d == 2:
                        pe.wait_ge(xg_done, i * 2 + 4)
                    if d >= 6:
                        pe.wait_ge(added, i * DT + (DT + d - 5))
                    cols = slice((d % 4) * P, (d % 4 + 1) * P)
                    pe.matmul(ps[:, add_bank[d], :], y_lo[:, d // 4, cols], back[:, :], start=True, stop=False)
                    pe.matmul(ps[:, add_bank[d], :], y_hi[:, d // 4, cols], back[:, :], start=False, stop=True).then_inc(added_full, 1)


def moe_phase(m):
    with Phase(m, "moe") as s:
        x_tok = s.sb("x_tok", [P, TT, D])
        place, weight = (s.sb(n, [P, TT, ITEM_COLS]) for n in ("place", "weight"))
        table, slots = s.sb("table", [1, ITEM_COLS + 1], mybir.dt.int32), s.sb("slots", [P, P])
        with Phase(m, "moe2") as s2:
            h = s2.sb("h", [P, DT, T])
            prob, chosen = (s2.sb(n, [P, TT, EXPERTS]) for n in ("prob", "chosen"))
            norm_phase(m, m.xT, "norm2_1", m.act_hi, m.act_lo, full=h)
            router_phase(m, prob, chosen, h, x_tok)
            items_phase(m, prob, chosen, place, weight, table, slots)
        experts_phase(m, x_tok, place, weight, table, slots)




def rg_part(m, ph, ps, px, py, hi, lo):
    i = m.ins
    N = 4
    wa, wx = ph.sb("wa", [P, N, HD]), ph.sb("wx", [P, N, HD])
    xb, ga, gx, mult = (ph.sb(n, [P, N, T]) for n in ("xb", "ga", "gx", "mult"))
    lam, neg = ph.sb("lam", [P, N]), ph.sb("neg", [P, N])
    gelu, out, landed, conv, lam_a, lam_v, full, sig, v_done, a_done = (
        ph.sem(s) for s in ("gelu", "out", "landed", "conv", "lam_a", "lam_v", "full", "sig", "v_done", "a_done"))
    lam_cols = m.params[:, m.columns["lru_lambda"]:m.columns["lru_lambda"] + N]

    def sync(sp):
        for w, src in ((wa, "w_rg_a_2"), (wx, "w_rg_x_2")):
            sp.dma_start(w[:, :, :], i[src][0].rearrange("(j k) c d -> (k c) j d", k=2)).then_inc(landed, 16)

    def tensor(pe):
        pe.wait_ge(landed, 32)
        for w, b in ((wa, 0), (wx, 4)):
            for j in range(N):
                pe.wait_ge(conv, 4 * (j + 1))
                pe.matmul(ps[0:HD, b + j, :], w[0:HD, j, :], xb[0:HD, j, :], start=True, stop=True).then_inc(full, 1)
                pe.wait_ge(full, 2 * (b + j) + 1)
                pe.matmul(ps[HD:P, b + j, :], w[HD:P, j, :], xb[HD:P, j, :], start=True, stop=True).then_inc(full, 1)

    def scalar(act):
        act.activation(py[:, :, :], py[:, :, :], ACT.Gelu_apprx_tanh).then_inc(gelu, 1)
        act.activation(lam[:, :], lam_cols, ACT.Abs).then_inc(lam_a, 1)
        act.wait_ge(lam_a, 1)
        act.activation(lam[:, :], lam[:, :], ACT.Exp, scale=-1.0).then_inc(lam_a, 1)
        act.wait_ge(lam_a, 2)
        act.activation(lam[:, :], lam[:, :], ACT.Ln, bias=m.ones[:, 0:1]).then_inc(lam_a, 1)
        for j in range(N):
            act.wait_ge(full, 2 * j + 2)
            act.activation(ga[:, j, :], ps[:, j, :], ACT.Sigmoid, bias=col(m, "b_rg_a", j)).then_inc(sig, 1)
        for j in range(N):
            act.wait_ge(full, 2 * (4 + j) + 2)
            act.activation(gx[:, j, :], ps[:, 4 + j, :], ACT.Sigmoid, bias=col(m, "b_rg_x", j)).then_inc(sig, 1)
        act.wait_ge(lam_v, 3)
        act.wait_ge(sig, 2 * N)
        for j in range(N):
            act.activation(mult[:, j, :], ga[:, j, :], ACT.Tanh, scale=neg[:, j:j + 1]).then_inc(a_done, 1)
        act.wait_ge(lam_v, 4)
        act.wait_ge(a_done, N)
        for j in range(N):
            act.activation(ga[:, j, :], ga[:, j, :], ACT.Exp, scale=lam[:, j:j + 1]).then_inc(a_done, 1)
        act.activation(px[:, :, :], mult[:, :, :], ACT.Ln, bias=m.ones[:, 0:1]).then_inc(a_done, 1)
        act.wait_ge(a_done, 2 * N + 1)
        act.activation(px[:, :, :], px[:, :, :], ACT.Exp, scale=-0.5).then_inc(a_done, 1)
        act.activation(mult[:, :, :], mult[:, :, :], ACT.Sqrt, scale=2.0).then_inc(a_done, 1)
        for j in range(N):
            act.wait_ge(v_done, 4 + 2 * (j + 1))
            act.activation(hi[:, j, :], xb[:, j, :], ACT.Copy).then_inc(out, 1)

    def start(dve):
        for j in range(N):
            dve.tensor_scalar(xb[:, j, :], px[:, j, :], col(m, "conv_b_w_3", j), col(m, "conv_b_b", j), ALU.mult,
                              ALU.add).then_inc(conv, 1)
            for s in range(1, 4):
                dve.wait_ge(conv, 4 * j + s)
                dve.scalar_tensor_tensor(out=xb[:, j, s:T], in0=px[:, j, 0:T - s], scalar=col(m, f"conv_b_w_{3 - s}", j),
                                         in1=xb[:, j, s:T], op0=ALU.mult, op1=ALU.add).then_inc(conv, 1)
        dve.tensor_scalar(neg[:, :], lam_cols, 0.0, None, ALU.min).then_inc(lam_v, 1)
        dve.wait_ge(lam_v, 1)
        dve.wait_ge(lam_a, 3)
        dve.tensor_tensor(neg[:, :], lam[:, :], neg[:, :], ALU.subtract).then_inc(lam_v, 1)
        dve.wait_ge(lam_v, 2)
        dve.tensor_scalar(neg[:, :], neg[:, :], 8.0, None, ALU.mult).then_inc(lam_v, 1)
        dve.wait_ge(lam_v, 3)
        dve.tensor_scalar(lam[:, :], neg[:, :], -1.0, None, ALU.mult).then_inc(lam_v, 1)

    def vector(dve):
        n = 0

        def step(ins):
            nonlocal n
            n += 1
            ins.then_inc(v_done, 1)
            dve.wait_ge(v_done, n)

        dve.wait_ge(conv, 4 * N)
        dve.wait_ge(conv, 4 * N)
        dve.wait_ge(a_done, 2 * N + 3)
        step(dve.tensor_tensor(mult[:, :, :], mult[:, :, :], px[:, :, :], ALU.mult))
        step(dve.memset(mult[:, :, 0:1], 1.0))
        step(dve.tensor_tensor(xb[:, :, :], xb[:, :, :], gx[:, :, :], ALU.mult))
        step(dve.tensor_tensor(xb[:, :, :], xb[:, :, :], mult[:, :, :], ALU.mult))
        dve.wait_ge(gelu, 1)
        for j in range(N):
            step(dve.tensor_tensor_scan(px[:, j, :], ga[:, j, :], xb[:, j, :], 0.0, ALU.mult, ALU.add))
            step(dve.tensor_tensor(xb[:, j, :], px[:, j, :], py[:, j, :], ALU.mult))
        for j in range(N):
            dve.wait_ge(out, j + 1)
            step(dve.tensor_tensor(lo[:, j, :], xb[:, j, :], hi[:, j, :].bitcast(F32), ALU.subtract))

    return Part(sync=sync, tensor=tensor, scalar=scalar, start=start, vector=vector)


def rw_shift_part(m, ph, rw):
    N = 14
    d = ph.sb("d", [P, N, T])
    diff, mixed, a_done = ph.sem("diff"), ph.sem("mixed"), ph.sem("a_done")

    def vector(dve):
        dve.tensor_tensor(d[:, :, 1:T], rw[:, :, 0:T - 1], rw[:, :, 1:T], ALU.subtract).then_inc(diff, 1)
        dve.tensor_scalar(d[:, :, 0:1], rw[:, :, 0:1], -1.0, None, ALU.mult).then_inc(diff, 1)
        dve.wait_ge(diff, 2)
        for j in reversed(range(N)):
            dve.scalar_tensor_tensor(out=rw[:, j, :], in0=d[:, j, :], scalar=col(m, "mu_shift", j), in1=rw[:, j, :],
                                     op0=ALU.mult, op1=ALU.add).then_inc(mixed, 1)

    def scalar(act):
        act.wait_ge(mixed, 1)
        act.activation(rw[:, 13, :], rw[:, 13, :], ACT.Sigmoid).then_inc(a_done, 1)
        act.wait_ge(mixed, 2)
        act.activation(rw[0:HD, 12, :], rw[0:HD, 12, :], ACT.Tanh).then_inc(a_done, 1)

    return Part(vector=vector, scalar=scalar)


def rg_and_shift_phase(m, px, py, hi, lo, rw):
    with Phase(m, "rg") as ph:
        rg = rg_part(m, ph, ph.banks(), px, py, hi, lo)
        shift = rw_shift_part(m, ph, rw)
        block = ph.enter_context(m.nc.Block())

        @block.sync
        def _(sp):
            rg.sync(sp)

        @block.tensor
        def _(pe):
            rg.tensor(pe)

        @block.scalar
        def _(act):
            rg.scalar(act)
            shift.scalar(act)

        @block.vector
        def _(dve):
            rg.start(dve)
            shift.vector(dve)
            rg.vector(dve)


def rw_lora_phase(m, rw, ld, a, g):
    nc = m.nc
    i = m.ins
    with Phase(m, "rw_lora") as ph:
        wa, wg = ph.sb("wa", [P, 4 * P]), ph.sb("wg", [P, 4 * P])
        ps = ph.banks()
        landed, full, kept, scaled = (ph.sem(s) for s in ("landed", "full", "kept", "scaled"))
        block = ph.enter_context(nc.Block())

        @block.sync
        def _(sp):
            sp.dma_start(wa[0:HD, :], i["w_lora_up_2"][0]).then_inc(landed, 16)
            sp.dma_start(wa[HD:P, :], i["a_lora_up_2"][0]).then_inc(landed, 16)
            sp.dma_start(wg[:, :], i["g_lora_up_2"][0]).then_inc(landed, 16)

        @block.tensor
        def _(pe):
            pe.wait_ge(landed, 48)
            for n in range(12):
                q, j = n // 4, n % 4
                cols = slice(j * P, (j + 1) * P)
                if q == 2:
                    pe.wait_ge(kept, j + 1)
                lhs, rhs = ((wa[0:HD, cols], rw[0:HD, 12, :]), (wa[HD:P, cols], rw[HD:P, 12, :]), (wg[:, cols], rw[:, 13, :]))[q]
                pe.matmul(ps[:, n % 8, :], lhs, rhs, start=True, stop=True).then_inc(full, 1)

        @block.scalar
        def _(act):
            for n in range(12):
                q, j = n // 4, n % 4
                act.wait_ge(full, n + 1)
                if q == 2:
                    act.activation(g[:, j, :], ps[:, n % 8, :], ACT.Copy).then_inc(kept, 1)
                else:
                    dst, name = ((ld, "w0"), (a, "a0"))[q]
                    act.activation(dst[:, j, :], ps[:, n % 8, :], ACT.Sigmoid, bias=col(m, name, j)).then_inc(kept, 1)

        @block.vector
        def _(dve):
            for j in range(4):
                dve.wait_ge(kept, j + 1)
                dve.tensor_scalar(ld[:, j, :], ld[:, j, :], -math.exp(-0.5), None, ALU.mult).then_inc(scaled, 1)


def rw_keys_phase(m, rw, a, kk, b, bonus_rows):
    nc = m.nc
    N = 4
    r, k = rw[:, 0:4], rw[:, 4:8]
    with Phase(m, "rw_keys") as ph:
        sq = ph.sb("sq", [P, N, T])
        one_less = ph.sb("one_less", [P, N])
        ps = ph.banks()
        v_done, a_done, summed = (ph.sem(s) for s in ("v_done", "a_done", "summed"))
        block = ph.enter_context(nc.Block())
        ka = m.params[:, m.columns["k_a"]:m.columns["k_a"] + N]
        LENGTHS = N + 1 + 2 * N + 1
        STEPS = LENGTHS + 2 + N

        @block.scalar
        def _(act):
            act.wait_ge(v_done, N)
            act.activation(sq[:, :, :], kk[:, :, :], ACT.Square).then_inc(a_done, 1)
            act.wait_ge(v_done, LENGTHS)
            act.activation(sq[:, :, :], sq[:, :, :], ACT.Ln, scale=2.0 ** 30).then_inc(a_done, 1)
            act.wait_ge(a_done, 2)
            act.activation(sq[:, :, :], sq[:, :, :], ACT.Exp, scale=-0.5).then_inc(a_done, 1)

        @block.tensor
        def _(pe):
            pe.wait_ge(a_done, 1)
            for j in range(N):
                pe.matmul(ps[:, j, :], m.pair_ones[:, :], sq[:, j, :], start=True, stop=True).then_inc(summed, 1)
            pe.wait_ge(v_done, STEPS)
            for j in range(N):
                pe.matmul(ps[:, N + j, :], m.pair_ones[:, :], sq[:, j, :], start=True, stop=True).then_inc(summed, 1)

        @block.vector
        def _(dve):
            n = 0

            def step(ins):
                nonlocal n
                n += 1
                ins.then_inc(v_done, 1)
                dve.wait_ge(v_done, n)

            for j in range(N):
                step(dve.tensor_scalar(kk[:, j, :], k[:, j, :], col(m, "k_k", j), None, ALU.mult))
            step(dve.tensor_scalar(one_less[:, :], ka, -1.0, 1.0, ALU.mult, ALU.add))
            for j in range(N):
                step(dve.tensor_scalar(bonus_rows[:, j, :], a[:, j, :], col(m, "k_a", j), one_less[:, j:j + 1], ALU.mult, ALU.add))
                step(dve.tensor_tensor(k[:, j, :], k[:, j, :], bonus_rows[:, j, :], ALU.mult))
            dve.wait_ge(summed, N)
            step(dve.tensor_scalar(sq[:, :, :], ps[:, 0:N, :], 1e-24, None, ALU.max))
            dve.wait_ge(a_done, 3)
            step(dve.scalar_tensor_tensor(out=kk[:, :, :], in0=kk[:, :, :], scalar=-2.0 ** 15, in1=sq[:, :, :], op0=ALU.mult, op1=ALU.mult))
            step(dve.scalar_tensor_tensor(out=b[:, :, :], in0=kk[:, :, :], scalar=-1.0, in1=a[:, :, :], op0=ALU.mult, op1=ALU.mult))
            for j in range(N):
                step(dve.scalar_tensor_tensor(out=sq[:, j, :], in0=r[:, j, :], scalar=col(m, "r_k", j), in1=k[:, j, :],
                                              op0=ALU.mult, op1=ALU.mult))
            assert n == STEPS
            for j in range(N):
                dve.wait_ge(summed, N + j + 1)
                step(dve.tensor_copy(bonus_rows[:, j, :], ps[:, N + j, :]))


def rw_scale_part(m, ph, rw, ld, kk, b, bd, kd, last):
    N = 4
    r, k = rw[:, 0:4], rw[:, 4:8]
    run, e = ph.sb("run", [P, N, T]), ph.sb("e", [P, N, T])
    scanned, before, a_done, v_done = (ph.sem(s) for s in ("scanned", "before", "a_done", "v_done"))
    chunks = lambda x: x.rearrange("p j (c t) -> p j c t", t=CH)

    def scalar(act):
        act.wait_ge(scanned, N)
        act.activation(e[:, :, :], run[:, :, :], ACT.Exp).then_inc(a_done, 1)
        act.wait_ge(before, 1)
        act.activation(ld[:, :, :], ld[:, :, :], ACT.Exp).then_inc(a_done, 1)
        act.activation(run[:, :, :], run[:, :, :], ACT.Exp, scale=-1.0).then_inc(a_done, 1)

    def vector(dve):
        n = 0

        def step(ins):
            nonlocal n
            n += 1
            ins.then_inc(v_done, 1)
            dve.wait_ge(v_done, n)

        for j in range(N):
            dve.tensor_tensor_scan(run[:, j, :], m.reset[:, :], ld[:, j, :], 0.0, ALU.mult, ALU.add).then_inc(scanned, 1)
        dve.wait_ge(scanned, N)
        dve.tensor_tensor(ld[:, :, :], run[:, :, :], ld[:, :, :], ALU.subtract).then_inc(before, 1)
        dve.wait_ge(a_done, 1)
        step(dve.tensor_tensor(r[:, :, :], r[:, :, :], e[:, :, :], ALU.mult))
        step(dve.tensor_copy(last[:, :, :], e[:, :, CH - 1:T:CH]))
        dve.wait_ge(a_done, 2)
        step(dve.tensor_tensor(kk[:, :, :], kk[:, :, :], ld[:, :, :], ALU.mult))
        dve.wait_ge(a_done, 3)
        step(dve.tensor_tensor(b[:, :, :], b[:, :, :], run[:, :, :], ALU.mult))
        step(dve.tensor_tensor(k[:, :, :], k[:, :, :], run[:, :, :], ALU.mult))
        for j in range(N):
            end = last[:, j, :].unsqueeze(2).to_broadcast([P, NCH, CH])
            step(dve.tensor_tensor(chunks(bd[:, :, :])[:, j], chunks(b[:, :, :])[:, j], end, ALU.mult))
            step(dve.tensor_tensor(chunks(kd[:, :, :])[:, j], chunks(k[:, :, :])[:, j], end, ALU.mult))

    return Part(scalar=scalar, vector=vector, steps=v_done)


def rw_scale_and_turn_phase(m, rw, ld, kk, b, bd, kd, v, r):
    N = 4
    with Phase(m, "rw_scale") as ph:
        ps = ph.banks()
        scale = rw_scale_part(m, ph, rw, ld, kk, b, bd, kd, r.last)
        turned, kept = ph.sem("turned"), ph.sem("kept")
        block = ph.enter_context(m.nc.Block())
        tiles = [(v, r.v_tok, j, 0) for j in range(N)] + [(kk, r.a_tok, j, 3) for j in range(N)]
        for j in range(N):
            tiles += [(bd, r.bd_tok, j, 5 + 2 * j + 1), (kd, r.kd_tok, j, 5 + 2 * j + 2)]

        @block.tensor
        def _(pe):
            for n, (src, _, j, steps) in enumerate(tiles):
                if steps:
                    pe.wait_ge(scale.steps, steps)
                if n >= 8:
                    pe.wait_ge(kept, n - 7)
                for t in range(TT):
                    last = pe.transpose(ps[:, n % 8, t * P:(t + 1) * P], src[:, j, t * P:(t + 1) * P], m.ident[:, :])
                last.then_inc(turned, 1)

        @block.scalar
        def _(act):
            scale.scalar(act)
            for n, (_, dst, j, _) in enumerate(tiles):
                act.wait_ge(turned, n + 1)
                act.activation(dst[:, :, j * P:(j + 1) * P], ps[:, n % 8, :].rearrange("p (t n) -> p t n", t=TT),
                               ACT.Copy).then_inc(kept, 1)

        @block.vector
        def _(dve):
            scale.vector(dve)


def rw_out_phase(m, y, v, bonus, g, hi, lo):
    nc = m.nc
    N = 4
    with Phase(m, "rw_out") as ph:
        sq = ph.sb("sq", [P, N, T])
        lnx_eps = ph.sb("lnx_eps", [P, 1])
        ps = ph.banks()
        v_done, a_done, summed, eps_done = (ph.sem(s) for s in ("v_done", "a_done", "summed", "eps_done"))
        block = ph.enter_context(nc.Block())

        @block.gpsimd
        def _(pool):
            pool.memset(lnx_eps[:, :], 64e-5).then_inc(eps_done, 1)

        @block.tensor
        def _(pe):
            for j in range(N):
                pe.matmul(ps[:, j, :], m.pair_ones[:, :], y[:, j, :], start=True, stop=True).then_inc(summed, 1)
            pe.wait_ge(a_done, 1)
            for j in range(N):
                pe.matmul(ps[:, N + j, :], m.pair_ones[:, :], sq[:, j, :], start=True, stop=True).then_inc(summed, 1)

        @block.scalar
        def _(act):
            act.wait_ge(v_done, 1)
            act.activation(sq[:, :, :], y[:, :, :], ACT.Square).then_inc(a_done, 1)
            act.wait_ge(summed, 2 * N)
            act.wait_ge(eps_done, 1)
            act.activation(sq[:, :, :], ps[:, N:2 * N, :], ACT.Ln, scale=1.0 / HD, bias=lnx_eps[:, 0:1]).then_inc(a_done, 1)
            act.wait_ge(a_done, 2)
            act.activation(sq[:, :, :], sq[:, :, :], ACT.Exp, scale=-0.5).then_inc(a_done, 1)
            act.wait_ge(v_done, 2 + 2 * N + 1)
            act.activation(hi[:, :, :], y[:, :, :], ACT.Copy).then_inc(a_done, 1)

        @block.vector
        def _(dve):
            n = 0

            def step(ins):
                nonlocal n
                n += 1
                ins.then_inc(v_done, 1)
                dve.wait_ge(v_done, n)

            dve.wait_ge(summed, N)
            step(dve.scalar_tensor_tensor(out=y[:, :, :], in0=ps[:, 0:N, :], scalar=-1.0 / HD, in1=y[:, :, :], op0=ALU.mult, op1=ALU.add))
            step(dve.tensor_tensor(v[:, :, :], v[:, :, :], bonus[:, :, :], ALU.mult))
            dve.wait_ge(a_done, 3)
            for j in range(N):
                step(dve.scalar_tensor_tensor(out=y[:, j, :], in0=y[:, j, :], scalar=col(m, "lnx_g", j), in1=sq[:, j, :],
                                              op0=ALU.mult, op1=ALU.mult))
                step(dve.scalar_tensor_tensor(out=y[:, j, :], in0=y[:, j, :], scalar=col(m, "lnx_b", j), in1=v[:, j, :],
                                              op0=ALU.add, op1=ALU.add))
            step(dve.tensor_tensor(y[:, :, :], y[:, :, :], g[:, :, :], ALU.mult))
            dve.wait_ge(a_done, 4)
            step(dve.tensor_tensor(lo[:, :, :], y[:, :, :], hi[:, :, :].bitcast(F32), ALU.subtract))


def bias_job(m, ps, w, first, groups, nf, dst, name, bias0):
    def load(g, c):
        return two_loads(k_major(w), g * (nf * P) + first, nf)

    def dve(eng, g, b, n):
        for f in range(nf):
            c = g * nf + (m.columns[name] + bias0 + f)
            last = eng.tensor_scalar(dst[:, bass.ds(g * nf + f, 1), :], ps[:, b + f, :], m.params[:, bass.ds(c, 1)], None, ALU.add)
        return last

    return Job(groups, nf, load, m.act_hi, m.act_lo, dve)


def second_mixer(m):
    i = m.ins
    w = i["w_in_2"][0]
    RW = 14
    with Phase(m, "mix2") as s:
        rw = s.sb("rw", [P, RW, T])
        with Phase(m, "pxy") as s2:
            px, py = s2.sb("px", [P, 4, T]), s2.sb("py", [P, 4, T])
            dense_phase(m, lambda ph, ps: [bias_job(m, ps, w, 0, 7, 2, rw, "b_in", 0),
                                           bias_job(m, ps, w, RW * P, 2, 2, px, "b_in", RW),
                                           bias_job(m, ps, w, (RW + 4) * P, 2, 2, py, "b_in", RW + 4)], "proj2",
                        norm_of(m, "norm_mix_g"))
            rg_and_shift_phase(m, px, py, m.act_hi[:, 4:8], m.act_lo[:, 4:8], rw)
        r = Rule()
        r.heads, r.decayed = 8, False
        kk, b, g, bonus = (s.sb(n, [P, 4, T]) for n in ("kk", "b", "g", "bonus"))
        r.last = s.sb("last", [P, 4, NCH])
        r.a_tok, r.v_tok, r.bd_tok, r.kd_tok = (s.sb(n, [P, TT, 4 * P]) for n in ("a_tok", "v_tok", "bd_tok", "kd_tok"))
        with Phase(m, "ld") as s3:
            ld, a = s3.sb("ld", [P, 4, T]), s3.sb("a", [P, 4, T])
            rw_lora_phase(m, rw, ld, a, g)
            rw_keys_phase(m, rw, a, kk, b, bonus)
            with Phase(m, "bdkd") as s4:
                kd = s4.sb("kd", [P, 4, T])
                rw_scale_and_turn_phase(m, rw, ld, kk, b, a, kd, rw[:, 8:12], r)
        with Phase(m, "qb") as s5:
            r.qb = s5.sb("qb", [P, 8, TT, P])
            r.k_t, r.a_t, r.b_t, r.q_t, r.r_t = rw[:, 4:8], kk, b, rw[:, 0:4], rw[:, 0:4]
            r.w_t, r.y_t, r.tz_tok, r.u_tok = kk, rw[:, 4:8], r.a_tok, r.a_tok
            chunk_phase(m, r)
            r.states = s5.sb("states", [P, NCH, 4, HD])
            scan_phase(m, r)
            read_phase(m, r)
        rw_out_phase(m, rw[:, 4:8], rw[:, 8:12], bonus, g, m.act_hi[:, 0:4], m.act_lo[:, 0:4])
    with Phase(m, "merge") as s:
        h_hi, h_lo = s.sb("h_hi", [P, DT, T], F32R), s.sb("h_lo", [P, DT, T], F32R)
        ga, gb = s.sb("ga", [P, DT, T]), s.sb("gb", [P, DT, T])

        def jobs(ph, ps):
            sig, merged, m_hi, times = ph.sem("sig"), ph.sem("merged"), ph.sem("m_hi"), ph.sem("times")

            def gate_job(dst, n0, tile0):
                def load(g, c):
                    return two_loads(k_major(w), g * (2 * P) + tile0 * P, 2)

                def act(eng, g, b, n):
                    for f in range(2):
                        c = g * 2 + (m.columns["b_in"] + tile0 + f)
                        eng.activation(dst[:, bass.ds(g * 2 + f, 1), :], ps[:, b + f, :], ACT.Sigmoid,
                                       bias=m.params[:, bass.ds(c, 1)]).then_inc(sig, 1)

                def dve(eng, g, b, n):
                    eng.wait_ge(sig, n * 2 + 2 * n0)
                    return eng.nop()

                return Job(4, 2, load, h_hi, h_lo, dve, act)

            def branch_job(w_branch, first, second):
                def load(g, c):
                    return two_loads(k_major(w_branch), g * (2 * P), 2)

                def dve(eng, g, b, n):
                    gate = (gb if second else ga)[:, bass.ds(g * 2, 2), :]
                    if not second:
                        return eng.tensor_tensor(gate, gate, ps[:, b:b + 2, :], ALU.mult)
                    into = ga[:, bass.ds(g * 2, 2), :]
                    eng.tensor_tensor(gate, gate, ps[:, b:b + 2, :], ALU.mult).then_inc(times, 1)
                    eng.wait_ge(times, n)
                    eng.tensor_tensor(into, into, gate, ALU.add).then_inc(merged, 1)
                    eng.wait_ge(m_hi, n)
                    return eng.tensor_tensor(h_lo[:, bass.ds(g * 2, 2), :], into, h_hi[:, bass.ds(g * 2, 2), :].bitcast(F32),
                                             ALU.subtract)

                def act(eng, g, b, n):
                    eng.wait_ge(merged, n)
                    eng.activation(h_hi[:, bass.ds(g * 2, 2), :], ga[:, bass.ds(g * 2, 2), :], ACT.Copy).then_inc(m_hi, 1)

                x = slice(first, first + 4)
                return Job(4, 2, load, m.act_hi[:, x], m.act_lo[:, x], dve, act if second else None, kt=4)

            out = add_job(m, i["w_mix_out_2"][0], ps)
            out.hi, out.lo, out.after = h_hi, h_lo, 3
            return [gate_job(ga, 0, RW + 8), gate_job(gb, 4, RW + 16), branch_job(i["w_branch_a_2"][0], 0, False),
                    branch_job(i["w_branch_b_2"][0], 4, True), out]

        dense_phase(m, jobs, "merge", norm_of(m, "norm_mix_g", h_hi, h_lo, ga))


def memory_phase(m, mem_t, hi, lo):
    nc = m.nc
    M = 2 * P
    with Phase(m, "memory") as ph:
        rows = ph.sb("rows", [P, 2, D])
        ps = ph.banks()
        norm = Norm(m, ph, ps[:, 7:8], mem_t, "norm_mem_g", hi, lo, DT, M)
        landed, turned, kept = ph.sem("landed"), ph.sem("turned"), ph.sem("kept")
        block = ph.enter_context(nc.Block())

        @block.sync
        def _(sp):
            for t in range(2):
                sp.dma_start(rows[:, t, :], m.ins["mem_2"][0, t * P:(t + 1) * P, :]).then_inc(landed, 16)

        @block.tensor
        def _(pe):
            pe.wait_ge(landed, 32)
            for k in range(DT):
                if k >= 7:
                    pe.wait_ge(kept, k - 6)
                for t in range(2):
                    last = pe.transpose(ps[:, k % 7, t * P:(t + 1) * P], rows[:, t, k * P:(k + 1) * P], m.ident[:, :])
                last.then_inc(turned, 1)
            norm.sum_up(pe)

        @block.vector
        def _(dve):
            for k in range(DT):
                dve.wait_ge(turned, k + 1)
                dve.tensor_copy(mem_t[:, k, :], ps[:, k % 7, 0:M]).then_inc(kept, 1)
            dve.wait_ge(kept, DT)
            norm.scale(dve)
            norm.rest_tiles(dve)

        @block.scalar
        def _(act):
            act.wait_ge(kept, DT)
            norm.roots(act)
            norm.round_tiles(act)


def cross_attention_phase(m, q, k, v_tok, o_t):
    nc = m.nc
    H, M = 4, 256
    with Phase(m, "cross") as ph:
        prob, prob_t = ph.sb("prob", [P, TT, M]), ph.sb("prob_t", [P, 2, T])
        top, total = ph.sb("top", [P, TT]), ph.sb("total", [P, TT])
        ps = ph.banks()
        scored, topped, exped, inverse, normed, turned, kept, out_full, out_kept = (
            ph.sem(s) for s in ("scored", "topped", "exped", "inverse", "normed", "turned", "kept", "out_full", "out_kept"))
        block = ph.enter_context(nc.Block())

        @block.tensor
        def _(pe):
            for h in range(H):
                for i in range(TT):
                    n = TT * h + i
                    if h:
                        pe.wait_ge(exped, n - TT + 1)
                    for d in range(2):
                        last = pe.matmul(ps[:, i, 0:M], q[:, 2 * h + d, i * P:(i + 1) * P], k[:, 2 * h + d, :], start=d == 0, stop=d == 1)
                    last.then_inc(scored, 1)
                pe.wait_ge(normed, TT * (h + 1))
                for j in range(2):
                    if h:
                        pe.wait_ge(kept, 2 * (h - 1) + j + 1)
                    for i in range(TT):
                        last = pe.transpose(ps[:, 4 + j, i * P:(i + 1) * P], prob[:, i, j * P:(j + 1) * P], m.ident[:, :])
                    last.then_inc(turned, 1)
                pe.wait_ge(kept, 2 * (h + 1))
                for d in range(2):
                    if h:
                        pe.wait_ge(out_kept, 2 * (h - 1) + d + 1)
                    for j in range(2):
                        last = pe.matmul(ps[:, 6 + d, :], v_tok[:, j, (2 * h + d) * P:(2 * h + d + 1) * P], prob_t[:, j, :],
                                         start=j == 0, stop=j == 1)
                    last.then_inc(out_full, 1)

        @block.vector
        def _(dve):
            for h in range(H):
                for i in range(TT):
                    n = TT * h + i
                    dve.wait_ge(scored, n + 1)
                    if h:
                        dve.wait_ge(exped, n - TT + 1)
                    dve.tensor_reduce(top[:, i:i + 1], ps[:, i, 0:M], AX.X, ALU.max, negate=True).then_inc(topped, 1)
                for i in range(TT):
                    n = TT * h + i
                    dve.wait_ge(exped, n + 1)
                    dve.reciprocal(total[:, i:i + 1], total[:, i:i + 1]).then_inc(inverse, 1)
                    dve.wait_ge(inverse, n + 1)
                    dve.tensor_scalar(prob[:, i, :], prob[:, i, :], total[:, i:i + 1], None, ALU.mult).then_inc(normed, 1)
                for d in range(2):
                    dve.wait_ge(out_full, 2 * h + d + 1)
                    dve.tensor_copy(o_t[:, 2 * h + d, :], ps[:, 6 + d, :]).then_inc(out_kept, 1)

        @block.scalar
        def _(act):
            for h in range(H):
                for i in range(TT):
                    n = TT * h + i
                    act.wait_ge(topped, n + 1)
                    if h:
                        act.wait_ge(turned, 2 * h)
                        act.wait_ge(normed, n - TT + 1)
                    act.activation(prob[:, i, :], ps[:, i, 0:M], ACT.Exp, bias=top[:, i:i + 1],
                                   accum_out=total[:, i:i + 1]).then_inc(exped, 1)
                for j in range(2):
                    act.wait_ge(turned, 2 * h + j + 1)
                    if h:
                        act.wait_ge(out_full, 2 * h)
                    act.activation(prob_t[:, j, :], ps[:, 4 + j, :], ACT.Copy).then_inc(kept, 1)


def cross_mixer(m):
    i = m.ins
    M = 256
    with Phase(m, "cr") as s:
        q, k = s.sb("q", [P, DT, T]), s.sb("k", [P, DT, M])
        v_tok = s.sb("v_tok", [P, 2, D])
        with Phase(m, "cr2") as s2:
            mem_t, v = s2.sb("mem_t", [P, DT, M]), s2.sb("v", [P, DT, M])
            mem_hi, mem_lo = s2.sb("mem_hi", [P, DT, M], F32R), s2.sb("mem_lo", [P, DT, M], F32R)
            memory_phase(m, mem_t, mem_hi, mem_lo)

            def jobs(ph, ps):
                def dve(eng, g, b, n):
                    return eng.tensor_scalar(q[:, bass.ds(g * 2, 2), :], ps[:, b:b + 2, :], 1.0 / 16, None, ALU.mult)

                q_job = plain_job(m, i["w_cq_2"][0], 0, 4, 2, q, ps=ps)
                q_job.dve = dve
                more = dict(ps=ps, n=M, hi=mem_hi, lo=mem_lo)
                return [q_job, plain_job(m, i["w_ckv_2"][0], 0, 4, 2, k, **more), plain_job(m, i["w_ckv_2"][0], D, 4, 2, v, **more)]

            dense_phase(m, jobs, "cross_proj", norm_of(m, "norm_x_g", full=q))
            turn_phase(m, [(v, v_tok, DT)], M)
        o = s.sb("o", [P, DT, T])
        cross_attention_phase(m, q, k, v_tok, o)
        dense_phase(m, lambda ph, ps: [add_job(m, i["w_co_2"][0], ps)], "w_co", 
                    lambda ph, ps: Split(ph, [o[:, t, :] for t in range(DT)], m.act_hi, m.act_lo))


def conv_ffn_phase(m):
    i = m.ins
    half = 11
    w = i["w_ffn_in_2"][0]

    def all_jobs(ph, ps):
        buffers, conv, result = swiglu_buffers(ph, half), ph.sb("conv", [P, T]), []
        for s in range(2):
            f = slice(s * half * P, (s + 1) * half * P)
            up_f = slice(22 * P + s * half * P, 22 * P + (s + 1) * half * P)
            jobs = swiglu_jobs(m, ph, ps, buffers, w[:, f], w[:, up_f], i["w_ffn_out_2"][0][f, :], half, 2 * s)
            up = jobs[0]
            tap = [ph.sem("tap0"), ph.sem("tap1")]
            act0, dve0 = up.act, up.dve
            param = lambda name, g, s=s: m.params[:, bass.ds(g + (m.columns[name] + s * half), 1)]

            def act(eng, g, b, n, tap=tap, act0=act0, param=param):
                eng.activation(conv[:, :], ps[:, b, :], ACT.Identity, scale=param("ffn_conv_w_2", g),
                               bias=param("ffn_conv_b", g)).then_inc(tap[0], 1)
                eng.wait_ge(tap[1], n * 2)
                act0(eng, g, b, n, conv[:, :], ACT.Gelu_apprx_tanh)

            def dve(eng, g, b, n, tap=tap, dve0=dve0, param=param):
                eng.wait_ge(tap[0], n)
                for d in (1, 2):
                    if d == 2:
                        eng.wait_ge(tap[1], n * 2 - 1)
                    ins = eng.scalar_tensor_tensor(out=conv[:, d:T], in0=ps[:, b, 0:T - d], scalar=param(f"ffn_conv_w_{2 - d}", g),
                                                   in1=conv[:, d:T], op0=ALU.mult, op1=ALU.add)
                    ins.then_inc(tap[1], 1)
                return dve0(eng, g, b, n)

            up.act, up.dve = act, dve
            result += jobs
        return result

    dense_phase(m, all_jobs, "conv_ffn", norm_of(m, "norm_ffn_g"))


def final_phase(m, x, gain):
    nc = m.nc
    with Phase(m, "final") as ph:
        sq = ph.sb("sq", [P, DT, T])
        rstd = ph.sb("rstd", [P, T])
        rows = ph.sb("rows", [P, TT, D])
        ps = ph.banks()
        squared, summed, root, scaled, turned, copied, stored = (
            ph.sem(s) for s in ("squared", "summed", "root", "scaled", "turned", "copied", "stored"))
        block = ph.enter_context(nc.Block())
        pieces = [(half, t) for half in range(2) for t in range(TT)]

        @block.scalar
        def _(act):
            for k in range(DT):
                act.activation(sq[:, k, :], x[:, k, :], ACT.Square).then_inc(squared, 1)
            act.wait_ge(summed, 1)
            act.activation(rstd[:, :], ps[:, 7, :], ACT.Ln, scale=1.0 / D, bias=m.eps[:, 0:1]).then_inc(root, 1)
            act.wait_ge(root, 1)
            act.activation(rstd[:, :], rstd[:, :], ACT.Exp, scale=-0.5).then_inc(root, 1)
            for n, (half, t) in enumerate(pieces):
                act.wait_ge(turned, n + 1)
                act.activation(rows[:, t, half * BANK:(half + 1) * BANK], ps[:, n, :], ACT.Copy).then_inc(copied, 1)

        @block.tensor
        def _(pe):
            for k in range(DT):
                pe.wait_ge(squared, k + 1)
                last = pe.matmul(ps[:, 7, :], m.ones[:, :], sq[:, k, :], start=k == 0, stop=k == DT - 1)
            last.then_inc(summed, 1)
            for n, (half, t) in enumerate(pieces):
                pe.wait_ge(scaled, 4 * half + 4)
                for k in range(4):
                    last = pe.transpose(ps[:, n, k * P:(k + 1) * P], x[:, 4 * half + k, t * P:(t + 1) * P], m.ident[:, :])
                last.then_inc(turned, 1)

        @block.vector
        def _(dve):
            dve.wait_ge(root, 2)
            for k in range(DT):
                dve.scalar_tensor_tensor(out=x[:, k, :], in0=x[:, k, :], scalar=col(m, gain, k), in1=rstd[:, :],
                                         op0=ALU.mult, op1=ALU.mult).then_inc(scaled, 1)

        @block.sync
        def _(sp):
            for n, (half, t) in enumerate(pieces):
                cols = slice(half * BANK, (half + 1) * BANK)
                sp.wait_ge(copied, n + 1)
                sp.dma_start(m.out[0, t * P:(t + 1) * P, cols], rows[:, t, cols]).then_inc(stored, 16)
            sp.wait_ge(stored, 16 * len(pieces))




def program(m):
    with Phase(m, "keep") as keep:
        setup_phase(m, keep)
        mixer(m, 0)
        ffn_phase(m)
        mixer(m, 1)
        moe_phase(m)
        second_mixer(m)
        cross_mixer(m)
        conv_ffn_phase(m)
        final_phase(m, m.xT, "norm_final_g")


def kernel(**inputs):
    import numpy as np

    import concourse.bacc as bacc
    from concourse.bass_utils import run_bass_kernel_spmd

    nc = bacc.Bacc("TRN2", target_bir_lowering=False, num_devices=1)
    arrays, ins = {}, {}
    for name, a in inputs.items():
        a = np.ascontiguousarray(a)
        arrays[f"in_{name}"] = a
        ins[name] = nc.dram_tensor(f"in_{name}", a.shape, mybir.dt.from_np(a.dtype), kind="ExternalInput").ap()
    out = nc.dram_tensor("out", inputs["x"].shape, F32, kind="ExternalOutput").ap()
    program(Machine(nc, ins, out))
    return run_bass_kernel_spmd(nc, [arrays], core_ids=[0]).results[0]["out"]
```
